# Optimizing a Trainium2 kernel written in Bass

```python
import math
import jax, jax.numpy as jnp
from jax import lax
import numpy as np

D_MODEL = 1024
BATCH = 1
SEQ = 512
DEPTH = 1

MLA_HEADS = 8
MLA_NOPE = 64
MLA_ROPE = 32
MLA_V = 64
MLA_Q_RANK = 384
MLA_KV_RANK = 256
RET_HEADS = 4
RET_DK = 64
RET_DV = 128
RET_CHUNK = 128
FF_DIM = 2816
Q_BLOCK = 128
ROPE_BASE = 10000.0
NORM_EPS = 1e-6
GN_EPS = 1e-6

IN_SIZES = (MLA_Q_RANK, MLA_KV_RANK, MLA_ROPE,
            RET_HEADS * RET_DK, RET_HEADS * RET_DK, RET_HEADS * RET_DV, RET_HEADS * RET_DV,
            D_MODEL, D_MODEL)
IN_WIDTH = sum(IN_SIZES)

kernel_name = "hybrid_mla_retention_gated_macaron"

def _rmsnorm(x, w):
    xf = x.astype(jnp.float32)
    y = xf * lax.rsqrt(jnp.mean(xf * xf, axis=-1, keepdims=True) + NORM_EPS)
    return (y * w.astype(jnp.float32)).astype(x.dtype)

def _swiglu(x, w1, w2):
    gate, up = jnp.split(x @ w1, 2, axis=-1)
    return (jax.nn.silu(gate) * up) @ w2

def _rope(x, positions):
    half = x.shape[-1] // 2
    inv_freq = ROPE_BASE ** (-jnp.arange(half, dtype=jnp.float32) / half)
    ang = positions.astype(jnp.float32)[..., None] * inv_freq
    cos = jnp.cos(ang)[:, :, None, :]
    sin = jnp.sin(ang)[:, :, None, :]
    xf = x.astype(jnp.float32)
    x1, x2 = xf[..., :half], xf[..., half:]
    return jnp.concatenate([x1 * cos - x2 * sin, x2 * cos + x1 * sin], axis=-1).astype(x.dtype)

def _split_points():
    points, acc = [], 0
    for s in IN_SIZES[:-1]:
        acc += s
        points.append(acc)
    return points

def _causal_attention(q, k, v, scale):
    b, h, s, dqk = q.shape
    nb = s // Q_BLOCK
    q_blocks = jnp.moveaxis(q.reshape(b, h, nb, Q_BLOCK, dqk), 2, 0)
    k_pos = jnp.arange(s)

    def one_block(args):
        q_blk, i = args
        scores = jnp.einsum('bhqd,bhkd->bhqk', q_blk, k).astype(jnp.float32) * scale
        q_pos = i * Q_BLOCK + jnp.arange(Q_BLOCK)
        scores = jnp.where(q_pos[:, None] >= k_pos[None, :], scores, -jnp.inf)
        p = jax.nn.softmax(scores, axis=-1)
        return jnp.einsum('bhqk,bhkd->bhqd', p.astype(v.dtype), v)

    out = lax.map(one_block, (q_blocks, jnp.arange(nb)))
    return jnp.moveaxis(out, 0, 2).reshape(b, h, s, v.shape[-1])

def _chunkwise_retention(q, k, v):
    b, h, s, dk = q.shape
    dv = v.shape[-1]
    n = s // RET_CHUNK
    log_gamma = jnp.log(1.0 - 2.0 ** (-5.0 - jnp.arange(h, dtype=jnp.float32)))
    idx = jnp.arange(RET_CHUNK, dtype=jnp.float32)
    diff = idx[:, None] - idx[None, :]
    decay_intra = jnp.where(diff >= 0, jnp.exp(jnp.maximum(diff, 0.0) * log_gamma[:, None, None]), 0.0)
    zeta = jnp.exp((RET_CHUNK - 1 - idx) * log_gamma[:, None])
    xi = jnp.exp((idx + 1.0) * log_gamma[:, None])
    chunk_decay = jnp.exp(RET_CHUNK * log_gamma)

    qc = q.reshape(b, h, n, RET_CHUNK, dk)
    kc = k.reshape(b, h, n, RET_CHUNK, dk)
    vc = v.reshape(b, h, n, RET_CHUNK, dv)

    inner = jnp.einsum('bhncd,bhnsd->bhncs', qc, kc) * decay_intra[None, :, None].astype(q.dtype)
    y_inner = jnp.einsum('bhncs,bhnse->bhnce', inner, vc)

    kv = jnp.einsum('bhnsd,bhnse->bhnde', kc * zeta[None, :, None, :, None].astype(k.dtype), vc)
    decay_c = chunk_decay.astype(kv.dtype)[None, :, None, None]

    def step(state, kv_n):
        return state * decay_c + kv_n, state

    _, r_prev = lax.scan(step, jnp.zeros_like(kv[:, :, 0]), jnp.moveaxis(kv, 2, 0))
    r_prev = jnp.moveaxis(r_prev, 0, 2)
    y_cross = jnp.einsum('bhncd,bhnde->bhnce', qc, r_prev) * xi[None, :, None, :, None].astype(q.dtype)
    y = (y_inner + y_cross).reshape(b, h, s, dv)

    yf = y.astype(jnp.float32)
    mu = jnp.mean(yf, axis=-1, keepdims=True)
    var = jnp.mean(jnp.square(yf - mu), axis=-1, keepdims=True)
    return ((yf - mu) * lax.rsqrt(var + GN_EPS)).astype(v.dtype)

def _token_mixer(h, positions, w_in, mla_q_norm_w, mla_w_uq, mla_kv_norm_w, mla_w_ukv,
                 ret_gn_w, w_branch_mla, w_branch_ret, w_out):
    b, s, _ = h.shape
    proj = h @ w_in
    c_q, c_kv, k_rope_raw, rq, rk, rv, rg, gate_mla, gate_ret = jnp.split(proj, _split_points(), axis=-1)

    q = (_rmsnorm(c_q, mla_q_norm_w) @ mla_w_uq).reshape(b, s, MLA_HEADS, MLA_NOPE + MLA_ROPE)
    q = jnp.concatenate([q[..., :MLA_NOPE], _rope(q[..., MLA_NOPE:], positions)], axis=-1)
    kv = (_rmsnorm(c_kv, mla_kv_norm_w) @ mla_w_ukv).reshape(b, s, MLA_HEADS, MLA_NOPE + MLA_V)
    k_nope, v_mla = kv[..., :MLA_NOPE], kv[..., MLA_NOPE:]
    k_rope = _rope(k_rope_raw[:, :, None, :], positions)
    k = jnp.concatenate([k_nope, jnp.broadcast_to(k_rope, (b, s, MLA_HEADS, MLA_ROPE))], axis=-1)
    o_mla = _causal_attention(q.transpose(0, 2, 1, 3), k.transpose(0, 2, 1, 3),
                              v_mla.transpose(0, 2, 1, 3), 1.0 / math.sqrt(MLA_NOPE + MLA_ROPE))
    o_mla = o_mla.transpose(0, 2, 1, 3).reshape(b, s, MLA_HEADS * MLA_V) @ w_branch_mla

    rq = _rope(rq.reshape(b, s, RET_HEADS, RET_DK), positions).transpose(0, 2, 1, 3)
    rk = (_rope(rk.reshape(b, s, RET_HEADS, RET_DK), positions) * (RET_DK ** -0.5)).transpose(0, 2, 1, 3)
    rv = rv.reshape(b, s, RET_HEADS, RET_DV).transpose(0, 2, 1, 3)
    y_ret = _chunkwise_retention(rq, rk, rv).transpose(0, 2, 1, 3).reshape(b, s, RET_HEADS * RET_DV)
    o_ret = (jax.nn.silu(rg) * (y_ret * ret_gn_w)) @ w_branch_ret

    merged = jax.nn.sigmoid(gate_mla) * o_mla + jax.nn.sigmoid(gate_ret) * o_ret
    return merged @ w_out

def setup_inputs(seed: int = 0) -> dict:
    key = jax.random.key(seed)
    ks = jax.random.split(key, 24)
    f32 = jnp.float32

    def w(k, shape, fan_in):
        return jax.random.normal(k, (DEPTH,) + shape, f32) * (fan_in ** -0.5)

    def gain(k, n):
        return 1.0 + 0.02 * jax.random.normal(k, (DEPTH, n), f32)

    return {
        "x": jax.random.normal(ks[0], (BATCH, SEQ, D_MODEL), f32),
        "positions": jnp.broadcast_to(jnp.arange(SEQ, dtype=jnp.int32), (BATCH, SEQ)),
        "ffn1_pre_w": gain(ks[1], D_MODEL),
        "ffn1_w1": w(ks[2], (D_MODEL, 2 * FF_DIM), D_MODEL),
        "ffn1_w2": w(ks[3], (FF_DIM, D_MODEL), FF_DIM),
        "ffn1_post_w": gain(ks[4], D_MODEL),
        "mix_pre_w": gain(ks[5], D_MODEL),
        "w_in": w(ks[6], (D_MODEL, IN_WIDTH), D_MODEL),
        "mla_q_norm_w": gain(ks[7], MLA_Q_RANK),
        "mla_w_uq": w(ks[8], (MLA_Q_RANK, MLA_HEADS * (MLA_NOPE + MLA_ROPE)), MLA_Q_RANK),
        "mla_kv_norm_w": gain(ks[9], MLA_KV_RANK),
        "mla_w_ukv": w(ks[10], (MLA_KV_RANK, MLA_HEADS * (MLA_NOPE + MLA_V)), MLA_KV_RANK),
        "ret_gn_w": gain(ks[11], RET_HEADS * RET_DV),
        "w_branch_mla": w(ks[12], (MLA_HEADS * MLA_V, D_MODEL), MLA_HEADS * MLA_V),
        "w_branch_ret": w(ks[13], (RET_HEADS * RET_DV, D_MODEL), RET_HEADS * RET_DV),
        "w_out": w(ks[14], (D_MODEL, D_MODEL), D_MODEL),
        "mix_post_w": gain(ks[15], D_MODEL),
        "ffn2_pre_w": gain(ks[16], D_MODEL),
        "ffn2_w1": w(ks[17], (D_MODEL, 2 * FF_DIM), D_MODEL),
        "ffn2_w2": w(ks[18], (FF_DIM, D_MODEL), FF_DIM),
        "ffn2_post_w": gain(ks[19], D_MODEL),
    }

def reference(x, positions, ffn1_pre_w, ffn1_w1, ffn1_w2, ffn1_post_w, mix_pre_w, w_in,
              mla_q_norm_w, mla_w_uq, mla_kv_norm_w, mla_w_ukv, ret_gn_w, w_branch_mla,
              w_branch_ret, w_out, mix_post_w, ffn2_pre_w, ffn2_w1, ffn2_w2, ffn2_post_w):
    h = x
    for l in range(DEPTH):
        f = _swiglu(_rmsnorm(h, ffn1_pre_w[l]), ffn1_w1[l], ffn1_w2[l])
        h = h + 0.5 * _rmsnorm(f, ffn1_post_w[l])
        m = _token_mixer(_rmsnorm(h, mix_pre_w[l]), positions, w_in[l], mla_q_norm_w[l], mla_w_uq[l],
                         mla_kv_norm_w[l], mla_w_ukv[l], ret_gn_w[l], w_branch_mla[l],
                         w_branch_ret[l], w_out[l])
        h = h + _rmsnorm(m, mix_post_w[l])
        f = _swiglu(_rmsnorm(h, ffn2_pre_w[l]), ffn2_w1[l], ffn2_w2[l])
        h = h + 0.5 * _rmsnorm(f, ffn2_post_w[l])
    return h


_drawn_inputs = setup_inputs


def setup_inputs(seed=0):
    import zlib

    import numpy as np

    out = dict(_drawn_inputs(seed))
    spreads = {}
    factors = {'ffn1_post_w': 3.93,
     'mla_q_norm_w': 8.0,
     'mla_kv_norm_w': 8.0,
     'ret_gn_w': 32.568,
     'mix_post_w': 11.041,
     'ffn2_pre_w': 19.289,
     'ffn2_post_w': 34.744}
    for name, (base, spread) in spreads.items():
        noise = np.random.default_rng([zlib.crc32(name.encode()), seed]).standard_normal(out[name].shape)
        drawn = base * np.exp(spread * noise) if base else spread * noise
        out[name] = __import__('jax').numpy.asarray(drawn.astype(out[name].dtype))
    for name, factor in factors.items():
        out[name] = (out[name] * factor).astype(out[name].dtype)
    return out
```

```python
import math

import concourse.bass as bass
from concourse import mybir

F32 = mybir.dt.float32
F32R = mybir.dt.float32r
BF16 = mybir.dt.bfloat16
I32 = mybir.dt.int32
ACT = mybir.ActivationFunctionType
ALU = mybir.AluOpType
AX = mybir.AxisListType

P = 128
D = 1024
KD = D // P
T = 512
TB = T // P
FF = 2816
NJ = FF // P
HALF = NJ // 2
QR, KVR = 384, 256
NQ, NKV = QR // P, KVR // P
HEADS, NOPE, ROPE, DV = 8, 64, 32, 64
DQK = NOPE + ROPE
RH, RDK, RDV = 4, 64, 128
EPS = 1e-6
ROPE_BASE = 10000.0
MASKED = -1e30

UNIT = KD * P
UNIT2 = HALF * P
HEAD_UNIT = (NQ + NKV) * P
W1_UNITS, W2_UNITS = 2 * NJ, 2 * KD

MIX = (["cq0", "cq1", "cq2", "ckv0", "ckv1", "kr", "rq0", "rq1", "rk0", "rk1"]
       + [f"rv{i}" for i in range(4)] + [f"rg{i}" for i in range(4)] + ["v", "head0"])
FILL = [["br0", "br1", "br2", "br3"], ["gr0"], ["gr1"], ["gr2"], ["gr3"], ["gr4"], ["gr5"], ["gr6", "gr7"]]
for _h in range(HEADS):
    if _h + 1 < HEADS:
        MIX.append(f"head{_h + 1}")
    MIX += FILL[_h]
for _i in range(4):
    MIX += [f"bm{_i}", f"gm{2 * _i}", f"gm{2 * _i + 1}"]
MIX += [f"wo{m}" for m in range(KD)]
UF1 = 0
UM = UF1 + W1_UNITS + W2_UNITS
UF2 = UM + len(MIX)
U_END = UF2 + W1_UNITS + W2_UNITS
UNIT_OF = {name: UM + i for i, name in enumerate(MIX)}

PRE1, POST1, PREM, CQ, CKV, GN, POSTM, PRE2, POST2 = 0, 1, 2, 3, 4, 5, 9, 10, 11
CHUNKS = [KD, KD, KD, NQ, NKV, 1, 1, 1, 1, KD, KD, KD]
SQ0 = [sum(CHUNKS[:n]) for n in range(len(CHUNKS) + 1)]
AC0 = [SQ0[n] - n for n in range(len(CHUNKS) + 1)]

COLS, _at = {}, 0
for _name, _n in (("pre1", KD), ("post1", KD), ("prem", KD), ("qn", NQ), ("kvn", NKV), ("gn", RH), ("postm", KD),
                  ("pre2", KD), ("post2", KD), ("eps", 1), ("eps4", 1), ("freq_m", 1), ("sign_m", 1),
                  ("freq_r", 1), ("sign_r", 1), ("half_pi", 1)):
    COLS[_name] = _at
    _at += _n
NCOLS = _at

ROW_AT = {512: 0, 384: 512, 128: 896, 256: 1024}
TRI = 1280



def pi_parts(n):
    rest, out = 2 * math.pi, []
    for i in range(n):
        step = 2.0 ** (-9 - 12 * i)
        part = math.floor(rest / step) * step if i < n - 1 else rest
        out.append(part)
        rest -= part
    return out


BANK = {"cq0": 0, "cq1": 1, "cq2": 2, "ckv0": 3, "ckv1": 0, "kr": 1, "rq0": 0, "rq1": 1, "rk0": 0, "rk1": 1,
        "rv0": 2, "rv1": 3, "rv2": 4, "rv3": 5, "rg0": 0, "rg1": 1, "rg2": 0, "rg3": 1,
        "v0": 2, "v1": 3, "v2": 4, "v3": 0, "q0": 1, "k0": 0}


def build(nc, x, pos, wf1a, wf1b, wmix, wf2a, wf2b, cols, consts, decay, out):
    h1_dram = nc.dram_tensor("h1_spill", (P, KD, T), F32, kind="Internal").ap()
    base = -(-nc.sbuf_base // 128) * 128
    top = [base]

    def at(name, shape, dt, offset):
        return nc.alloc_sbuf_tensor_at(name, shape, dt, offset=offset)

    def place(name, shape, dt):
        size = (math.prod(shape[1:]) * 4 + 31) // 32 * 32
        top[0] += size
        return at(name, shape, dt, top[0] - size)

    raw = [place(f"raw{s}", [P, UNIT2], F32) for s in range(2)]
    whi = [place(f"whi{s}", [P, UNIT2], F32R) for s in range(4)]
    wlo = [place(f"wlo{s}", [P, UNIT2], F32R) for s in range(4)]
    xh_at = top[0]
    xh = place("xh", [P, KD, T], F32R)
    xl = place("xl", [P, KD, T], F32R)
    fo = at("fo", [P, KD, T], F32, xh_at)
    sq = [place(f"sq{s}", [P, T], F32) for s in range(2)]
    av = [place(f"av{s}", [P, T], F32) for s in range(2)]
    acc = place("acc", [P, T], F32)
    rsb = place("rsb", [P, T], F32)
    dg = place("dg", [P, TB, P], F32)
    cst = place("cst", [P, 2 * P], F32)
    ones, ident = cst[:, 0:P], cst[:, P:2 * P]
    gain = place("gain", [P, NCOLS], F32)
    rms = place("rms", [P, TB], F32)
    rcol = place("rcol", [P, TB], F32)
    rscol = place("rscol", [P, TB], F32)
    mx = place("mx", [P, TB], F32)
    nmx = place("nmx", [P, TB], F32)
    lsum = place("lsum", [P, TB], F32)
    linv = place("linv", [P, TB], F32)
    u = -(-top[0] // 64) * 64

    ah = at("ah", [P, NJ, T], F32R, u)
    al = at("al", [P, NJ, T], F32R, u + 45056)
    hres = at("hres", [P, KD, T], F32, u + 90112)
    assert u + 90112 + 16384 <= nc.sbuf_usable_end, (u, nc.sbuf_usable_end)
    maskb = at("maskb", [P, P], BF16, u)
    identb = at("identb", [P, P], BF16, u + 256)
    rope_m = at("rope_m", [P, T], F32, u + 512)
    cnh = at("cnh", [P, NQ + NKV, T], F32R, u + 2560)
    cnl = at("cnl", [P, NQ + NKV, T], F32R, u + 12800)
    kr = at("kr", [P, T], F32, u + 23040)
    cos_r = at("cos_r", [P, T], F32, u + 25088)
    sin_r = at("sin_r", [P, T], F32, u + 27136)
    rh = at("rh", [P, 4, T], F32R, u + 29184)
    rl = at("rl", [P, 4, T], F32R, u + 37376)
    rvh = at("rvh", [P, TB, T], F32R, u + 45568)
    rvl = at("rvl", [P, TB, T], F32R, u + 53760)
    st = at("st", [P, TRI], F32, u + 61952)
    sth = at("sth", [P, TRI], F32R, u + 67072)
    stl = at("stl", [P, TRI], F32R, u + 72192)
    angle = at("angle", [P, 2, T], F32, u + 61952)
    turns = at("turns", [P, 2, T], F32, u + 66048)
    turns_hi = at("turns_hi", [P, 2, T], F32, u + 70144)
    posi = at("posi", [P, T], I32, u + 74240)
    cf = at("cf", [P, NQ + NKV, T], F32, u + 77312)
    trif = at("trif", [P, P], F32, u + 87552)
    srg = at("srg", [P, RH, T], F32, u + 77312)
    yc = [at(f"yc{s}", [P, T], F32, u + 85504 + 2048 * s) for s in range(2)]
    dec = at("dec", [P, RH, T], F32, u + 89600)
    yh = at("yh", [P, 4, T], F32R, u + 89600)
    yl = at("yl", [P, 4, T], F32R, u + 97792)
    vh = at("vh", [P, TB, T], F32R, u + 25088)
    vl = at("vl", [P, TB, T], F32R, u + 33280)
    qh = at("qh", [P, T], F32R, u + 41472)
    ql = at("ql", [P, T], F32R, u + 43520)
    kh = at("kh", [P, T], F32R, u + 45568)
    kl = at("kl", [P, T], F32R, u + 47616)
    qf = at("qf", [P, T], F32, u + 49664)
    pr = at("pr", [P, TRI], F32, u + 51712)
    pth = at("pth", [P, TRI], F32R, u + 56832)
    ptl = at("ptl", [P, TRI], F32R, u + 61952)
    mret = at("mret", [P, KD, T], F32, u + 69120)
    mh = at("mh", [P, KD, T], F32R, u + 2560)
    ml = at("ml", [P, KD, T], F32R, u + 18944)

    psum = nc.alloc_psum_tensor("psum", [P, 8, T], F32)
    tri = psum[:, 2:5, :].rearrange("p b t -> p (b t)")
    COL, BC = 6, 7

    def g(name, i=0, rows=slice(0, P)):
        return gain[rows, COLS[name] + i:COLS[name] + i + 1]

    names = ("raw_even raw_odd cols_landed hi_ready lo_ready unit_used x0 x1 x2 x3 xh_ready xl_ready sq_ready "
             "acc_ready col_ready rms_ready rc_ready dg_ready bc_ready rsb_ready rscol_ready gs_ready silu_ready sgr_ready a_ready "
             "ah_ready al_ready f_copied fs_ready h_ready spilled pos_landed tri_landed decay_landed mask_ready "
             "chain rope_args sin_ready cos_scaled evac_done cn_scaled cnh_ready cnl_ready rot_ready rh_ready rl_ready rvh_ready "
             "silu_rg sr_done st_ready sth_ready stl_ready y_done yf_ready mu_done yc_ready yg_ready yh_ready "
             "yl_ready vh_ready kr_split qrot_ready qf_ready qh_ready kh_ready s_done nmx_ready exp_ready "
             "p_ready pt_done pth_ready ptl_ready pv_done oh_ready ol_ready tanh_ready merged_in mh_ready ml_ready "
             "h1_back out_landed").split()
    S = {n: nc.alloc_semaphore(n) for n in names}

    def s3(e, lhs_hi, lhs_lo, rhs_hi, rhs_lo, dst, start, stop):
        e.matmul(dst, lhs_hi, rhs_hi, start=start, stop=False, skip_group_check=True)
        e.matmul(dst, lhs_hi, rhs_lo, start=False, stop=False, skip_group_check=True)
        return e.matmul(dst, lhs_lo, rhs_hi, start=False, stop=stop, skip_group_check=True)

    EV = ["cq0", "cq1", "cq2", "ckv0", "ckv1", "kr", "rq0", "rq1", "rk0", "rk1", "rv0", "rv1", "rv2", "rv3",
          "rg0", "rg1", "rg2", "rg3", "v0", "v1", "v2", "v3", "k0", "q0"]
    bank, turn = dict(BANK), 0
    for h in range(HEADS):
        if h + 1 < HEADS:
            EV += [f"k{h + 1}", f"q{h + 1}"]
            bank[f"q{h + 1}"], bank[f"k{h + 1}"] = turn % 2, (turn + 1) % 2
            turn += 2
        for f in FILL[h]:
            for part in ([f + "a", f + "b"] if f[:2] == "br" else [f]):
                EV.append(part)
                bank[part] = turn % 2
                turn += 1
    for i in range(4):
        for m in (2 * i, 2 * i + 1):
            EV += [f"gm{m}", f"bm{m}"]
            bank[f"gm{m}"], bank[f"bm{m}"] = m % 2, 2 + m % 2
    evac = {n: i + 1 for i, n in enumerate(EV)}

    def free(e, name):
        before = [n for n in EV[:evac[name] - 1] if bank[n] == bank[name]]
        if before:
            e.wait_ge(S["evac_done"], evac[before[-1]])

    def unit_size(n):
        if n >= UF2:
            return UNIT if n < UF2 + W1_UNITS else UNIT2
        if n >= UM:
            return HEAD_UNIT if MIX[n - UM].startswith("head") else UNIT
        return UNIT if n < W1_UNITS else UNIT2


    def load(e, src, n0, adv=0):
        s = n0 % 2
        if n0 >= 2:
            e.wait_ge(S["lo_ready"], adv + n0 - 1)
        e.dma_start(raw[s][:, 0:src.shape[-1]], src).then_inc(S["raw_odd" if s else "raw_even"], 16)

    def split_hi(e, n0, adv=0, half_adv=0, size=None):
        if not isinstance(adv, int) or n0 < U_END:
            size = size or unit_size(n0)
            s = n0 % 2
            e.wait_ge(S["raw_odd" if s else "raw_even"], half_adv * 16 + 16 * (n0 // 2 + 1))
            if n0 >= 4:
                e.wait_ge(S["unit_used"], adv + n0 - 3)
            e.activation(whi[n0 % 4][:, 0:size], raw[s][:, 0:size], ACT.Copy).then_inc(S["hi_ready"], 1)

    def split_lo(e, n0, adv=0, size=None):
        if not isinstance(adv, int) or n0 < U_END:
            size = size or unit_size(n0)
            e.wait_ge(S["hi_ready"], adv + n0 + 1)
            e.tensor_tensor(wlo[n0 % 4][:, 0:size], raw[n0 % 2][:, 0:size],
                            whi[n0 % 4][:, 0:size].bitcast(F32), ALU.subtract).then_inc(S["lo_ready"], 1)

    def tile(n0, k):
        return whi[n0 % 4][:, P * k:P * k + P], wlo[n0 % 4][:, P * k:P * k + P]

    def square(e, n, i, src):
        idx = SQ0[n] + i
        if i >= 2:
            e.wait_ge(S["acc_ready"], AC0[n] + i - 1)
        elif n:
            e.wait_ge(S["col_ready"], n)
        e.activation(sq[idx % 2][:], src, ACT.Square).then_inc(S["sq_ready"], 1)

    def accumulate(e, n, i):
        if i >= CHUNKS[n] - 1:
            return
        e.wait_ge(S["sq_ready"], SQ0[n] + i + 1)
        src = sq[(SQ0[n] + i) % 2][:]
        if i == 0:
            if n:
                e.wait_ge(S["col_ready"], n)
            e.tensor_copy(acc[:], src).then_inc(S["acc_ready"], 1)
        else:
            e.wait_ge(S["acc_ready"], AC0[n] + i)
            e.tensor_tensor(acc[:], acc[:], src, ALU.add).then_inc(S["acc_ready"], 1)

    def sum_columns(e, n):
        if AC0[n + 1]:
            e.wait_ge(S["acc_ready"], AC0[n + 1])
        e.wait_ge(S["sq_ready"], SQ0[n + 1])
        if n:
            e.wait_ge(S["rms_ready"], n)
        last_sq = sq[(SQ0[n + 1] - 1) % 2]
        for b in range(TB):
            if CHUNKS[n] > 1:
                e.matmul(psum[:, COL, b:b + 1], acc[:, P * b:P * b + P], ones[:, 0:1], start=True, stop=False)
            mm = e.matmul(psum[:, COL, b:b + 1], last_sq[:, P * b:P * b + P], ones[:, 0:1],
                          start=CHUNKS[n] == 1, stop=True)
        mm.then_inc(S["col_ready"], 1)

    def root(e, n, width, halve=False):
        e.wait_ge(S["col_ready"], n + 1)
        if n:
            e.wait_ge(S["rc_ready"], n)
        f = 4.0 if halve else 1.0
        e.activation(rms[:], psum[:, COL, 0:TB], ACT.Sqrt, bias=g("eps4" if halve else "eps"),
                     scale=f / width).then_inc(S["rms_ready"], 1)

    def invert(e, n):
        e.wait_ge(S["rms_ready"], n + 1)
        if n:
            e.wait_ge(S["dg_ready"], n)
        e.reciprocal(rcol[:], rms[:]).then_inc(S["rc_ready"], 1)
        e.wait_ge(S["rc_ready"], n + 1)
        if n:
            e.wait_ge(S["bc_ready"], n)
        e.tensor_tensor(dg[:], ident[:, None, :].broadcast_to([P, TB, P]),
                        rcol[:, :, None].broadcast_to([P, TB, P]), ALU.mult).then_inc(S["dg_ready"], 1)

    def broadcast(e, n):
        e.wait_ge(S["dg_ready"], n + 1)
        if n in (POST1 + 1, POSTM + 1):
            e.wait_ge(S["h_ready"], 8 if n == PREM else 16)
        elif n in (POST1, CQ, POST2):
            e.wait_ge(S["rsb_ready"], {POST1: 1, CQ: 2, POST2: 3}[n])
        elif n == CKV:
            e.wait_ge(S["cn_scaled"], NQ)
        elif n == GN:
            e.wait_ge(S["yc_ready"], 1)
        e.matmul(psum[:, BC, :], ones, dg[:].rearrange("p b t -> p (b t)"), start=True,
                 stop=True).then_inc(S["bc_ready"], 1)

    def keep_rs(e, n, k):
        e.wait_ge(S["bc_ready"], n + 1)
        if k == 1:
            e.wait_ge(S["al_ready"], NJ)
        if k == 2:
            e.wait_ge(S["evac_done"], len(EV))
        e.activation(rsb[:], psum[:, BC, :], ACT.Copy).then_inc(S["rsb_ready"], 1)

    X_SEM = ("x0", "x1", "x2", "x3")
    PRE = ("pre1", "prem", "pre2")
    PRE_N = (PRE1, PREM, PRE2)
    POST_N = (POST1, POSTM, POST2)

    def have_h(e, s, k):
        if s == 0:
            e.wait_ge(S[X_SEM[k // 2]], 16)
        else:
            e.wait_ge(S["h_ready"], 8 * (s - 1) + k + 1)

    def enter_act(e, s, k):
        have_h(e, s, k)
        e.activation(xh[:, k, :], hres[:, k, :], ACT.Copy, scale=g(PRE[s], k)).then_inc(S["xh_ready"], 1)
        square(e, PRE_N[s], k, hres[:, k, :])

    def enter_dve(e, s, k):
        e.wait_ge(S["xh_ready"], 8 * s + k + 1)
        e.scalar_tensor_tensor(out=xl[:, k, :], in0=hres[:, k, :], scalar=g(PRE[s], k),
                               in1=xh[:, k, :].bitcast(F32), op0=ALU.mult, op1=ALU.subtract).then_inc(S["xl_ready"], 1)
        accumulate(e, PRE_N[s], k)

    def exit_dve(e, s, k):
        if k == 0:
            e.wait_ge(S["bc_ready"], POST_N[s] + 1)
            if s == 1:
                e.wait_ge(S["h1_back"], 16)
        e.tensor_tensor(fo[:, k, :], fo[:, k, :], psum[:, BC, :], ALU.mult).then_inc(S["fs_ready"], 1)
        e.wait_ge(S["fs_ready"], 8 * s + k + 1)
        e.tensor_tensor(hres[:, k, :], hres[:, k, :], fo[:, k, :], ALU.add).then_inc(S["h_ready"], 1)

    def sync_ffn(sp, wa, wb, n0):
        if n0:
            for c in range(4):
                load(sp, wa[c], n0 + c)
        else:
            for c in range(2, 4):
                load(sp, wa[c], c)
        with sp.Fori(0, W1_UNITS // 4 - 1) as i:
            for c in range(4):
                load(sp, wa[4 * i + (4 + c)], n0 + 4 + c, 4 * i)
        with sp.Fori(0, W2_UNITS // 4) as i:
            for c in range(4):
                load(sp, wb[4 * i + c], n0 + W1_UNITS + c, 4 * i)

    block = nc.Block()
    with block as block:
        @block.sync
        def _(sp):
            load(sp, wf1a[0], 0)
            sp.dma_start(gain[:], cols).then_inc(S["cols_landed"], 16)
            sp.dma_start(cst[:], consts[:, 0:2 * P]).then_inc(S["cols_landed"], 16)
            for c in range(4):
                sp.dma_start(hres[:, 2 * c:2 * c + 2, :], x[:, 2 * c:2 * c + 2, :]).then_inc(S[X_SEM[c]], 16)
                if c == 0:
                    load(sp, wf1a[1], 1)
            sync_ffn(sp, wf1a, wf1b, UF1)
            for n in range(UM, UF2):
                load(sp, wmix[n - UM][:, 0:unit_size(n)], n)
            sync_ffn(sp, wf2a, wf2b, UF2)
            for k in range(KD):
                sp.wait_ge(S["h_ready"], 16 + k + 1)
                sp.dma_start(out[:, k, :], hres[:, k, :]).then_inc(S["out_landed"], 16)
            sp.wait_ge(S["out_landed"], 16 * KD)

        @block.tensor
        def _(pe):
            def first_units(s, n0, banks):
                for c in range(4):
                    pe.wait_ge(S["lo_ready"], n0 + c + 1)
                for k in range(KD):
                    pe.wait_ge(S["xl_ready"], 8 * s + k + 1)
                    if k == KD - 1:
                        sum_columns(pe, PRE_N[s])
                    for c in range(4):
                        hi, lo = tile(n0 + c, k)
                        mm = s3(pe, hi, lo, xh[:, k, :], xl[:, k, :], psum[:, banks[c], :], k == 0, k == KD - 1)
                        if k == KD - 1:
                            mm.then_inc(S["unit_used"], 1)
                        if k == KD - 1 and c == 1:
                            broadcast(pe, PRE_N[s])

            def unit8(n0, adv, dst, hi_in, lo_in):
                pe.wait_ge(S["lo_ready"], adv + n0 + 1)
                for k in range(KD):
                    hi, lo = tile(n0, k)
                    mm = s3(pe, hi, lo, hi_in[:, k, :], lo_in[:, k, :], dst, k == 0, k == KD - 1)
                mm.then_inc(S["unit_used"], 1)

            def ffn(f, n0):
                s, j0 = (0, 2)[f], NJ * f
                if f:
                    pe.wait_ge(S["f_copied"], 2 * KD)
                first_units(s, n0, (0, 2, 1, 3))
                with pe.Fori(1, NJ // 2) as i:
                    for c in range(2):
                        pe.wait_ge(S["a_ready"], 2 * i + (j0 + c - 1))
                        for half in range(2):
                            unit8(n0 + 2 * c + half, 4 * i, psum[:, c + 2 * half, :], xh, xl)
                nb = n0 + W1_UNITS
                sq0 = SQ0[POST_N[s]]

                def out_chunks(i, first=False):
                    for c in range(2):
                        if not first:
                            pe.wait_ge(S["sq_ready"], 2 * i + (sq0 + c - 1))
                        for half in range(2):
                            pe.wait_ge(S["lo_ready"], 4 * i + (nb + 2 * c + half + 1))
                            for k in range(HALF):
                                j = HALF * half + k
                                if first and c == 0:
                                    pe.wait_ge(S["al_ready"], j0 + j + 1)
                                hi, lo = tile(nb + 2 * c + half, k)
                                mm = s3(pe, hi, lo, ah[:, j, :], al[:, j, :], psum[:, 4 + c, :],
                                        j == 0, j == NJ - 1)
                            mm.then_inc(S["unit_used"], 1)

                out_chunks(0, first=True)
                with pe.Fori(1, KD // 2) as i:
                    out_chunks(i)
                sum_columns(pe, POST_N[s])
                broadcast(pe, POST_N[s])

            def product(name, srcs, n0, tiles, done=True):
                free(pe, name)
                for i, (k, (hi_in, lo_in)) in enumerate(zip(tiles, srcs)):
                    hi, lo = tile(n0, k)
                    mm = s3(pe, hi, lo, hi_in, lo_in, psum[:, bank[name], :], i == 0, i == len(tiles) - 1)
                if done:
                    mm.then_inc(S["unit_used"], 1)

            X8 = [(xh[:, k, :], xl[:, k, :]) for k in range(KD)]

            def project(name):
                n0 = UNIT_OF[name]
                pe.wait_ge(S["lo_ready"], n0 + 1)
                product(name, X8, n0, range(KD))

            def head_unit(h):
                n0 = UNIT_OF[f"head{h}"]
                pe.wait_ge(S["lo_ready"], n0 + 1)
                if h == 0:
                    pe.wait_ge(S["cnl_ready"], NQ + NKV)
                product(f"k{h}", [(cnh[:, NQ + k, :], cnl[:, NQ + k, :]) for k in range(NKV)], n0,
                        range(NQ, NQ + NKV), done=False)
                product(f"q{h}", [(cnh[:, k, :], cnl[:, k, :]) for k in range(NQ)], n0, range(NQ))

            def ret_scores(h):
                c, r = h // 2, slice(64 * (h % 2), 64 * (h % 2) + 64)
                if h == 0:
                    pe.wait_ge(S["rl_ready"], 4)
                    pe.wait_ge(S["evac_done"], evac["rv2"])
                else:
                    pe.wait_ge(S["st_ready"], h)
                for b in range(TB):
                    n = T - P * b
                    blk = slice(P * b, P * b + P)
                    mm = s3(pe, rh[r, 2 + c, blk], rl[r, 2 + c, blk], rh[r, c, P * b:], rl[r, c, P * b:],
                            tri[:, ROW_AT[n]:ROW_AT[n] + n], True, True)
                mm.then_inc(S["sr_done"], 1)

            def ret_out(h):
                pe.wait_ge(S["stl_ready"], h + 1)
                if h == 0:
                    pe.wait_ge(S["evac_done"], evac["rv3"])
                else:
                    pe.wait_ge(S["yf_ready"], h)
                for b in range(TB):
                    n = T - P * b
                    row = slice(ROW_AT[n], ROW_AT[n] + n)
                    cols_h = slice(RDV * h, RDV * h + RDV)
                    mm = s3(pe, rvh[:, b, cols_h], rvl[:, b, cols_h], sth[:, row], stl[:, row],
                            psum[:, 5, P * b:], b == 0, b == TB - 1)
                mm.then_inc(S["y_done"], 1)

            def ret_mean(h):
                pe.wait_ge(S["yf_ready"], h + 1)
                if h == 0:
                    pe.wait_ge(S["cn_scaled"], NQ + NKV)
                else:
                    pe.wait_ge(S["yg_ready"], 2 * h - 1)
                pe.matmul(psum[:, BC, :], ones, yc[h % 2][:], start=True, stop=True).then_inc(S["mu_done"], 1)

            def ret_norm(h):
                pe.wait_ge(S["yc_ready"], h + 1)
                broadcast(pe, GN + h)

            def scores(h):
                pe.wait_ge(S["evac_done"], evac[f"q{h}"])
                if h == 0:
                    pe.wait_ge(S["kr_split"], 2)
                    pe.wait_ge(S["mask_ready"], 2)
                    pe.wait_ge(S["evac_done"], evac["v2"])
                else:
                    pe.wait_ge(S["ptl_ready"], h)
                for i in range(TB):
                    n = P * (i + 1)
                    a = ROW_AT[n]
                    q = slice(P * i, P * i + P)
                    s3(pe, qh[0:DQK, q], ql[0:DQK, q], kh[0:DQK, 0:n], kl[0:DQK, 0:n], tri[:, a:a + n], True, False)
                    mm = pe.matmul(tri[:, a + n - P:a + n], identb[:], maskb[:], start=False, stop=True,
                                   skip_group_check=True)
                mm.then_inc(S["s_done"], 1)

            def turn_probs(h):
                pe.wait_ge(S["p_ready"], h + 1)
                for b in range(TB):
                    for i in range(b, TB):
                        src = ROW_AT[P * (i + 1)] + P * b
                        dst = ROW_AT[T - P * b] + P * (i - b)
                        mm = pe.transpose(tri[:, dst:dst + P], pr[:, src:src + P], ident)
                mm.then_inc(S["pt_done"], 1)

            def attend(h):
                pe.wait_ge(S["ptl_ready"], h + 1)
                if h == 0:
                    pe.wait_ge(S["yf_ready"], RH)
                elif h == 1:
                    pe.wait_ge(S["yg_ready"], 2 * RH)
                else:
                    pe.wait_ge(S["ol_ready"], h - 1)
                for b in range(TB):
                    n = T - P * b
                    row = slice(ROW_AT[n], ROW_AT[n] + n)
                    pair = slice(P * (h // 2), P * (h // 2) + P)
                    mm = s3(pe, vh[:, b, pair], vl[:, b, pair], pth[:, row], ptl[:, row],
                            psum[:, 5 + 2 * (h % 2), P * b:], b == 0, b == TB - 1)
                mm.then_inc(S["pv_done"], 1)

            def fill(name):
                n0 = UNIT_OF[name]
                if name[:2] == "gr":
                    project(name)
                    return
                pe.wait_ge(S["lo_ready"], n0 + 1)
                pe.wait_ge(S["yl_ready"], RH)
                for half, part in enumerate("ab"):
                    product(name + part, [(yh[:, k, :], yl[:, k, :]) for k in range(4)], n0,
                            range(4 * half, 4 * half + 4), done=half == 1)

            pe.wait_ge(S["cols_landed"], 32)
            ffn(0, UF1)

            first_units(1, UM, (0, 1, 2, 3))
            project("ckv1")
            sum_columns(pe, CQ)
            project("kr")
            broadcast(pe, CQ)
            project("rq0")
            sum_columns(pe, CKV)
            project("rq1")
            broadcast(pe, CKV)
            project("rk0")
            project("rk1")
            for i in range(4):
                n0 = UNIT_OF[f"rv{i}"]
                pe.wait_ge(S["lo_ready"], n0 + 1)
                for b in range(TB):
                    if i == 0:
                        free(pe, f"rv{b}")
                        if b >= 2:
                            pe.wait_ge(S["f_copied"], KD)
                    for kk in range(2):
                        k = 2 * i + kk
                        blk = slice(P * b, P * b + P)
                        w = slice(T * kk, T * kk + T)
                        mm = s3(pe, xh[:, k, blk], xl[:, k, blk], whi[n0 % 4][:, w], wlo[n0 % 4][:, w],
                                psum[:, 2 + b, :], k == 0, k == KD - 1)
                mm.then_inc(S["unit_used"], 1)
            for h in range(RH):
                ret_scores(h)
                if h:
                    ret_mean(h - 1)
                project(f"rg{h}")
                if h:
                    sum_columns(pe, GN + h - 1)
                ret_out(h)
                if h:
                    ret_norm(h - 1)
            n0 = UNIT_OF["v"]
            pe.wait_ge(S["lo_ready"], n0 + 1)
            pe.wait_ge(S["cnl_ready"], NQ + NKV)
            pe.wait_ge(S["st_ready"], RH)
            for b in range(TB):
                free(pe, f"v{b}")
                for k in range(NKV):
                    blk = slice(P * b, P * b + P)
                    w = slice(T * k, T * k + T)
                    mm = s3(pe, cnh[:, NQ + k, blk], cnl[:, NQ + k, blk], whi[n0 % 4][:, w], wlo[n0 % 4][:, w],
                            psum[:, bank[f"v{b}"], :], k == 0, k == NKV - 1)
                if b == 1:
                    ret_mean(RH - 1)
            mm.then_inc(S["unit_used"], 1)
            head_unit(0)
            sum_columns(pe, GN + RH - 1)
            for h in range(HEADS):
                scores(h)
                if h == 0:
                    ret_norm(RH - 1)
                if h + 1 < HEADS:
                    head_unit(h + 1)
                fills = FILL[h]
                fill(fills[0])
                turn_probs(h)
                for f in fills[1:]:
                    fill(f)
                attend(h)
            for i in range(4):
                n0 = UNIT_OF[f"bm{i}"]
                pe.wait_ge(S["lo_ready"], n0 + 1)
                if i == 0:
                    pe.wait_ge(S["ol_ready"], HEADS)
                for half in range(2):
                    product(f"bm{2 * i + half}", [(yh[:, k, :], yl[:, k, :]) for k in range(4)], n0,
                            range(4 * half, 4 * half + 4), done=half == 1)
                project(f"gm{2 * i}")
                project(f"gm{2 * i + 1}")
            for m in range(KD):
                n0 = UNIT_OF[f"wo{m}"]
                pe.wait_ge(S["lo_ready"], n0 + 1)
                if m >= 2:
                    pe.wait_ge(S["sq_ready"], SQ0[POSTM] + m - 1)
                for k in range(KD):
                    if m == 0:
                        pe.wait_ge(S["ml_ready"], k + 1)
                    hi, lo = tile(n0, k)
                    mm = s3(pe, hi, lo, mh[:, k, :], ml[:, k, :], psum[:, 4 + m % 2, :], k == 0, k == KD - 1)
                mm.then_inc(S["unit_used"], 1)
            sum_columns(pe, POSTM)
            broadcast(pe, POSTM)

            ffn(1, UF2)

        @block.scalar
        def _(act):
            def ffn(f, n0):
                s, j0 = (0, 2)[f], NJ * f
                for k in range(KD):
                    if f == 0 and k < 4:
                        split_hi(act, n0 + k)
                    enter_act(act, s, k)
                root(act, PRE_N[s], D)
                keep_rs(act, PRE_N[s], s)

                def gates(i, last=False):
                    for c in range(2):
                        j = 2 * i + c
                        size = UNIT2 if last else UNIT
                        split_hi(act, n0 + 4 + 2 * c, 4 * i, 2 * i, size)
                        act.wait_ge(S["gs_ready"], j + (j0 + 1))
                        act.activation(sq[c][:], sq[c][:], ACT.Silu).then_inc(S["silu_ready"], 1)
                        split_hi(act, n0 + 5 + 2 * c, 4 * i, 2 * i, size)
                        act.wait_ge(S["a_ready"], j + (j0 + 1))
                        act.activation(ah[:, j, :], av[c][:], ACT.Copy).then_inc(S["ah_ready"], 1)

                with act.Fori(0, NJ // 2 - 1) as i:
                    gates(i)
                gates(NJ // 2 - 1, last=True)

                nb, n, post = n0 + W1_UNITS, POST_N[s], ("post1", "postm", "post2")[s]

                def out_chunks(i, first=False, last=False):
                    for c in range(2):
                        m = 2 * i + c
                        for half in range(2):
                            nxt = nb + 4 + 2 * c + half
                            if last:
                                split_hi(act, nxt + 4 * i)
                            else:
                                split_hi(act, nxt, 4 * i, 2 * i, UNIT2)
                        act.wait_ge(S["unit_used"], 4 * i + (nb + 2 * c + 2))
                        act.activation(fo[:, m, :], psum[:, 4 + c, :], ACT.Copy,
                                       scale=g(post, m)).then_inc(S["f_copied"], 1)
                        square(act, n, m, psum[:, 4 + c, :])

                for i in range(KD // 2):
                    out_chunks(i, last=i == KD // 2 - 1)
                root(act, n, D, halve=True)

            act.wait_ge(S["cols_landed"], 32)
            ffn(0, UF1)

            def nxt(name, ahead=4):
                split_hi(act, UNIT_OF[name] + ahead)

            for k in range(KD):
                enter_act(act, 1, k)
            root(act, PREM, D)
            keep_rs(act, PREM, 1)
            act.wait_ge(S["rope_args"], 2)
            act.activation(cos_r[:], turns[:, 1, :], ACT.Sin, bias=g("half_pi"), scale=-1.0).then_inc(S["sin_ready"], 1)
            act.activation(sin_r[:], angle[:, 1, :], ACT.Sin, scale=g("sign_r")).then_inc(S["sin_ready"], 1)
            act.activation(rope_m[64:96, :], turns[64:96, 0, :], ACT.Sin, bias=g("half_pi", rows=slice(64, 96)),
                           scale=-1.0).then_inc(S["sin_ready"], 1)
            act.activation(rope_m[96:P, :], angle[96:P, 0, :], ACT.Sin,
                           scale=g("sign_m", rows=slice(96, P))).then_inc(S["sin_ready"], 1)
            nxt("cq0")
            for c in range(NQ):
                act.wait_ge(S["evac_done"], evac[f"cq{c}"])
                square(act, CQ, c, cf[:, c, :])
                nxt(("cq1", "cq2", "ckv0")[c])
            nxt("ckv1")
            root(act, CQ, QR)
            for c in range(NKV):
                act.wait_ge(S["evac_done"], evac[f"ckv{c}"])
                square(act, CKV, c, cf[:, NQ + c, :])
            nxt("kr")

            def latent_hi(c):
                act.wait_ge(S["cn_scaled"], c + 1)
                act.activation(cnh[:, c, :], cf[:, c, :], ACT.Copy,
                               scale=g("qn", c) if c < NQ else g("kvn", c - NQ)).then_inc(S["cnh_ready"], 1)

            def rotated_hi(c4):
                act.wait_ge(S["rot_ready"], c4 + 1)
                act.activation(rh[:, c4, :], av[1][:], ACT.Copy).then_inc(S["rh_ready"], 1)

            for c in range(NQ):
                latent_hi(c)
            nxt("rq0")
            root(act, CKV, KVR)
            rotated_hi(0)
            nxt("rq1")
            rotated_hi(1)
            for c in range(NQ, NQ + NKV):
                latent_hi(c)
            nxt("rk0")
            rotated_hi(2)
            nxt("rk1")
            rotated_hi(3)
            for i in range(4):
                nxt(f"rv{i}")
            for b in range(TB):
                act.wait_ge(S["unit_used"], UNIT_OF["rv3"] + 1)
                if b == 0:
                    act.wait_ge(S["rscol_ready"], 1)
                act.activation(rvh[:, b, :], psum[:, 2 + b, :], ACT.Copy,
                               scale=rscol[:, b:b + 1]).then_inc(S["rvh_ready"], 1)

            def ret_split(h):
                act.wait_ge(S["st_ready"], h + 1)
                if h:
                    act.wait_ge(S["y_done"], h)
                act.activation(sth[:], st[:], ACT.Copy).then_inc(S["sth_ready"], 1)

            def ret_square(h):
                act.wait_ge(S["yc_ready"], h + 1)
                square(act, GN + h, 0, yc[h % 2][:])

            def ret_copy(h):
                act.wait_ge(S["y_done"], h + 1)
                if h == 1:
                    act.wait_ge(S["mask_ready"], 1)
                if h >= 2:
                    act.wait_ge(S["yl_ready"], h - 1)
                act.activation(yc[h % 2][:], psum[:, 5, :], ACT.Copy).then_inc(S["yf_ready"], 1)

            def ret_high(h):
                act.wait_ge(S["yg_ready"], 2 * h + 2)
                act.activation(yh[:, h, :], yc[h % 2][:], ACT.Copy, scale=g("gn", h)).then_inc(S["yh_ready"], 1)

            for h in range(RH):
                ret_split(h)
                if h:
                    ret_square(h - 1)
                nxt(f"rg{h}")
                act.wait_ge(S["evac_done"], evac[f"rg{h}"])
                act.activation(srg[:, h, :], av[h % 2][:], ACT.Silu).then_inc(S["silu_rg"], 1)
                if h:
                    root(act, GN + h - 1, RDV)
                ret_copy(h)
                if h:
                    ret_high(h - 1)
            for b in range(TB):
                act.wait_ge(S["unit_used"], UNIT_OF["v"] + 1)
                act.activation(vh[:, b, :], psum[:, bank[f"v{b}"], :], ACT.Copy).then_inc(S["vh_ready"], 1)
                if b == 1:
                    ret_square(RH - 1)
            nxt("v")
            act.activation(kh[64:96, :], kr[64:96, :], ACT.Copy).then_inc(S["kr_split"], 1)

            def head_split(h):
                act.wait_ge(S["unit_used"], UNIT_OF[f"head{h}"] + 1)
                act.activation(kh[0:NOPE, :], psum[0:NOPE, bank[f"k{h}"], :], ACT.Copy).then_inc(S["kh_ready"], 1)
                act.activation(qf[0:NOPE, :], psum[0:NOPE, bank[f"q{h}"], :], ACT.Copy).then_inc(S["qf_ready"], 1)
                act.wait_ge(S["qrot_ready"], h + 1)
                act.wait_ge(S["qf_ready"], h + 1)
                act.activation(qh[0:DQK, :], qf[0:DQK, :], ACT.Copy).then_inc(S["qh_ready"], 1)

            def fill_act(name):
                nxt(name)
                if name[:2] == "gr":
                    m = int(name[2])
                    act.wait_ge(S["evac_done"], evac[name])
                    act.activation(av[m % 2][:], av[m % 2][:], ACT.Tanh, scale=0.5).then_inc(S["tanh_ready"], 1)

            head_split(0)
            nxt("head0")
            root(act, GN + RH - 1, RDV)
            ret_high(RH - 1)
            scale = 1.0 / math.sqrt(DQK)
            for h in range(HEADS):
                act.wait_ge(S["nmx_ready"], h + 1)
                for i in range(TB):
                    n = P * (i + 1)
                    row = slice(ROW_AT[n], ROW_AT[n] + n)
                    act.activation(pr[:, row], tri[:, row], ACT.Exp, bias=nmx[:, i:i + 1], scale=scale,
                                   accum_out=lsum[:, i:i + 1]).then_inc(S["exp_ready"], 1)
                if h + 1 < HEADS:
                    head_split(h + 1)
                    nxt(f"head{h + 1}")
                fill_act(FILL[h][0])
                act.wait_ge(S["pt_done"], h + 1)
                act.activation(pth[:], tri[:, 0:TRI], ACT.Copy).then_inc(S["pth_ready"], 1)
                for f in FILL[h][1:]:
                    fill_act(f)
                act.wait_ge(S["pv_done"], h + 1)
                r = slice(64 * (h % 2), 64 * (h % 2) + 64)
                act.activation(yh[r, h // 2, :], psum[r, 5 + 2 * (h % 2), :], ACT.Copy).then_inc(S["oh_ready"], 1)
            for i in range(4):
                nxt(f"bm{i}")
                for m in (2 * i, 2 * i + 1):
                    nxt(f"gm{m}")
                    act.wait_ge(S["evac_done"], evac[f"gm{m}"])
                    act.activation(av[m % 2][:], av[m % 2][:], ACT.Tanh, scale=0.5).then_inc(S["tanh_ready"], 1)
                    act.wait_ge(S["merged_in"], m + 1)
                    act.activation(mh[:, m, :], mret[:, m, :], ACT.Copy, scale=0.5).then_inc(S["mh_ready"], 1)
            for m in range(KD):
                nxt(f"wo{m}")
                act.wait_ge(S["unit_used"], UNIT_OF[f"wo{m}"] + 1)
                act.activation(fo[:, m, :], psum[:, 4 + m % 2, :], ACT.Copy,
                               scale=g("postm", m)).then_inc(S["f_copied"], 1)
                square(act, POSTM, m, psum[:, 4 + m % 2, :])
            root(act, POSTM, D)

            ffn(1, UF2)

        @block.vector
        def _(dve):
            def ffn(f, n0):
                s, j0 = (0, 2)[f], NJ * f
                for k in range(KD):
                    if f == 0 and k < 4:
                        split_lo(dve, n0 + k)
                    if f == 1:
                        exit_dve(dve, 1, k)
                    enter_dve(dve, s, k)
                invert(dve, PRE_N[s])
                dve.wait_ge(S["rsb_ready"], s + 1)

                def gates(i, first=False, last=False):
                    for c in range(2):
                        j = 2 * i + c
                        size = UNIT2 if last else UNIT
                        dve.wait_ge(S["unit_used"], 4 * i + (n0 + 2 * c + 1))
                        if not first:
                            dve.wait_ge(S["a_ready"], j + (j0 - 1))
                        dve.tensor_tensor(sq[c][:], psum[:, c, :], rsb[:], ALU.mult).then_inc(S["gs_ready"], 1)
                        split_lo(dve, n0 + 4 + 2 * c, 4 * i, size)
                        dve.wait_ge(S["sgr_ready"], j + (j0 + 1))
                        dve.wait_ge(S["unit_used"], 4 * i + (n0 + 2 * c + 2))
                        dve.tensor_tensor(av[c][:], psum[:, 2 + c, :], av[c][:], ALU.mult).then_inc(S["a_ready"], 1)
                        split_lo(dve, n0 + 5 + 2 * c, 4 * i, size)
                        dve.wait_ge(S["ah_ready"], j + (j0 + 1))
                        dve.tensor_tensor(al[:, j, :], av[c][:], ah[:, j, :].bitcast(F32),
                                          ALU.subtract).then_inc(S["al_ready"], 1)

                gates(0, first=True)
                with dve.Fori(1, NJ // 2 - 1) as i:
                    gates(i)
                gates(NJ // 2 - 1, last=True)
                nb, n = n0 + W1_UNITS, POST_N[s]
                for i in range(KD // 2):
                    for c in range(2):
                        for half in range(2):
                            nxt_u = nb + 4 + 2 * c + half + 4 * i
                            split_lo(dve, nxt_u)
                        accumulate(dve, n, 2 * i + c)
                invert(dve, n)

            dve.wait_ge(S["cols_landed"], 32)
            ffn(0, UF1)

            for k in range(KD):
                exit_dve(dve, 0, k)
                enter_dve(dve, 1, k)
            invert(dve, PREM)
            dve.tensor_copy(rscol[:], rcol[:]).then_inc(S["rscol_ready"], 1)

            chain = [0]

            def link(ins):
                chain[0] += 1
                ins.then_inc(S["chain"], 1)
                dve.wait_ge(S["chain"], chain[0])

            dve.wait_ge(S["pos_landed"], 16)
            for t, name in ((0, "freq_m"), (1, "freq_r")):
                link(dve.tensor_scalar(angle[:, t, :], posi[:], g(name), None, ALU.mult))
            magic = 1.5 * 2.0 ** 23
            link(dve.tensor_scalar(turns[:], angle[:], 1 / (2 * math.pi), magic, ALU.mult, ALU.add))
            link(dve.tensor_scalar(turns[:], turns[:], magic, None, ALU.subtract))
            link(dve.tensor_scalar(turns_hi[:], turns[:], 1 / 4096.0, magic, ALU.mult, ALU.add))
            link(dve.tensor_scalar(turns_hi[:], turns_hi[:], magic, None, ALU.subtract))
            link(dve.scalar_tensor_tensor(out=turns[:], in0=turns_hi[:], scalar=-4096.0, in1=turns[:],
                                          op0=ALU.mult, op1=ALU.add))
            for part in pi_parts(4):
                for src, f in ((turns_hi, 4096.0), (turns, 1.0)):
                    link(dve.scalar_tensor_tensor(out=angle[:], in0=src[:], scalar=-part * f, in1=angle[:],
                                                  op0=ALU.mult, op1=ALU.add))
            link(dve.tensor_scalar(angle[:], angle[:], 3.1415925, -3.1415925, ALU.min, ALU.max))
            dve.scalar_tensor_tensor(out=turns[:], in0=angle[:], scalar=-1.0, in1=angle[:], op0=ALU.mult,
                                     op1=ALU.max).then_inc(S["rope_args"], 2)
            dve.wait_ge(S["rsb_ready"], 2)
            dve.wait_ge(S["sin_ready"], 2)
            dve.tensor_tensor(cos_r[:], cos_r[:], rsb[:], ALU.mult).then_inc(S["cos_scaled"], 1)
            dve.tensor_tensor(sin_r[:], sin_r[:], rsb[:], ALU.mult).then_inc(S["cos_scaled"], 1)

            given = [0]

            def gives(ins, name):
                assert EV[given[0]] == name, (EV[given[0]], name)
                given[0] += 1
                ins.then_inc(S["evac_done"], 1)

            def nxt(name):
                split_lo(dve, UNIT_OF[name] + 4)

            def used(name):
                dve.wait_ge(S["unit_used"], UNIT_OF[name] + 1)

            def latent(name, c):
                used(name)
                gives(dve.tensor_tensor(cf[:, c, :], psum[:, bank[name], :], rsb[:], ALU.mult), name)

            def latent_low(c):
                dve.wait_ge(S["cnh_ready"], c + 1)
                dve.scalar_tensor_tensor(out=cnl[:, c, :], in0=cf[:, c, :],
                                         scalar=g("qn", c) if c < NQ else g("kvn", c - NQ),
                                         in1=cnh[:, c, :].bitcast(F32), op0=ALU.mult,
                                         op1=ALU.subtract).then_inc(S["cnl_ready"], 1)

            def latent_scale(c):
                dve.wait_ge(S["bc_ready"], (CQ if c < NQ else CKV) + 1)
                dve.tensor_tensor(cf[:, c, :], cf[:, c, :], psum[:, BC, :], ALU.mult).then_inc(S["cn_scaled"], 1)

            for c in range(NQ):
                latent(f"cq{c}", c)
                nxt(f"cq{c}")
                accumulate(dve, CQ, c)
            latent("ckv0", NQ)
            nxt("ckv0")
            latent("ckv1", NQ + 1)
            nxt("ckv1")
            invert(dve, CQ)
            used("kr")
            dve.wait_ge(S["sin_ready"], 4)
            b = bank["kr"]
            dve.tensor_tensor(av[0][64:96, :], psum[96:P, b, :], rope_m[96:P, :], ALU.mult).then_inc(S["chain"], 1)
            chain[0] += 1
            gives(dve.tensor_tensor(av[1][64:96, :], psum[64:96, b, :], rope_m[64:96, :], ALU.mult), "kr")
            dve.wait_ge(S["chain"], chain[0])
            dve.wait_ge(S["evac_done"], evac["kr"])
            link(dve.tensor_tensor(av[0][64:96, :], av[0][64:96, :], av[1][64:96, :], ALU.add))
            link(dve.tensor_tensor(kr[64:96, :], av[0][64:96, :], rsb[64:96, :], ALU.mult))
            nxt("kr")
            accumulate(dve, CKV, 0)
            for c in range(NQ):
                latent_scale(c)
                latent_low(c)

            def rotate(name, c4):
                used(name)
                if c4:
                    dve.wait_ge(S["rl_ready"], c4)
                dve.wait_ge(S["cos_scaled"], 2)
                bk = bank[name]
                for q in range(4):
                    src, dst = 32 * (q ^ 1), 32 * q
                    ins = dve.tensor_tensor(av[0][dst:dst + 32, :], psum[src:src + 32, bk, :],
                                            sin_r[src:src + 32, :], ALU.mult)
                ins.then_inc(S["chain"], 1)
                chain[0] += 1
                gives(dve.tensor_tensor(av[1][:], psum[:, bk, :], cos_r[:], ALU.mult), name)
                dve.wait_ge(S["chain"], chain[0])
                dve.wait_ge(S["evac_done"], evac[name])
                dve.tensor_tensor(av[1][:], av[1][:], av[0][:], ALU.add).then_inc(S["rot_ready"], 1)
                nxt(name)
                dve.wait_ge(S["rh_ready"], c4 + 1)
                dve.tensor_tensor(rl[:, c4, :], av[1][:], rh[:, c4, :].bitcast(F32),
                                  ALU.subtract).then_inc(S["rl_ready"], 1)

            used("rq0")
            invert(dve, CKV)
            rotate("rq0", 0)
            rotate("rq1", 1)
            for c in range(NQ, NQ + NKV):
                latent_scale(c)
                latent_low(c)
            rotate("rk0", 2)
            rotate("rk1", 3)
            for i in range(4):
                nxt(f"rv{i}")
            for b in range(TB):
                dve.wait_ge(S["rvh_ready"], b + 1)
                gives(dve.scalar_tensor_tensor(out=rvl[:, b, :], in0=psum[:, 2 + b, :], scalar=rscol[:, b:b + 1],
                                               in1=rvh[:, b, :].bitcast(F32), op0=ALU.mult,
                                               op1=ALU.subtract), f"rv{b}")
            dve.wait_ge(S["decay_landed"], 16)

            def ret_center(h):
                dve.wait_ge(S["mu_done"], h + 1)
                dve.scalar_tensor_tensor(out=yc[h % 2][:], in0=psum[:, BC, :], scalar=-1.0 / RDV,
                                         in1=yc[h % 2][:], op0=ALU.mult, op1=ALU.add).then_inc(S["yc_ready"], 1)

            def ret_gate(h):
                dve.wait_ge(S["bc_ready"], GN + h + 1)
                y = yc[h % 2]
                dve.tensor_tensor(y[:], y[:], psum[:, BC, :], ALU.mult).then_inc(S["yg_ready"], 1)
                dve.wait_ge(S["silu_rg"], h + 1)
                dve.wait_ge(S["yg_ready"], 2 * h + 1)
                dve.tensor_tensor(y[:], y[:], srg[:, h, :], ALU.mult).then_inc(S["yg_ready"], 1)
                dve.wait_ge(S["yh_ready"], h + 1)
                dve.scalar_tensor_tensor(out=yl[:, h, :], in0=y[:], scalar=g("gn", h),
                                         in1=yh[:, h, :].bitcast(F32), op0=ALU.mult,
                                         op1=ALU.subtract).then_inc(S["yl_ready"], 1)

            for h in range(RH):
                dve.wait_ge(S["sr_done"], h + 1)
                for b in range(TB):
                    n = T - P * b
                    row = slice(ROW_AT[n], ROW_AT[n] + n)
                    if h:
                        dve.wait_ge(S["stl_ready"], h)
                    ins = dve.tensor_tensor(st[:, row], tri[:, row], dec[:, h, 0:n], ALU.mult)
                ins.then_inc(S["st_ready"], 1)
                dve.wait_ge(S["sth_ready"], h + 1)
                dve.tensor_tensor(stl[:], st[:], sth[:].bitcast(F32), ALU.subtract).then_inc(S["stl_ready"], 1)
                if h:
                    ret_center(h - 1)
                used(f"rg{h}")
                if h >= 2:
                    dve.wait_ge(S["silu_rg"], h - 1)
                ins = dve.tensor_tensor(av[h % 2][:], psum[:, bank[f"rg{h}"], :], rsb[:], ALU.mult)
                gives(ins, f"rg{h}")
                nxt(f"rg{h}")
                if h:
                    invert(dve, GN + h - 1)
                    ret_gate(h - 1)
            for b in range(TB):
                if b == 1:
                    ret_center(RH - 1)
                dve.wait_ge(S["vh_ready"], b + 1)
                gives(dve.tensor_tensor(vl[:, b, :], psum[:, bank[f"v{b}"], :], vh[:, b, :].bitcast(F32),
                                        ALU.subtract), f"v{b}")
            nxt("v")
            dve.wait_ge(S["kr_split"], 1)
            dve.tensor_tensor(kl[64:96, :], kr[64:96, :], kh[64:96, :].bitcast(F32),
                              ALU.subtract).then_inc(S["kr_split"], 1)

            def head_split(h):
                used(f"head{h}")
                bq, bk = bank[f"q{h}"], bank[f"k{h}"]
                link(dve.tensor_tensor(av[0][64:96, :], psum[96:P, bq, :], rope_m[96:P, :], ALU.mult))
                link(dve.tensor_tensor(av[1][64:96, :], psum[64:96, bq, :], rope_m[64:96, :], ALU.mult))
                dve.tensor_tensor(qf[64:96, :], av[0][64:96, :], av[1][64:96, :], ALU.add).then_inc(S["qrot_ready"], 1)
                dve.wait_ge(S["kh_ready"], h + 1)
                gives(dve.tensor_tensor(kl[0:NOPE, :], psum[0:NOPE, bk, :], kh[0:NOPE, :].bitcast(F32),
                                        ALU.subtract), f"k{h}")
                dve.wait_ge(S["qh_ready"], h + 1)
                ins = dve.tensor_tensor(ql[0:DQK, :], qf[0:DQK, :], qh[0:DQK, :].bitcast(F32), ALU.subtract)
                gives(ins, f"q{h}")

            def fill_dve(name):
                n0 = UNIT_OF[name]
                used(name)
                if name[:2] == "gr":
                    m = int(name[2])
                    gives(dve.tensor_tensor(av[m % 2][:], psum[:, bank[name], :], rsb[:], ALU.mult), name)
                    nxt(name)
                    dve.wait_ge(S["tanh_ready"], m + 1)
                    link(dve.scalar_tensor_tensor(out=mret[:, m, :], in0=av[m % 2][:], scalar=1.0,
                                                  in1=mret[:, m, :], op0=ALU.add, op1=ALU.mult))
                    return
                for half, part in enumerate("ab"):
                    m = 2 * int(name[2]) + half
                    gives(dve.tensor_copy(mret[:, m, :], psum[:, bank[name + part], :]), name + part)
                nxt(name)

            head_split(0)
            nxt("head0")
            invert(dve, GN + RH - 1)
            ret_gate(RH - 1)
            scale = 1.0 / math.sqrt(DQK)
            for h in range(HEADS):
                dve.wait_ge(S["s_done"], h + 1)
                for i in range(TB):
                    n = P * (i + 1)
                    row = slice(ROW_AT[n], ROW_AT[n] + n)
                    ins = dve.tensor_reduce(mx[:, i:i + 1], tri[:, row], AX.X, ALU.max)
                link(ins)
                dve.tensor_scalar(nmx[:], mx[:], -scale, None, ALU.mult).then_inc(S["nmx_ready"], 1)
                dve.wait_ge(S["exp_ready"], 4 * h + 4)
                link(dve.reciprocal(linv[:], lsum[:]))
                for i in range(TB):
                    n = P * (i + 1)
                    row = slice(ROW_AT[n], ROW_AT[n] + n)
                    ins = dve.tensor_scalar(pr[:, row], pr[:, row], linv[:, i:i + 1], None, ALU.mult)
                ins.then_inc(S["p_ready"], 1)
                if h + 1 < HEADS:
                    head_split(h + 1)
                    nxt(f"head{h + 1}")
                fill_dve(FILL[h][0])
                dve.wait_ge(S["pth_ready"], h + 1)
                dve.tensor_tensor(ptl[:], tri[:, 0:TRI], pth[:].bitcast(F32), ALU.subtract).then_inc(S["ptl_ready"], 1)
                for f in FILL[h][1:]:
                    fill_dve(f)
                dve.wait_ge(S["oh_ready"], h + 1)
                r = slice(64 * (h % 2), 64 * (h % 2) + 64)
                dve.tensor_tensor(yl[r, h // 2, :], psum[r, 5 + 2 * (h % 2), :], yh[r, h // 2, :].bitcast(F32),
                                  ALU.subtract).then_inc(S["ol_ready"], 1)
            for i in range(4):
                nxt(f"bm{i}")
                for m in (2 * i, 2 * i + 1):
                    used(f"gm{m}")
                    if m:
                        dve.wait_ge(S["merged_in"], m)
                    gives(dve.tensor_tensor(av[m % 2][:], psum[:, m % 2, :], rsb[:], ALU.mult), f"gm{m}")
                    nxt(f"gm{m}")
                    dve.wait_ge(S["tanh_ready"], KD + m + 1)
                    dve.wait_ge(S["evac_done"], evac[f"gm{m}"])
                    gives(dve.scalar_tensor_tensor(out=av[m % 2][:], in0=av[m % 2][:], scalar=1.0,
                                                   in1=psum[:, 2 + m % 2, :], op0=ALU.add, op1=ALU.mult), f"bm{m}")
                    dve.wait_ge(S["evac_done"], evac[f"bm{m}"])
                    dve.tensor_tensor(mret[:, m, :], mret[:, m, :], av[m % 2][:], ALU.add).then_inc(S["merged_in"], 1)
                    dve.wait_ge(S["mh_ready"], m + 1)
                    dve.scalar_tensor_tensor(out=ml[:, m, :], in0=mret[:, m, :], scalar=0.5,
                                             in1=mh[:, m, :].bitcast(F32), op0=ALU.mult,
                                             op1=ALU.subtract).then_inc(S["ml_ready"], 1)
            for m in range(KD):
                nxt(f"wo{m}")
                accumulate(dve, POSTM, m)
            invert(dve, POSTM)

            ffn(1, UF2)
            for k in range(KD):
                exit_dve(dve, 2, k)

        @block.gpsimd
        def _(pool):
            def ffn(f):
                j0 = NJ * f
                pool.wait_ge(S["rsb_ready"], (1, 3)[f])

                def gates(i, first=False):
                    for c in range(2):
                        j = 2 * i + c
                        pool.wait_ge(S["silu_ready"], j + (j0 + 1))
                        if not first:
                            pool.wait_ge(S["al_ready"], j + (j0 - 1))
                        pool.tensor_tensor(av[c][:], sq[c][:], rsb[:], ALU.mult).then_inc(S["sgr_ready"], 1)

                gates(0, first=True)
                with pool.Fori(1, NJ // 2) as i:
                    gates(i)

            ffn(0)
            pool.wait_ge(S["unit_used"], UM)
            pool.dma_start(posi[:], pos).then_inc(S["pos_landed"], 16)
            pool.dma_start(trif[:], consts[:, 2 * P:3 * P]).then_inc(S["tri_landed"], 16)
            pool.wait_ge(S["tri_landed"], 16)
            pool.tensor_copy(maskb[:], trif[:]).then_inc(S["mask_ready"], 1)
            pool.tensor_copy(identb[:], ident).then_inc(S["mask_ready"], 1)
            pool.wait_ge(S["h_ready"], 8)
            pool.dma_start(h1_dram, hres[:]).then_inc(S["spilled"], 16)
            pool.wait_ge(S["spilled"], 16)
            pool.wait_ge(S["xl_ready"], 16)
            pool.wait_ge(S["sq_ready"], SQ0[PREM] + KD)
            pool.dma_start(dec[:], decay).then_inc(S["decay_landed"], 16)
            pool.wait_ge(S["unit_used"], UNIT_OF["bm3"] + 1)
            pool.dma_start(hres[:], h1_dram).then_inc(S["h1_back"], 16)
            ffn(1)


def kernel(**inputs):
    import numpy as np
    import concourse.bacc as bacc
    from concourse.bass_utils import run_bass_kernel_spmd as run

    w = {k: np.asarray(v) for k, v in inputs.items()}

    def tiles(m, col_lists):
        t = m.reshape(-1, P, m.shape[1])
        return [np.ascontiguousarray(t[:, :, c].transpose(1, 0, 2).reshape(P, -1)) for c in col_lists]

    def ffn_units(w1, w2):
        order = []
        for j in range(NJ):
            order += [np.arange(P * j, P * j + P), FF + np.arange(P * j, P * j + P)]
        a = np.stack(tiles(w1, order))
        b = np.concatenate([np.stack(tiles(w2[FF // 2 * i:FF // 2 * (i + 1)],
                                           [np.arange(P * m, P * m + P) for m in range(KD)]))[:, None]
                            for i in range(2)], axis=1).reshape(W2_UNITS, P, UNIT2)
        return a, b

    w_in, uq, ukv = w["w_in"][0], w["mla_w_uq"][0], w["mla_w_ukv"][0]
    at = np.cumsum([0, QR, KVR, ROPE, RH * RDK, RH * RDK, RH * RDV, RH * RDV, D, D])
    half = ROPE // 2

    def mix_unit(name):
        kind, i = name.rstrip("0123456789"), int(name[len(name.rstrip("0123456789")):] or 0)
        run_of = {"cq": at[0], "ckv": at[1], "rq": at[3], "rk": at[4], "rg": at[6], "gm": at[7], "gr": at[8]}
        if kind in run_of:
            return tiles(w_in, [run_of[kind] + P * i + np.arange(P)])[0]
        if kind == "kr":
            r = at[2] + np.arange(ROPE)
            return tiles(w_in, [np.concatenate([at[2] - 64 + np.arange(64), r, r[half:], r[:half]])])[0]
        if kind == "rv":
            return tiles(w_in[2 * P * i:2 * P * (i + 1)], [at[5] + np.arange(T)])[0]
        if kind == "v":
            c = np.concatenate([(NOPE + DV) * h + NOPE + np.arange(DV) for h in range(HEADS)])
            return tiles(ukv, [c])[0]
        if kind == "head":
            c = DQK * i + np.arange(DQK)
            q = tiles(uq, [np.concatenate([c, c[NOPE + half:], c[NOPE:NOPE + half]])])[0]
            k = tiles(ukv, [(NOPE + DV) * i + np.arange(P)])[0]
            return np.concatenate([q, k, np.zeros((P, UNIT - HEAD_UNIT), q.dtype)], axis=1)
        if kind in ("br", "bm"):
            m = w["w_branch_ret" if kind == "br" else "w_branch_mla"][0]
            return np.concatenate(tiles(m, [P * c + np.arange(P) for c in (2 * i, 2 * i + 1)]), axis=1)
        return tiles(w["w_out"][0], [P * i + np.arange(P)])[0]

    f1a, f1b = ffn_units(w["ffn1_w1"][0], w["ffn1_w2"][0])
    f2a, f2b = ffn_units(w["ffn2_w1"][0], w["ffn2_w2"][0])

    cols = np.zeros((P, NCOLS), np.float32)
    for name, key in (("pre1", "ffn1_pre_w"), ("post1", "ffn1_post_w"), ("prem", "mix_pre_w"),
                      ("qn", "mla_q_norm_w"), ("kvn", "mla_kv_norm_w"), ("gn", "ret_gn_w"),
                      ("postm", "mix_post_w"), ("pre2", "ffn2_pre_w"), ("post2", "ffn2_post_w")):
        v = w[key][0].reshape(-1, P).T
        cols[:, COLS[name]:COLS[name] + v.shape[1]] = v
    p = np.arange(P)
    for name, v in (("eps", EPS), ("eps4", 4 * EPS), ("half_pi", math.pi / 2),
                    ("freq_m", ROPE_BASE ** (-(p % half) / half)),
                    ("sign_m", np.where(p % ROPE < half, -1.0, 1.0)),
                    ("freq_r", ROPE_BASE ** (-(p % 32) / 32.0)),
                    ("sign_r", np.where(p % 64 < 32, 1.0, -1.0))):
        cols[:, COLS[name]] = v
    consts = np.concatenate([np.ones((P, P)), np.eye(P), np.where(p[:, None] >= p[None, :], 0.0, MASKED)],
                            axis=1).astype(np.float32)
    lag = np.arange(T)[None, :] - p[:, None]
    decay = np.stack([np.where(lag >= 0, np.exp(np.maximum(lag, 0) * np.log(1 - 2.0 ** (-5.0 - h))), 0.0)
                      for h in range(RH)], axis=1) * RDK ** -0.5

    arrays = {
        "x_t": np.ascontiguousarray(w["x"][0].T.reshape(KD, P, T).transpose(1, 0, 2)),
        "pos_b": np.ascontiguousarray(np.broadcast_to(w["positions"][0][None, :], (P, T))),
        "w_ffn1_a": f1a, "w_ffn1_b": f1b, "w_mix": np.stack([mix_unit(n) for n in MIX]),
        "w_ffn2_a": f2a, "w_ffn2_b": f2b,
        "cols": cols, "consts": consts, "decay": decay.astype(np.float32),
    }
    nc = bacc.Bacc("TRN2", target_bir_lowering=False, num_devices=1)
    args = [nc.dram_tensor(n, a.shape, mybir.dt.from_np(a.dtype), kind="ExternalInput").ap()
            for n, a in arrays.items()]
    args.append(nc.dram_tensor("out_t", (P, KD, T), F32, kind="ExternalOutput").ap())
    build(nc, *args)
    r = run(nc, [arrays], core_ids=[0])
    got = r.results[0]["out_t"]
    return np.ascontiguousarray(got.transpose(2, 1, 0).reshape(1, T, D))
```

```python
import math

import concourse.bass as bass
from concourse import mybir

F32 = mybir.dt.float32
F32R = mybir.dt.float32r
BF16 = mybir.dt.bfloat16
I32 = mybir.dt.int32
ACT = mybir.ActivationFunctionType
ALU = mybir.AluOpType
AX = mybir.AxisListType

P = 128
D = 1024
KD = D // P
T = 512
TB = T // P
FF = 2816
NJ = FF // P
PART = [8, 7, 7]
PART0 = [0, 8, 15]
QR, KVR = 384, 256
NQ, NKV = QR // P, KVR // P
HEADS, NOPE, ROPE, DV = 8, 64, 32, 64
DQK = NOPE + ROPE
RH, RDK, RDV = 4, 64, 128
EPS = 1e-6
ROPE_BASE = 10000.0
MASKED = -1e30

UNIT = KD * P
HEAD_UNIT = (NQ + NKV) * P
W1_UNITS, W2_UNITS = 2 * NJ, len(PART) * KD
RING = 4

MIX = (["cq0", "cq1", "cq2", "ckv0", "ckv1", "kr", "rq0", "rq1", "rk0", "rk1"]
       + [f"rv{i}" for i in range(4)] + [f"rg{i}" for i in range(4)] + ["v", "head0"])
EARLY = [2, 0, 0, 0, 0, 0, 0, 1]
FILL = [["br0", "br1", "br2", "br3"], ["gr0"], ["gr1"], ["gr2"], ["gr3"], ["gr4"], ["gr5"], ["gr6", "gr7"]]
for _h in range(HEADS):
    if _h + 1 < HEADS:
        MIX.append(f"head{_h + 1}")
    MIX += FILL[_h]
for _i in range(4):
    MIX += [f"bm{_i}", f"gm{2 * _i}", f"gm{2 * _i + 1}"]
MIX += [f"wo{m}" for m in range(KD)]
UF1 = 0
UM = UF1 + W1_UNITS + W2_UNITS
UF2 = UM + len(MIX)
U_END = UF2 + W1_UNITS + W2_UNITS
UNIT_OF = {name: UM + i for i, name in enumerate(MIX)}

PRE1, POST1, PREM, CQ, CKV, GN, POSTM, PRE2, POST2 = 0, 1, 2, 3, 4, 5, 9, 10, 11
CHUNKS = [KD, KD, KD, NQ, NKV, 1, 1, 1, 1, KD, KD, KD]
SQ0 = [sum(CHUNKS[:n]) for n in range(len(CHUNKS) + 1)]
AC0 = [SQ0[n] - n for n in range(len(CHUNKS) + 1)]

COLS, _at = {}, 0
for _name, _n in (("pre1", KD), ("post1", KD), ("prem", KD), ("qn", NQ), ("kvn", NKV), ("gn", RH), ("postm", KD),
                  ("pre2", KD), ("post2", KD), ("eps", 1), ("eps4", 1), ("freq_m", 1), ("sign_m", 1),
                  ("freq_r", 1), ("sign_r", 1), ("half_pi", 1)):
    COLS[_name] = _at
    _at += _n
NCOLS = _at

ROW_AT = {512: 0, 384: 512, 128: 896, 256: 1024}
TRI = 1280



def pi_parts(n):
    rest, out = 2 * math.pi, []
    for i in range(n):
        step = 2.0 ** (-9 - 12 * i)
        part = math.floor(rest / step) * step if i < n - 1 else rest
        out.append(part)
        rest -= part
    return out


BANK = {"cq0": 0, "cq1": 1, "cq2": 2, "ckv0": 3, "ckv1": 0, "kr": 1, "rq0": 0, "rq1": 1, "rk0": 0, "rk1": 1,
        "rv0": 2, "rv1": 3, "rv2": 4, "rv3": 5, "rg0": 0, "rg1": 1, "rg2": 0, "rg3": 1,
        "v0": 2, "v1": 3, "v2": 4, "v3": 0, "q0": 1, "k0": 0}


def build(nc, x, pos, wf1, wmix, wf2, cols, consts, decay, out):
    h1_dram = nc.dram_tensor("h1_spill", (P, KD, T), F32, kind="Internal").ap()
    base = -(-nc.sbuf_base // 128) * 128
    top = [base]

    def at(name, shape, dt, offset):
        return nc.alloc_sbuf_tensor_at(name, shape, dt, offset=offset)

    def place(name, shape, dt):
        size = (math.prod(shape[1:]) * 4 + 31) // 32 * 32
        top[0] += size
        return at(name, shape, dt, top[0] - size)

    raw = [place(f"raw{s}", [P, UNIT], F32) for s in range(RING)]
    whi = [place(f"whi{s}", [P, UNIT], F32R) for s in range(RING)]
    wlo = [place(f"wlo{s}", [P, UNIT], F32R) for s in range(RING)]
    xh_at = top[0]
    xh = place("xh", [P, KD, T], F32R)
    xl = place("xl", [P, KD, T], F32R)
    fo = at("fo", [P, KD, T], F32, xh_at)
    sq = [place(f"sq{s}", [P, T], F32) for s in range(2)]
    av = [place(f"av{s}", [P, T], F32) for s in range(2)]
    acc = place("acc", [P, T], F32)
    rsb = place("rsb", [P, T], F32)
    dg = place("dg", [P, TB, P], F32)
    cst = place("cst", [P, 2 * P], F32)
    ones, ident = cst[:, 0:P], cst[:, P:2 * P]
    gain = place("gain", [P, NCOLS], F32)
    rms = place("rms", [P, TB], F32)
    rcol = place("rcol", [P, TB], F32)
    rscol = place("rscol", [P, TB], F32)
    mx = place("mx", [P, TB], F32)
    nmx = place("nmx", [P, TB], F32)
    lsum = place("lsum", [P, TB], F32)
    linv = place("linv", [P, TB], F32)
    u = -(-top[0] // 64) * 64

    ah = at("ah", [P, NJ, T], F32R, u)
    al = at("al", [P, NJ, T], F32R, u + 45056)
    hres = at("hres", [P, KD, T], F32, u + 90112)
    assert u + 90112 + 16384 <= nc.sbuf_usable_end, (u, nc.sbuf_usable_end)
    maskb = at("maskb", [P, P], BF16, u)
    identb = at("identb", [P, P], BF16, u + 256)
    rope_m = at("rope_m", [P, T], F32, u + 512)
    cnh = at("cnh", [P, NQ + NKV, T], F32R, u + 2560)
    cnl = at("cnl", [P, NQ + NKV, T], F32R, u + 12800)
    kr = at("kr", [P, T], F32, u + 23040)
    cos_r = at("cos_r", [P, T], F32, u + 25088)
    sin_r = at("sin_r", [P, T], F32, u + 27136)
    rh = at("rh", [P, 4, T], F32R, u + 29184)
    rl = at("rl", [P, 4, T], F32R, u + 37376)
    rvh = at("rvh", [P, TB, T], F32R, u + 45568)
    rvl = at("rvl", [P, TB, T], F32R, u + 53760)
    st = at("st", [P, TRI], F32, u + 61952)
    sth = at("sth", [P, TRI], F32R, u + 67072)
    stl = at("stl", [P, TRI], F32R, u + 72192)
    angle = at("angle", [P, 2, T], F32, u + 61952)
    turns = at("turns", [P, 2, T], F32, u + 66048)
    turns_hi = at("turns_hi", [P, 2, T], F32, u + 70144)
    posi = at("posi", [P, T], I32, u + 74240)
    cf = at("cf", [P, NQ + NKV, T], F32, u + 77312)
    trif = at("trif", [P, P], F32, u + 87552)
    srg = at("srg", [P, RH, T], F32, u + 77312)
    yc = [at(f"yc{s}", [P, T], F32, u + 85504 + 2048 * s) for s in range(2)]
    dec = at("dec", [P, RH, T], F32, u + 89600)
    yh = at("yh", [P, 4, T], F32R, u + 89600)
    yl = at("yl", [P, 4, T], F32R, u + 97792)
    vh = at("vh", [P, TB, T], F32R, u + 25088)
    vl = at("vl", [P, TB, T], F32R, u + 33280)
    qh = at("qh", [P, T], F32R, u + 41472)
    ql = at("ql", [P, T], F32R, u + 43520)
    kh = at("kh", [P, T], F32R, u + 45568)
    kl = at("kl", [P, T], F32R, u + 47616)
    qf = at("qf", [P, T], F32, u + 49664)
    pr = at("pr", [P, TRI], F32, u + 51712)
    pth = at("pth", [P, TRI], F32R, u + 56832)
    ptl = at("ptl", [P, TRI], F32R, u + 61952)
    mret = at("mret", [P, KD, T], F32, u + 69120)
    mh = at("mh", [P, KD, T], F32R, u + 2560)
    ml = at("ml", [P, KD, T], F32R, u + 18944)

    psum = nc.alloc_psum_tensor("psum", [P, 8, T], F32)
    tri = psum[:, 2:5, :].rearrange("p b t -> p (b t)")
    COL, BC = 6, 7

    def g(name, i=0, rows=slice(0, P)):
        return gain[rows, COLS[name] + i:COLS[name] + i + 1]

    sems = ("raw0 raw1 raw2 raw3 cols_landed cst_landed hi_ready lo_ready unit_used x0 x1 x2 x3 x4 x5 x6 x7 xh_ready xl_ready sq_ready "
             "acc_ready col_ready rms_ready rc_ready dg_ready bc_ready rsb_ready rscol_ready gs_ready silu_ready sgr_ready a_ready "
             "ah_ready al_ready f_copied fs_ready h_ready h_odd_ready spilled pos_landed tri_landed decay_landed mask_ready "
             "chain rope_args sin_ready cos_scaled evac_done cn_scaled cnh_ready cnl_ready rot_ready rh_ready rl_ready rvh_ready "
             "silu_rg sr_done st_ready sth_ready stl_ready y_done yf_ready mu_done yc_ready yg_ready yh_ready "
             "yl_ready vh_ready kr_split qrot_ready qf_ready qh_ready kh_ready s_done nmx_ready exp_ready "
             "p_ready pt_done pth_ready ptl_ready pv_done oh_ready ol_ready tanh_ready merged_in mh_ready ml_ready "
             "h1_back out_landed").split()
    S = {n: nc.alloc_semaphore(n) for n in sems}

    def s3(e, lhs_hi, lhs_lo, rhs_hi, rhs_lo, dst, start, stop):
        e.matmul(dst, lhs_hi, rhs_hi, start=start, stop=False, skip_group_check=True)
        e.matmul(dst, lhs_hi, rhs_lo, start=False, stop=False, skip_group_check=True)
        return e.matmul(dst, lhs_lo, rhs_hi, start=False, stop=stop, skip_group_check=True)

    EV = ["cq0", "cq1", "cq2", "ckv0", "ckv1", "kr", "rq0", "rq1", "rk0", "rk1", "rv0", "rv1", "rv2", "rv3",
          "rg0", "rg1", "rg2", "rg3", "v0", "v1", "v2", "v3", "k0", "q0"]
    MADE = list(EV)
    bank = dict(BANK)
    for h in range(HEADS):
        names = [p for f in FILL[h] for p in ((f + "a", f + "b") if f[:2] == "br" else (f,))]
        if h + 1 < HEADS:
            names = [f"k{h + 1}", f"q{h + 1}"] + names
            bank[f"q{h + 1}"], bank[f"k{h + 1}"] = 0, 1
        EV += names
        MADE += names
        for i, p in enumerate(names):
            if p[:2] == "br":
                bank[p] = i % 2
            elif p[:2] == "gr":
                bank[p] = 0 if p == FILL[-1][-1] else COL
    for i in range(4):
        for m in (2 * i, 2 * i + 1):
            EV += [f"gm{m}", f"bm{m}"]
            MADE += [f"bm{m}", f"gm{m}"]
            bank[f"gm{m}"], bank[f"bm{m}"] = m % 2, 2 + m % 2
    evac = {n: i + 1 for i, n in enumerate(EV)}

    def free(e, name):
        before = [n for n in MADE[:MADE.index(name)] if bank[n] == bank[name]]
        if name == FILL[1][0]:
            e.wait_ge(S["rms_ready"], POSTM)
        if before:
            e.wait_ge(S["evac_done"], evac[before[-1]])

    def unit_size(n):
        return HEAD_UNIT if UM <= n < UF2 and MIX[n - UM].startswith("head") else UNIT


    def load(e, src, n0, adv=0):
        if n0 >= RING:
            e.wait_ge(S["lo_ready"], adv + n0 - RING + 1)
        e.dma_start(raw[n0 % RING][:, 0:src.shape[-1]], src).then_inc(S[f"raw{n0 % RING}"], 16)

    def split_hi(e, n0, adv=0, turns_of_ring=0):
        if isinstance(adv, int) and n0 >= U_END:
            return
        size = unit_size(n0) if isinstance(adv, int) else UNIT
        e.wait_ge(S[f"raw{n0 % RING}"], turns_of_ring * 16 + 16 * (n0 // RING + 1))
        if n0 >= RING:
            e.wait_ge(S["unit_used"], adv + n0 - RING + 1)
        e.activation(whi[n0 % RING][:, 0:size], raw[n0 % RING][:, 0:size], ACT.Copy).then_inc(S["hi_ready"], 1)

    def split_lo(e, n0, adv=0):
        if isinstance(adv, int) and n0 >= U_END:
            return
        size = unit_size(n0) if isinstance(adv, int) else UNIT
        e.wait_ge(S["hi_ready"], adv + n0 + 1)
        e.tensor_tensor(wlo[n0 % RING][:, 0:size], raw[n0 % RING][:, 0:size],
                        whi[n0 % RING][:, 0:size].bitcast(F32), ALU.subtract).then_inc(S["lo_ready"], 1)

    def tile(n0, k):
        return whi[n0 % RING][:, P * k:P * k + P], wlo[n0 % RING][:, P * k:P * k + P]

    def square(e, n, i, src):
        idx = SQ0[n] + i
        if i >= 2:
            e.wait_ge(S["acc_ready"], AC0[n] + i - 1)
        elif n:
            e.wait_ge(S["col_ready"], n)
        e.activation(sq[idx % 2][:], src, ACT.Square).then_inc(S["sq_ready"], 1)

    def accumulate(e, n, i):
        if i >= CHUNKS[n] - 1:
            return
        e.wait_ge(S["sq_ready"], SQ0[n] + i + 1)
        src = sq[(SQ0[n] + i) % 2][:]
        if i == 0:
            if n:
                e.wait_ge(S["col_ready"], n)
            e.tensor_copy(acc[:], src).then_inc(S["acc_ready"], 1)
        else:
            e.wait_ge(S["acc_ready"], AC0[n] + i)
            e.tensor_tensor(acc[:], acc[:], src, ALU.add).then_inc(S["acc_ready"], 1)

    def sum_columns(e, n):
        if AC0[n + 1]:
            e.wait_ge(S["acc_ready"], AC0[n + 1])
        e.wait_ge(S["sq_ready"], SQ0[n + 1])
        if n:
            e.wait_ge(S["rms_ready"], n)
        if n == POSTM:
            e.wait_ge(S["evac_done"], len(EV))
        last_sq = sq[(SQ0[n + 1] - 1) % 2]
        for b in range(TB):
            if CHUNKS[n] > 1:
                e.matmul(psum[:, COL, b:b + 1], acc[:, P * b:P * b + P], ones[:, 0:1], start=True, stop=False)
            mm = e.matmul(psum[:, COL, b:b + 1], last_sq[:, P * b:P * b + P], ones[:, 0:1],
                          start=CHUNKS[n] == 1, stop=True)
        mm.then_inc(S["col_ready"], 1)

    def root(e, n, width, halve=False):
        e.wait_ge(S["col_ready"], n + 1)
        if n:
            e.wait_ge(S["rc_ready"], n)
        f = 4.0 if halve else 1.0
        e.activation(rms[:], psum[:, COL, 0:TB], ACT.Sqrt, bias=g("eps4" if halve else "eps"),
                     scale=f / width).then_inc(S["rms_ready"], 1)

    def invert(e, n):
        e.wait_ge(S["rms_ready"], n + 1)
        if n:
            e.wait_ge(S["dg_ready"], n)
        e.reciprocal(rcol[:], rms[:]).then_inc(S["rc_ready"], 1)
        e.wait_ge(S["rc_ready"], n + 1)
        if n:
            e.wait_ge(S["bc_ready"], n)
        e.tensor_tensor(dg[:], ident[:, None, :].broadcast_to([P, TB, P]),
                        rcol[:, :, None].broadcast_to([P, TB, P]), ALU.mult).then_inc(S["dg_ready"], 1)

    def broadcast(e, n):
        e.wait_ge(S["dg_ready"], n + 1)
        if n in (POST1 + 1, POSTM + 1):
            e.wait_ge(S["h_ready"], 8 if n == PREM else 16)
        elif n in (POST1, CQ, POST2):
            e.wait_ge(S["rsb_ready"], {POST1: 1, CQ: 2, POST2: 3}[n])
        elif n == CKV:
            e.wait_ge(S["cn_scaled"], NQ)
        elif n == GN:
            e.wait_ge(S["yc_ready"], 1)
        e.matmul(psum[:, BC, :], ones, dg[:].rearrange("p b t -> p (b t)"), start=True,
                 stop=True).then_inc(S["bc_ready"], 1)

    def keep_rs(e, n, k):
        e.wait_ge(S["bc_ready"], n + 1)
        if k == 1:
            e.wait_ge(S["al_ready"], NJ)
        if k == 2:
            e.wait_ge(S["evac_done"], len(EV))
        e.activation(rsb[:], psum[:, BC, :], ACT.Copy).then_inc(S["rsb_ready"], 1)

    PRE = ("pre1", "prem", "pre2")
    PRE_N = (PRE1, PREM, PRE2)
    POST_N = (POST1, POSTM, POST2)

    def have_h(e, s, k):
        if s == 0:
            e.wait_ge(S[f"x{k}"], 16)
        else:
            e.wait_ge(S["h_ready"], 8 * (s - 1) + k + 1)

    def enter_act(e, s, k):
        have_h(e, s, k)
        e.activation(xh[:, k, :], hres[:, k, :], ACT.Copy, scale=g(PRE[s], k)).then_inc(S["xh_ready"], 1)
        square(e, PRE_N[s], k, hres[:, k, :])

    def enter_dve(e, s, k):
        e.wait_ge(S["xh_ready"], 8 * s + k + 1)
        e.scalar_tensor_tensor(out=xl[:, k, :], in0=hres[:, k, :], scalar=g(PRE[s], k),
                               in1=xh[:, k, :].bitcast(F32), op0=ALU.mult, op1=ALU.subtract).then_inc(S["xl_ready"], 1)

    def phase_out(e, n, m, post):
        src = psum[:, 4 + m % 2, :]
        if m == KD - 1:
            square(e, n, m, src)
        e.activation(fo[:, m, :], src, ACT.Copy, scale=g(post, m)).then_inc(S["f_copied"], 1)
        if m < KD - 1:
            square(e, n, m, src)

    def exit_dve(e, s, k):
        if k == 0:
            e.wait_ge(S["bc_ready"], POST_N[s] + 1)
            if s == 1:
                e.wait_ge(S["h1_back"], 16)
        e.tensor_tensor(fo[:, k, :], fo[:, k, :], psum[:, BC, :], ALU.mult).then_inc(S["fs_ready"], 1)
        if s == 2 and k % 2:
            return
        e.wait_ge(S["fs_ready"], 8 * s + k + 1)
        e.tensor_tensor(hres[:, k, :], hres[:, k, :], fo[:, k, :], ALU.add).then_inc(S["h_ready"], 1)

    block = nc.Block()
    with block as block:
        @block.sync
        def _(sp):
            def ffn(w, n0, first=0):
                for c in range(first, 4):
                    load(sp, w[c], n0 + c)
                with sp.Fori(0, (W1_UNITS + W2_UNITS) // 4 - 1) as i:
                    for c in range(4):
                        load(sp, w[4 * i + (4 + c)], n0 + 4 + c, 4 * i)

            sp.dma_start(gain[:], cols).then_inc(S["cols_landed"], 16)
            load(sp, wf1[0], 0)
            for k in range(KD):
                sp.dma_start(hres[:, k, :], x[:, k, :]).then_inc(S[f"x{k}"], 16)
            sp.dma_start(cst[:], consts[:, 0:2 * P]).then_inc(S["cst_landed"], 16)
            ffn(wf1, UF1, 1)
            for n in range(UM, UF2):
                load(sp, wmix[n - UM][:, 0:unit_size(n)], n)
                if n == UM + 7:
                    sp.wait_ge(S["unit_used"], UM)
                    sp.dma_start(posi[:], pos).then_inc(S["pos_landed"], 16)
                    sp.dma_start(trif[:], consts[:, 2 * P:3 * P]).then_inc(S["tri_landed"], 16)
                if n == UM + 8:
                    sp.wait_ge(S["h_ready"], 8)
                    sp.dma_start(h1_dram, hres[:]).then_inc(S["spilled"], 16)
                if n == UM + 13:
                    sp.wait_ge(S["spilled"], 16)
                    sp.wait_ge(S["xl_ready"], 16)
                    sp.wait_ge(S["sq_ready"], SQ0[PREM] + KD)
                    sp.dma_start(dec[:], decay).then_inc(S["decay_landed"], 16)
                if n == UNIT_OF["bm3"] + 8:
                    sp.wait_ge(S["unit_used"], UNIT_OF["bm3"] + 1)
                    sp.dma_start(hres[:], h1_dram).then_inc(S["h1_back"], 16)
            ffn(wf2, UF2)
            for k in range(KD):
                if k % 2:
                    sp.wait_ge(S["h_odd_ready"], k // 2 + 1)
                else:
                    sp.wait_ge(S["h_ready"], 16 + k // 2 + 1)
                sp.dma_start(out[:, k, :], hres[:, k, :]).then_inc(S["out_landed"], 16)
            sp.wait_ge(S["out_landed"], 16 * KD)

        @block.tensor
        def _(pe):
            def first_units(s, n0, banks):
                for c in range(4):
                    pe.wait_ge(S["lo_ready"], n0 + c + 1)
                for k in range(KD):
                    pe.wait_ge(S["xl_ready"], 8 * s + k + 1)
                    if k == KD - 1:
                        sum_columns(pe, PRE_N[s])
                    for c in range(4):
                        hi, lo = tile(n0 + c, k)
                        mm = s3(pe, hi, lo, xh[:, k, :], xl[:, k, :], psum[:, banks[c], :], k == 0, k == KD - 1)
                        if k == KD - 1:
                            mm.then_inc(S["unit_used"], 1)
                        if k == KD - 1 and c == 1:
                            broadcast(pe, PRE_N[s])

            def unit8(n0, adv, dst, hi_in, lo_in, arriving=False):
                pe.wait_ge(S["lo_ready"], adv + n0 + 1)
                for k in range(KD):
                    if arriving:
                        pe.wait_ge(S["xl_ready"], k + 1)
                    hi, lo = tile(n0, k)
                    mm = s3(pe, hi, lo, hi_in[:, k, :], lo_in[:, k, :], dst, k == 0, k == KD - 1)
                mm.then_inc(S["unit_used"], 1)

            def ffn(f, n0):
                s, j0 = (0, 2)[f], NJ * f
                if f:
                    pe.wait_ge(S["f_copied"], 2 * KD)
                if f:
                    first_units(s, n0, (0, 2, 1, 3))
                else:
                    unit8(n0, 0, psum[:, 0, :], xh, xl, arriving=True)
                    unit8(n0 + 1, 0, psum[:, 2, :], xh, xl)
                    pe.wait_ge(S["cst_landed"], 16)
                    sum_columns(pe, PRE1)
                    unit8(n0 + 2, 0, psum[:, 1, :], xh, xl)
                    broadcast(pe, PRE1)
                    unit8(n0 + 3, 0, psum[:, 3, :], xh, xl)
                with pe.Fori(1, NJ // 2) as i:
                    for c in range(2):
                        pe.wait_ge(S["a_ready"], 2 * i + (j0 + c - 1))
                        for half in range(2):
                            unit8(n0 + 2 * c + half, 4 * i, psum[:, c + 2 * half, :], xh, xl)
                nb = n0 + W1_UNITS
                sq0 = SQ0[POST_N[s]]
                with pe.Fori(0, KD // 4) as i:
                    for c in range(4):
                        pe.wait_ge(S["sq_ready"], 4 * i + (sq0 + c - 1))
                        for part, tiles_in in enumerate(PART):
                            pe.wait_ge(S["lo_ready"], 12 * i + (nb + 3 * c + part + 1))
                            pe.wait_ge(S["al_ready"], j0 + PART0[part] + tiles_in)
                            for k in range(tiles_in):
                                j = PART0[part] + k
                                hi, lo = tile(nb + 3 * c + part, k)
                                mm = s3(pe, hi, lo, ah[:, j, :], al[:, j, :], psum[:, 4 + c % 2, :],
                                        j == 0, j == NJ - 1)
                            mm.then_inc(S["unit_used"], 1)
                sum_columns(pe, POST_N[s])
                broadcast(pe, POST_N[s])

            def product(name, srcs, n0, tiles, done=True):
                free(pe, name)
                for i, (k, (hi_in, lo_in)) in enumerate(zip(tiles, srcs)):
                    hi, lo = tile(n0, k)
                    mm = s3(pe, hi, lo, hi_in, lo_in, psum[:, bank[name], :], i == 0, i == len(tiles) - 1)
                if done:
                    mm.then_inc(S["unit_used"], 1)

            def project(name, ks=range(KD)):
                n0 = UNIT_OF[name]
                if ks[0] == 0:
                    pe.wait_ge(S["lo_ready"], n0 + 1)
                    free(pe, name)
                for k in ks:
                    hi, lo = tile(n0, k)
                    mm = s3(pe, hi, lo, xh[:, k, :], xl[:, k, :], psum[:, bank[name], :], k == 0, k == KD - 1)
                if ks[-1] == KD - 1:
                    mm.then_inc(S["unit_used"], 1)

            def head_unit(h):
                n0 = UNIT_OF[f"head{h}"]
                pe.wait_ge(S["lo_ready"], n0 + 1)
                if h == 0:
                    pe.wait_ge(S["cnl_ready"], NQ + NKV)
                product(f"k{h}", [(cnh[:, NQ + k, :], cnl[:, NQ + k, :]) for k in range(NKV)], n0,
                        range(NQ, NQ + NKV), done=False)
                product(f"q{h}", [(cnh[:, k, :], cnl[:, k, :]) for k in range(NQ)], n0, range(NQ))

            def ret_scores(h):
                c, r = h // 2, slice(64 * (h % 2), 64 * (h % 2) + 64)
                if h == 0:
                    pe.wait_ge(S["rl_ready"], 4)
                    pe.wait_ge(S["evac_done"], evac["rv2"])
                else:
                    pe.wait_ge(S["st_ready"], h)
                for b in range(TB):
                    n = T - P * b
                    blk = slice(P * b, P * b + P)
                    mm = s3(pe, rh[r, 2 + c, blk], rl[r, 2 + c, blk], rh[r, c, P * b:], rl[r, c, P * b:],
                            tri[:, ROW_AT[n]:ROW_AT[n] + n], True, True)
                mm.then_inc(S["sr_done"], 1)

            def ret_out(h):
                pe.wait_ge(S["stl_ready"], h + 1)
                if h == 0:
                    pe.wait_ge(S["evac_done"], evac["rv3"])
                else:
                    pe.wait_ge(S["yf_ready"], h)
                for b in range(TB):
                    n = T - P * b
                    row = slice(ROW_AT[n], ROW_AT[n] + n)
                    cols_h = slice(RDV * h, RDV * h + RDV)
                    mm = s3(pe, rvh[:, b, cols_h], rvl[:, b, cols_h], sth[:, row], stl[:, row],
                            psum[:, 5, P * b:], b == 0, b == TB - 1)
                mm.then_inc(S["y_done"], 1)

            def ret_mean(h):
                pe.wait_ge(S["yf_ready"], h + 1)
                if h == 0:
                    pe.wait_ge(S["cn_scaled"], NQ + NKV)
                else:
                    pe.wait_ge(S["yg_ready"], 2 * h - 1)
                pe.matmul(psum[:, BC, :], ones, yc[h % 2][:], start=True, stop=True).then_inc(S["mu_done"], 1)

            def ret_norm(h):
                pe.wait_ge(S["yc_ready"], h + 1)
                broadcast(pe, GN + h)

            def scores(h):
                pe.wait_ge(S["evac_done"], evac[f"q{h}"])
                if h == 0:
                    pe.wait_ge(S["kr_split"], 2)
                    pe.wait_ge(S["mask_ready"], 2)
                    pe.wait_ge(S["evac_done"], evac["v2"])
                else:
                    pe.wait_ge(S["ptl_ready"], h)
                for i in range(TB):
                    n = P * (i + 1)
                    a = ROW_AT[n]
                    q = slice(P * i, P * i + P)
                    s3(pe, qh[0:DQK, q], ql[0:DQK, q], kh[0:DQK, 0:n], kl[0:DQK, 0:n], tri[:, a:a + n], True, False)
                    mm = pe.matmul(tri[:, a + n - P:a + n], identb[:], maskb[:], start=False, stop=True,
                                   skip_group_check=True)
                mm.then_inc(S["s_done"], 1)

            def turn_probs(h):
                pe.wait_ge(S["p_ready"], h + 1)
                for b in range(TB):
                    for i in range(b, TB):
                        src = ROW_AT[P * (i + 1)] + P * b
                        dst = ROW_AT[T - P * b] + P * (i - b)
                        mm = pe.transpose(tri[:, dst:dst + P], pr[:, src:src + P], ident)
                mm.then_inc(S["pt_done"], 1)

            def attend(h):
                pe.wait_ge(S["ptl_ready"], h + 1)
                if h == 0:
                    pe.wait_ge(S["yf_ready"], RH)
                elif h == 1:
                    pe.wait_ge(S["yg_ready"], 2 * RH)
                else:
                    pe.wait_ge(S["ol_ready"], h - 1)
                for b in range(TB):
                    n = T - P * b
                    row = slice(ROW_AT[n], ROW_AT[n] + n)
                    pair = slice(P * (h // 2), P * (h // 2) + P)
                    mm = s3(pe, vh[:, b, pair], vl[:, b, pair], pth[:, row], ptl[:, row],
                            psum[:, 5 + 2 * (h % 2), P * b:], b == 0, b == TB - 1)
                mm.then_inc(S["pv_done"], 1)

            def fill(name):
                n0 = UNIT_OF[name]
                pe.wait_ge(S["lo_ready"], n0 + 1)
                pe.wait_ge(S["yl_ready"], RH)
                for half, part in enumerate("ab"):
                    product(name + part, [(yh[:, k, :], yl[:, k, :]) for k in range(4)], n0,
                            range(4 * half, 4 * half + 4), done=half == 1)

            ffn(0, UF1)

            first_units(1, UM, (0, 1, 2, 3))
            project("ckv1")
            sum_columns(pe, CQ)
            project("kr")
            broadcast(pe, CQ)
            project("rq0")
            sum_columns(pe, CKV)
            project("rq1")
            broadcast(pe, CKV)
            project("rk0")
            project("rk1")
            for i in range(4):
                n0 = UNIT_OF[f"rv{i}"]
                pe.wait_ge(S["lo_ready"], n0 + 1)
                for b in range(TB):
                    if i == 0:
                        free(pe, f"rv{b}")
                        if b >= 2:
                            pe.wait_ge(S["f_copied"], KD)
                    for kk in range(2):
                        k = 2 * i + kk
                        blk = slice(P * b, P * b + P)
                        w = slice(T * kk, T * kk + T)
                        mm = s3(pe, xh[:, k, blk], xl[:, k, blk], whi[n0 % RING][:, w], wlo[n0 % RING][:, w],
                                psum[:, 2 + b, :], k == 0, k == KD - 1)
                mm.then_inc(S["unit_used"], 1)
            for h in range(RH):
                ret_scores(h)
                if h:
                    ret_mean(h - 1)
                project(f"rg{h}")
                if h:
                    sum_columns(pe, GN + h - 1)
                ret_out(h)
                if h:
                    ret_norm(h - 1)
            n0 = UNIT_OF["v"]
            pe.wait_ge(S["lo_ready"], n0 + 1)
            pe.wait_ge(S["cnl_ready"], NQ + NKV)
            pe.wait_ge(S["st_ready"], RH)
            for b in range(TB):
                free(pe, f"v{b}")
                for k in range(NKV):
                    blk = slice(P * b, P * b + P)
                    w = slice(T * k, T * k + T)
                    mm = s3(pe, cnh[:, NQ + k, blk], cnl[:, NQ + k, blk], whi[n0 % RING][:, w], wlo[n0 % RING][:, w],
                            psum[:, bank[f"v{b}"], :], k == 0, k == NKV - 1)
                if b == 1:
                    ret_mean(RH - 1)
            mm.then_inc(S["unit_used"], 1)
            head_unit(0)
            sum_columns(pe, GN + RH - 1)
            for h in range(HEADS):
                scores(h)
                if h == 0:
                    ret_norm(RH - 1)
                if h + 1 < HEADS:
                    head_unit(h + 1)
                fills = FILL[h]
                if h == 0:
                    fill(fills[0])
                    fill(fills[1])
                elif EARLY[h]:
                    project(fills[0])
                else:
                    project(fills[0], range(KD // 2))
                turn_probs(h)
                if h == 0:
                    fill(fills[2])
                    fill(fills[3])
                elif EARLY[h]:
                    project(fills[1])
                else:
                    project(fills[0], range(KD // 2, KD))
                attend(h)
            for i in range(4):
                n0 = UNIT_OF[f"bm{i}"]
                pe.wait_ge(S["lo_ready"], n0 + 1)
                if i == 0:
                    pe.wait_ge(S["ol_ready"], HEADS)
                for half in range(2):
                    product(f"bm{2 * i + half}", [(yh[:, k, :], yl[:, k, :]) for k in range(4)], n0,
                            range(4 * half, 4 * half + 4), done=half == 1)
                project(f"gm{2 * i}")
                project(f"gm{2 * i + 1}")
            for m in range(KD):
                n0 = UNIT_OF[f"wo{m}"]
                pe.wait_ge(S["lo_ready"], n0 + 1)
                if m >= 2:
                    pe.wait_ge(S["sq_ready"], SQ0[POSTM] + m - 1)
                for k in range(KD):
                    if m == 0:
                        pe.wait_ge(S["ml_ready"], k + 1)
                    hi, lo = tile(n0, k)
                    mm = s3(pe, hi, lo, mh[:, k, :], ml[:, k, :], psum[:, 4 + m % 2, :], k == 0, k == KD - 1)
                mm.then_inc(S["unit_used"], 1)
            sum_columns(pe, POSTM)
            broadcast(pe, POSTM)

            ffn(1, UF2)

        @block.scalar
        def _(act):
            def ffn(f, n0):
                s, j0 = (0, 2)[f], NJ * f
                if f == 0:
                    split_hi(act, n0)
                for k in range(KD):
                    enter_act(act, s, k)
                if f == 0:
                    split_hi(act, n0 + 1)
                root(act, PRE_N[s], D)
                if f == 0:
                    split_hi(act, n0 + 2)
                keep_rs(act, PRE_N[s], s)
                if f == 0:
                    split_hi(act, n0 + 3)

                with act.Fori(0, NJ // 2) as i:
                    for c in range(2):
                        j = 2 * i + c
                        split_hi(act, n0 + 4 + 2 * c, 4 * i, i)
                        act.wait_ge(S["gs_ready"], j + (j0 + 1))
                        act.activation(sq[c][:], sq[c][:], ACT.Silu).then_inc(S["silu_ready"], 1)
                        split_hi(act, n0 + 5 + 2 * c, 4 * i, i)
                        act.wait_ge(S["a_ready"], j + (j0 + 1))
                        act.activation(ah[:, j, :], av[c][:], ACT.Copy).then_inc(S["ah_ready"], 1)

                nb, n, post = n0 + W1_UNITS, POST_N[s], ("post1", "postm", "post2")[s]
                for m in range(KD):
                    u0 = nb + 3 * m
                    split_hi(act, u0 + 4)
                    split_hi(act, u0 + 5)
                    act.wait_ge(S["unit_used"], u0 + 3)
                    phase_out(act, n, m, post)
                    split_hi(act, u0 + 6)
                root(act, n, D, halve=True)

            act.wait_ge(S["cols_landed"], 16)
            ffn(0, UF1)

            def nxt(name, ahead=4):
                split_hi(act, UNIT_OF[name] + ahead)

            for k in range(KD):
                enter_act(act, 1, k)
            root(act, PREM, D)
            keep_rs(act, PREM, 1)
            act.wait_ge(S["rope_args"], 2)
            act.activation(cos_r[:], turns[:, 1, :], ACT.Sin, bias=g("half_pi"), scale=-1.0).then_inc(S["sin_ready"], 1)
            act.activation(sin_r[:], angle[:, 1, :], ACT.Sin, scale=g("sign_r")).then_inc(S["sin_ready"], 1)
            act.activation(rope_m[64:96, :], turns[64:96, 0, :], ACT.Sin, bias=g("half_pi", rows=slice(64, 96)),
                           scale=-1.0).then_inc(S["sin_ready"], 1)
            act.activation(rope_m[96:P, :], angle[96:P, 0, :], ACT.Sin,
                           scale=g("sign_m", rows=slice(96, P))).then_inc(S["sin_ready"], 1)
            nxt("cq0")
            for c in range(NQ):
                act.wait_ge(S["evac_done"], evac[f"cq{c}"])
                square(act, CQ, c, cf[:, c, :])
                nxt(("cq1", "cq2", "ckv0")[c])
            nxt("ckv1")
            root(act, CQ, QR)
            for c in range(NKV):
                act.wait_ge(S["evac_done"], evac[f"ckv{c}"])
                square(act, CKV, c, cf[:, NQ + c, :])
            nxt("kr")

            def latent_hi(c):
                act.wait_ge(S["cn_scaled"], c + 1)
                act.activation(cnh[:, c, :], cf[:, c, :], ACT.Copy,
                               scale=g("qn", c) if c < NQ else g("kvn", c - NQ)).then_inc(S["cnh_ready"], 1)

            def rotated_hi(c4):
                act.wait_ge(S["rot_ready"], c4 + 1)
                act.activation(rh[:, c4, :], av[1][:], ACT.Copy).then_inc(S["rh_ready"], 1)

            for c in range(NQ):
                latent_hi(c)
            nxt("rq0")
            root(act, CKV, KVR)
            rotated_hi(0)
            nxt("rq1")
            rotated_hi(1)
            for c in range(NQ, NQ + NKV):
                latent_hi(c)
            nxt("rk0")
            rotated_hi(2)
            nxt("rk1")
            rotated_hi(3)
            for i in range(4):
                nxt(f"rv{i}")
            for b in range(TB):
                act.wait_ge(S["unit_used"], UNIT_OF["rv3"] + 1)
                if b == 0:
                    act.wait_ge(S["rscol_ready"], 1)
                act.activation(rvh[:, b, :], psum[:, 2 + b, :], ACT.Copy,
                               scale=rscol[:, b:b + 1]).then_inc(S["rvh_ready"], 1)

            def ret_split(h):
                act.wait_ge(S["st_ready"], h + 1)
                if h:
                    act.wait_ge(S["y_done"], h)
                act.activation(sth[:], st[:], ACT.Copy).then_inc(S["sth_ready"], 1)

            def ret_square(h):
                act.wait_ge(S["yc_ready"], h + 1)
                square(act, GN + h, 0, yc[h % 2][:])

            def ret_copy(h):
                act.wait_ge(S["y_done"], h + 1)
                if h == 1:
                    act.wait_ge(S["mask_ready"], 1)
                if h >= 2:
                    act.wait_ge(S["yl_ready"], h - 1)
                act.activation(yc[h % 2][:], psum[:, 5, :], ACT.Copy).then_inc(S["yf_ready"], 1)

            def ret_high(h):
                act.wait_ge(S["yg_ready"], 2 * h + 2)
                act.activation(yh[:, h, :], yc[h % 2][:], ACT.Copy, scale=g("gn", h)).then_inc(S["yh_ready"], 1)

            for h in range(RH):
                ret_split(h)
                if h:
                    ret_square(h - 1)
                nxt(f"rg{h}")
                act.wait_ge(S["evac_done"], evac[f"rg{h}"])
                act.activation(srg[:, h, :], av[h % 2][:], ACT.Silu).then_inc(S["silu_rg"], 1)
                if h:
                    root(act, GN + h - 1, RDV)
                ret_copy(h)
                if h:
                    ret_high(h - 1)
            for b in range(TB):
                act.wait_ge(S["unit_used"], UNIT_OF["v"] + 1)
                act.activation(vh[:, b, :], psum[:, bank[f"v{b}"], :], ACT.Copy).then_inc(S["vh_ready"], 1)
                if b == 1:
                    ret_square(RH - 1)
            nxt("v")
            act.activation(kh[64:96, :], kr[64:96, :], ACT.Copy).then_inc(S["kr_split"], 1)

            def head_split(h):
                act.wait_ge(S["unit_used"], UNIT_OF[f"head{h}"] + 1)
                act.activation(kh[0:NOPE, :], psum[0:NOPE, bank[f"k{h}"], :], ACT.Copy).then_inc(S["kh_ready"], 1)
                act.activation(qf[0:NOPE, :], psum[0:NOPE, bank[f"q{h}"], :], ACT.Copy).then_inc(S["qf_ready"], 1)

            def query_split(h):
                act.wait_ge(S["qrot_ready"], h + 1)
                act.wait_ge(S["qf_ready"], h + 1)
                act.activation(qh[0:DQK, :], qf[0:DQK, :], ACT.Copy).then_inc(S["qh_ready"], 1)

            def fill_act(name):
                nxt(name)
                if name[:2] == "gr":
                    m = int(name[2])
                    act.wait_ge(S["evac_done"], evac[name])
                    act.activation(av[m % 2][:], av[m % 2][:], ACT.Tanh, scale=0.5).then_inc(S["tanh_ready"], 1)

            head_split(0)
            query_split(0)
            nxt("head0")
            root(act, GN + RH - 1, RDV)
            ret_high(RH - 1)
            scale = 1.0 / math.sqrt(DQK)
            for h in range(HEADS):
                act.wait_ge(S["nmx_ready"], h + 1)
                for i in range(TB):
                    n = P * (i + 1)
                    row = slice(ROW_AT[n], ROW_AT[n] + n)
                    act.activation(pr[:, row], tri[:, row], ACT.Exp, bias=nmx[:, i:i + 1], scale=scale,
                                   accum_out=lsum[:, i:i + 1]).then_inc(S["exp_ready"], 1)
                if h + 1 < HEADS:
                    head_split(h + 1)
                    nxt(f"head{h + 1}")
                if EARLY[h] and h + 1 < HEADS:
                    query_split(h + 1)
                for f in FILL[h][:EARLY[h]]:
                    fill_act(f)
                act.wait_ge(S["pt_done"], h + 1)
                act.activation(pth[:], tri[:, 0:TRI], ACT.Copy).then_inc(S["pth_ready"], 1)
                if not EARLY[h] and h + 1 < HEADS:
                    query_split(h + 1)
                for f in FILL[h][EARLY[h]:]:
                    fill_act(f)
                act.wait_ge(S["pv_done"], h + 1)
                r = slice(64 * (h % 2), 64 * (h % 2) + 64)
                act.activation(yh[r, h // 2, :], psum[r, 5 + 2 * (h % 2), :], ACT.Copy).then_inc(S["oh_ready"], 1)
            for i in range(4):
                nxt(f"bm{i}")
                for m in (2 * i, 2 * i + 1):
                    nxt(f"gm{m}")
                    act.wait_ge(S["evac_done"], evac[f"gm{m}"])
                    act.activation(av[m % 2][:], av[m % 2][:], ACT.Tanh, scale=0.5).then_inc(S["tanh_ready"], 1)
                    act.wait_ge(S["merged_in"], m + 1)
                    act.activation(mh[:, m, :], mret[:, m, :], ACT.Copy, scale=0.5).then_inc(S["mh_ready"], 1)
            for m in range(KD):
                act.wait_ge(S["unit_used"], UNIT_OF[f"wo{m}"] + 1)
                phase_out(act, POSTM, m, "postm")
                nxt(f"wo{m}")
            root(act, POSTM, D)

            ffn(1, UF2)

        @block.vector
        def _(dve):
            def ffn(f, n0):
                s, j0 = (0, 2)[f], NJ * f
                if f == 0:
                    split_lo(dve, n0)
                for k in range(KD):
                    if f == 1:
                        exit_dve(dve, 1, k)
                    enter_dve(dve, s, k)
                if f == 0:
                    split_lo(dve, n0 + 1)
                invert(dve, PRE_N[s])
                if f == 0:
                    split_lo(dve, n0 + 2)
                    split_lo(dve, n0 + 3)
                else:
                    dve.wait_ge(S["lo_ready"], n0 + 4)
                dve.wait_ge(S["rsb_ready"], s + 1)

                def gates(i, first=False):
                    for c in range(2):
                        j = 2 * i + c
                        dve.wait_ge(S["unit_used"], 4 * i + (n0 + 2 * c + 1))
                        if not first:
                            dve.wait_ge(S["a_ready"], j + (j0 - 1))
                        dve.tensor_tensor(sq[c][:], psum[:, c, :], rsb[:], ALU.mult).then_inc(S["gs_ready"], 1)
                        split_lo(dve, n0 + 4 + 2 * c, 4 * i)
                        dve.wait_ge(S["sgr_ready"], j + (j0 + 1))
                        dve.wait_ge(S["unit_used"], 4 * i + (n0 + 2 * c + 2))
                        dve.tensor_tensor(av[c][:], psum[:, 2 + c, :], av[c][:], ALU.mult).then_inc(S["a_ready"], 1)
                        split_lo(dve, n0 + 5 + 2 * c, 4 * i)
                        dve.wait_ge(S["ah_ready"], j + (j0 + 1))
                        dve.tensor_tensor(al[:, j, :], av[c][:], ah[:, j, :].bitcast(F32),
                                          ALU.subtract).then_inc(S["al_ready"], 1)

                gates(0, first=True)
                with dve.Fori(1, NJ // 2) as i:
                    gates(i)
                nb, n = n0 + W1_UNITS, POST_N[s]
                for m in range(KD):
                    for part in range(2):
                        split_lo(dve, nb + 3 * m + 4 + part)
                    accumulate(dve, n, m)
                    split_lo(dve, nb + 3 * m + 6)
                invert(dve, n)

            dve.wait_ge(S["cols_landed"], 16)
            ffn(0, UF1)

            for k in range(KD):
                exit_dve(dve, 0, k)
                enter_dve(dve, 1, k)
            invert(dve, PREM)
            dve.tensor_copy(rscol[:], rcol[:]).then_inc(S["rscol_ready"], 1)

            chain = [0]

            def link(ins):
                chain[0] += 1
                ins.then_inc(S["chain"], 1)
                dve.wait_ge(S["chain"], chain[0])

            dve.wait_ge(S["pos_landed"], 16)
            for t, name in ((0, "freq_m"), (1, "freq_r")):
                link(dve.tensor_scalar(angle[:, t, :], posi[:], g(name), None, ALU.mult))
            magic = 1.5 * 2.0 ** 23
            link(dve.tensor_scalar(turns[:], angle[:], 1 / (2 * math.pi), magic, ALU.mult, ALU.add))
            link(dve.tensor_scalar(turns[:], turns[:], magic, None, ALU.subtract))
            link(dve.tensor_scalar(turns_hi[:], turns[:], 1 / 4096.0, magic, ALU.mult, ALU.add))
            link(dve.tensor_scalar(turns_hi[:], turns_hi[:], magic, None, ALU.subtract))
            link(dve.scalar_tensor_tensor(out=turns[:], in0=turns_hi[:], scalar=-4096.0, in1=turns[:],
                                          op0=ALU.mult, op1=ALU.add))
            for part in pi_parts(4):
                for src, f in ((turns_hi, 4096.0), (turns, 1.0)):
                    link(dve.scalar_tensor_tensor(out=angle[:], in0=src[:], scalar=-part * f, in1=angle[:],
                                                  op0=ALU.mult, op1=ALU.add))
            link(dve.tensor_scalar(angle[:], angle[:], 3.1415925, -3.1415925, ALU.min, ALU.max))
            dve.scalar_tensor_tensor(out=turns[:], in0=angle[:], scalar=-1.0, in1=angle[:], op0=ALU.mult,
                                     op1=ALU.max).then_inc(S["rope_args"], 2)
            dve.wait_ge(S["rsb_ready"], 2)
            dve.wait_ge(S["sin_ready"], 2)
            dve.tensor_tensor(cos_r[:], cos_r[:], rsb[:], ALU.mult).then_inc(S["cos_scaled"], 1)
            dve.tensor_tensor(sin_r[:], sin_r[:], rsb[:], ALU.mult).then_inc(S["cos_scaled"], 1)

            given = [0]

            def gives(ins, name):
                assert EV[given[0]] == name, (EV[given[0]], name)
                given[0] += 1
                ins.then_inc(S["evac_done"], 1)

            def used(name):
                dve.wait_ge(S["unit_used"], UNIT_OF[name] + 1)

            def latent(name, c):
                used(name)
                gives(dve.tensor_tensor(cf[:, c, :], psum[:, bank[name], :], rsb[:], ALU.mult), name)

            def latent_low(c):
                dve.wait_ge(S["cnh_ready"], c + 1)
                dve.scalar_tensor_tensor(out=cnl[:, c, :], in0=cf[:, c, :],
                                         scalar=g("qn", c) if c < NQ else g("kvn", c - NQ),
                                         in1=cnh[:, c, :].bitcast(F32), op0=ALU.mult,
                                         op1=ALU.subtract).then_inc(S["cnl_ready"], 1)

            def latent_scale(c):
                dve.wait_ge(S["bc_ready"], (CQ if c < NQ else CKV) + 1)
                dve.tensor_tensor(cf[:, c, :], cf[:, c, :], psum[:, BC, :], ALU.mult).then_inc(S["cn_scaled"], 1)

            for c in range(NQ):
                latent(f"cq{c}", c)
                accumulate(dve, CQ, c)
            latent("ckv0", NQ)
            latent("ckv1", NQ + 1)
            invert(dve, CQ)
            used("kr")
            dve.wait_ge(S["sin_ready"], 4)
            b = bank["kr"]
            dve.tensor_tensor(av[0][64:96, :], psum[96:P, b, :], rope_m[96:P, :], ALU.mult).then_inc(S["chain"], 1)
            chain[0] += 1
            gives(dve.tensor_tensor(av[1][64:96, :], psum[64:96, b, :], rope_m[64:96, :], ALU.mult), "kr")
            dve.wait_ge(S["chain"], chain[0])
            dve.wait_ge(S["evac_done"], evac["kr"])
            link(dve.tensor_tensor(av[0][64:96, :], av[0][64:96, :], av[1][64:96, :], ALU.add))
            link(dve.tensor_tensor(kr[64:96, :], av[0][64:96, :], rsb[64:96, :], ALU.mult))
            accumulate(dve, CKV, 0)
            for c in range(NQ):
                latent_scale(c)
                latent_low(c)

            def rotate(name, c4):
                used(name)
                if c4:
                    dve.wait_ge(S["rl_ready"], c4)
                dve.wait_ge(S["cos_scaled"], 2)
                bk = bank[name]
                for q in range(4):
                    src, dst = 32 * (q ^ 1), 32 * q
                    ins = dve.tensor_tensor(av[0][dst:dst + 32, :], psum[src:src + 32, bk, :],
                                            sin_r[src:src + 32, :], ALU.mult)
                ins.then_inc(S["chain"], 1)
                chain[0] += 1
                gives(dve.tensor_tensor(av[1][:], psum[:, bk, :], cos_r[:], ALU.mult), name)
                dve.wait_ge(S["chain"], chain[0])
                dve.wait_ge(S["evac_done"], evac[name])
                dve.tensor_tensor(av[1][:], av[1][:], av[0][:], ALU.add).then_inc(S["rot_ready"], 1)
                dve.wait_ge(S["rh_ready"], c4 + 1)
                dve.tensor_tensor(rl[:, c4, :], av[1][:], rh[:, c4, :].bitcast(F32),
                                  ALU.subtract).then_inc(S["rl_ready"], 1)

            used("rq0")
            invert(dve, CKV)
            rotate("rq0", 0)
            rotate("rq1", 1)
            for c in range(NQ, NQ + NKV):
                latent_scale(c)
                latent_low(c)
            rotate("rk0", 2)
            rotate("rk1", 3)
            for b in range(TB):
                dve.wait_ge(S["rvh_ready"], b + 1)
                gives(dve.scalar_tensor_tensor(out=rvl[:, b, :], in0=psum[:, 2 + b, :], scalar=rscol[:, b:b + 1],
                                               in1=rvh[:, b, :].bitcast(F32), op0=ALU.mult,
                                               op1=ALU.subtract), f"rv{b}")
            dve.wait_ge(S["decay_landed"], 16)

            def ret_center(h):
                dve.wait_ge(S["mu_done"], h + 1)
                dve.scalar_tensor_tensor(out=yc[h % 2][:], in0=psum[:, BC, :], scalar=-1.0 / RDV,
                                         in1=yc[h % 2][:], op0=ALU.mult, op1=ALU.add).then_inc(S["yc_ready"], 1)

            def ret_gate(h):
                dve.wait_ge(S["bc_ready"], GN + h + 1)
                y = yc[h % 2]
                dve.tensor_tensor(y[:], y[:], psum[:, BC, :], ALU.mult).then_inc(S["yg_ready"], 1)
                dve.wait_ge(S["silu_rg"], h + 1)
                dve.wait_ge(S["yg_ready"], 2 * h + 1)
                dve.tensor_tensor(y[:], y[:], srg[:, h, :], ALU.mult).then_inc(S["yg_ready"], 1)
                dve.wait_ge(S["yh_ready"], h + 1)
                dve.scalar_tensor_tensor(out=yl[:, h, :], in0=y[:], scalar=g("gn", h),
                                         in1=yh[:, h, :].bitcast(F32), op0=ALU.mult,
                                         op1=ALU.subtract).then_inc(S["yl_ready"], 1)

            for h in range(RH):
                dve.wait_ge(S["sr_done"], h + 1)
                for b in range(TB):
                    n = T - P * b
                    row = slice(ROW_AT[n], ROW_AT[n] + n)
                    if h:
                        dve.wait_ge(S["stl_ready"], h)
                    ins = dve.tensor_tensor(st[:, row], tri[:, row], dec[:, h, 0:n], ALU.mult)
                ins.then_inc(S["st_ready"], 1)
                dve.wait_ge(S["sth_ready"], h + 1)
                dve.tensor_tensor(stl[:], st[:], sth[:].bitcast(F32), ALU.subtract).then_inc(S["stl_ready"], 1)
                if h:
                    ret_center(h - 1)
                used(f"rg{h}")
                if h >= 2:
                    dve.wait_ge(S["silu_rg"], h - 1)
                ins = dve.tensor_tensor(av[h % 2][:], psum[:, bank[f"rg{h}"], :], rsb[:], ALU.mult)
                gives(ins, f"rg{h}")
                if h:
                    invert(dve, GN + h - 1)
                    ret_gate(h - 1)
            for b in range(TB):
                if b == 1:
                    ret_center(RH - 1)
                dve.wait_ge(S["vh_ready"], b + 1)
                gives(dve.tensor_tensor(vl[:, b, :], psum[:, bank[f"v{b}"], :], vh[:, b, :].bitcast(F32),
                                        ALU.subtract), f"v{b}")
            dve.wait_ge(S["kr_split"], 1)
            dve.tensor_tensor(kl[64:96, :], kr[64:96, :], kh[64:96, :].bitcast(F32),
                              ALU.subtract).then_inc(S["kr_split"], 1)

            def head_split(h):
                used(f"head{h}")
                bq, bk = bank[f"q{h}"], bank[f"k{h}"]
                link(dve.tensor_tensor(av[0][64:96, :], psum[96:P, bq, :], rope_m[96:P, :], ALU.mult))
                link(dve.tensor_tensor(av[1][64:96, :], psum[64:96, bq, :], rope_m[64:96, :], ALU.mult))
                dve.tensor_tensor(qf[64:96, :], av[0][64:96, :], av[1][64:96, :], ALU.add).then_inc(S["qrot_ready"], 1)
                dve.wait_ge(S["kh_ready"], h + 1)
                gives(dve.tensor_tensor(kl[0:NOPE, :], psum[0:NOPE, bk, :], kh[0:NOPE, :].bitcast(F32),
                                        ALU.subtract), f"k{h}")

            def query_split(h):
                dve.wait_ge(S["qh_ready"], h + 1)
                ins = dve.tensor_tensor(ql[0:DQK, :], qf[0:DQK, :], qh[0:DQK, :].bitcast(F32), ALU.subtract)
                gives(ins, f"q{h}")

            def fill_dve(name):
                n0 = UNIT_OF[name]
                used(name)
                if name[:2] == "gr":
                    m = int(name[2])
                    gives(dve.tensor_tensor(av[m % 2][:], psum[:, bank[name], :], rsb[:], ALU.mult), name)
                    dve.wait_ge(S["tanh_ready"], m + 1)
                    link(dve.scalar_tensor_tensor(out=mret[:, m, :], in0=av[m % 2][:], scalar=1.0,
                                                  in1=mret[:, m, :], op0=ALU.add, op1=ALU.mult))
                    return
                for half, part in enumerate("ab"):
                    m = 2 * int(name[2]) + half
                    gives(dve.tensor_copy(mret[:, m, :], psum[:, bank[name + part], :]), name + part)

            head_split(0)
            query_split(0)
            invert(dve, GN + RH - 1)
            ret_gate(RH - 1)
            scale = 1.0 / math.sqrt(DQK)
            for h in range(HEADS):
                dve.wait_ge(S["s_done"], h + 1)
                for i in range(TB):
                    n = P * (i + 1)
                    row = slice(ROW_AT[n], ROW_AT[n] + n)
                    ins = dve.tensor_reduce(mx[:, i:i + 1], tri[:, row], AX.X, ALU.max)
                link(ins)
                dve.tensor_scalar(nmx[:], mx[:], -scale, None, ALU.mult).then_inc(S["nmx_ready"], 1)
                dve.wait_ge(S["exp_ready"], 4 * h + 4)
                link(dve.reciprocal(linv[:], lsum[:]))
                for i in range(TB):
                    n = P * (i + 1)
                    row = slice(ROW_AT[n], ROW_AT[n] + n)
                    ins = dve.tensor_scalar(pr[:, row], pr[:, row], linv[:, i:i + 1], None, ALU.mult)
                ins.then_inc(S["p_ready"], 1)
                if h + 1 < HEADS:
                    head_split(h + 1)
                if EARLY[h] and h + 1 < HEADS:
                    query_split(h + 1)
                for f in FILL[h][:EARLY[h]]:
                    fill_dve(f)
                dve.wait_ge(S["pth_ready"], h + 1)
                dve.tensor_tensor(ptl[:], tri[:, 0:TRI], pth[:].bitcast(F32), ALU.subtract).then_inc(S["ptl_ready"], 1)
                if not EARLY[h] and h + 1 < HEADS:
                    query_split(h + 1)
                for f in FILL[h][EARLY[h]:]:
                    fill_dve(f)
                dve.wait_ge(S["oh_ready"], h + 1)
                r = slice(64 * (h % 2), 64 * (h % 2) + 64)
                dve.tensor_tensor(yl[r, h // 2, :], psum[r, 5 + 2 * (h % 2), :], yh[r, h // 2, :].bitcast(F32),
                                  ALU.subtract).then_inc(S["ol_ready"], 1)
            for i in range(4):
                for m in (2 * i, 2 * i + 1):
                    used(f"gm{m}")
                    if m:
                        dve.wait_ge(S["merged_in"], m)
                    gives(dve.tensor_tensor(av[m % 2][:], psum[:, m % 2, :], rsb[:], ALU.mult), f"gm{m}")
                    dve.wait_ge(S["tanh_ready"], KD + m + 1)
                    dve.wait_ge(S["evac_done"], evac[f"gm{m}"])
                    gives(dve.scalar_tensor_tensor(out=av[m % 2][:], in0=av[m % 2][:], scalar=1.0,
                                                   in1=psum[:, 2 + m % 2, :], op0=ALU.add, op1=ALU.mult), f"bm{m}")
                    dve.wait_ge(S["evac_done"], evac[f"bm{m}"])
                    dve.tensor_tensor(mret[:, m, :], mret[:, m, :], av[m % 2][:], ALU.add).then_inc(S["merged_in"], 1)
                    dve.wait_ge(S["mh_ready"], m + 1)
                    dve.scalar_tensor_tensor(out=ml[:, m, :], in0=mret[:, m, :], scalar=0.5,
                                             in1=mh[:, m, :].bitcast(F32), op0=ALU.mult,
                                             op1=ALU.subtract).then_inc(S["ml_ready"], 1)
            for m in range(KD):
                accumulate(dve, POSTM, m)
            invert(dve, POSTM)

            ffn(1, UF2)
            for k in range(KD):
                exit_dve(dve, 2, k)

        @block.gpsimd
        def _(pool):
            def ffn(f):
                s, j0 = (0, 2)[f], NJ * f
                for k in range(KD):
                    accumulate(pool, PRE_N[s], k)
                pool.wait_ge(S["rsb_ready"], (1, 3)[f])

                def gates(i, first=False):
                    for c in range(2):
                        j = 2 * i + c
                        pool.wait_ge(S["silu_ready"], j + (j0 + 1))
                        if not first:
                            pool.wait_ge(S["al_ready"], j + (j0 - 1))
                        pool.tensor_tensor(av[c][:], sq[c][:], rsb[:], ALU.mult).then_inc(S["sgr_ready"], 1)

                gates(0, first=True)
                with pool.Fori(1, NJ // 2) as i:
                    gates(i)

            ffn(0)
            for k in range(KD):
                accumulate(pool, PREM, k)
            pool.wait_ge(S["lo_ready"], UM + 4)
            for n in range(UM + 4, UF2 + 4):
                split_lo(pool, n)
                if n == UM + 8:
                    pool.wait_ge(S["tri_landed"], 16)
                    pool.tensor_copy(maskb[:], trif[:]).then_inc(S["mask_ready"], 1)
                    pool.tensor_copy(identb[:], ident).then_inc(S["mask_ready"], 1)
            ffn(1)
            for k in range(1, KD, 2):
                pool.wait_ge(S["fs_ready"], 16 + k + 1)
                pool.tensor_tensor(hres[:, k, :], hres[:, k, :], fo[:, k, :], ALU.add).then_inc(S["h_odd_ready"], 1)


def kernel(**inputs):
    import numpy as np
    import concourse.bacc as bacc
    from concourse.bass_utils import run_bass_kernel_spmd as run

    w = {k: np.asarray(v) for k, v in inputs.items()}

    def tiles(m, col_lists):
        t = m.reshape(-1, P, m.shape[1])
        return [np.ascontiguousarray(t[:, :, c].transpose(1, 0, 2).reshape(P, -1)) for c in col_lists]

    def ffn_units(w1, w2):
        order = []
        for j in range(NJ):
            order += [np.arange(P * j, P * j + P), FF + np.arange(P * j, P * j + P)]
        units = np.zeros((W1_UNITS + W2_UNITS, P, UNIT), w1.dtype)
        units[:W1_UNITS] = tiles(w1, order)
        for part, (k0, n) in enumerate(zip(PART0, PART)):
            units[W1_UNITS + part::len(PART), :, :n * P] = tiles(
                w2[P * k0:P * (k0 + n)], [np.arange(P * m, P * m + P) for m in range(KD)])
        return units

    w_in, uq, ukv = w["w_in"][0], w["mla_w_uq"][0], w["mla_w_ukv"][0]
    at = np.cumsum([0, QR, KVR, ROPE, RH * RDK, RH * RDK, RH * RDV, RH * RDV, D, D])
    half = ROPE // 2

    def mix_unit(name):
        kind, i = name.rstrip("0123456789"), int(name[len(name.rstrip("0123456789")):] or 0)
        run_of = {"cq": at[0], "ckv": at[1], "rq": at[3], "rk": at[4], "rg": at[6], "gm": at[7], "gr": at[8]}
        if kind in run_of:
            return tiles(w_in, [run_of[kind] + P * i + np.arange(P)])[0]
        if kind == "kr":
            r = at[2] + np.arange(ROPE)
            return tiles(w_in, [np.concatenate([at[2] - 64 + np.arange(64), r, r[half:], r[:half]])])[0]
        if kind == "rv":
            return tiles(w_in[2 * P * i:2 * P * (i + 1)], [at[5] + np.arange(T)])[0]
        if kind == "v":
            c = np.concatenate([(NOPE + DV) * h + NOPE + np.arange(DV) for h in range(HEADS)])
            return tiles(ukv, [c])[0]
        if kind == "head":
            c = DQK * i + np.arange(DQK)
            q = tiles(uq, [np.concatenate([c, c[NOPE + half:], c[NOPE:NOPE + half]])])[0]
            k = tiles(ukv, [(NOPE + DV) * i + np.arange(P)])[0]
            return np.concatenate([q, k, np.zeros((P, UNIT - HEAD_UNIT), q.dtype)], axis=1)
        if kind in ("br", "bm"):
            m = w["w_branch_ret" if kind == "br" else "w_branch_mla"][0]
            return np.concatenate(tiles(m, [P * c + np.arange(P) for c in (2 * i, 2 * i + 1)]), axis=1)
        return tiles(w["w_out"][0], [P * i + np.arange(P)])[0]

    cols = np.zeros((P, NCOLS), np.float32)
    for name, key in (("pre1", "ffn1_pre_w"), ("post1", "ffn1_post_w"), ("prem", "mix_pre_w"),
                      ("qn", "mla_q_norm_w"), ("kvn", "mla_kv_norm_w"), ("gn", "ret_gn_w"),
                      ("postm", "mix_post_w"), ("pre2", "ffn2_pre_w"), ("post2", "ffn2_post_w")):
        v = w[key][0].reshape(-1, P).T
        cols[:, COLS[name]:COLS[name] + v.shape[1]] = v
    p = np.arange(P)
    for name, v in (("eps", EPS), ("eps4", 4 * EPS), ("half_pi", math.pi / 2),
                    ("freq_m", ROPE_BASE ** (-(p % half) / half)),
                    ("sign_m", np.where(p % ROPE < half, -1.0, 1.0)),
                    ("freq_r", ROPE_BASE ** (-(p % 32) / 32.0)),
                    ("sign_r", np.where(p % 64 < 32, 1.0, -1.0))):
        cols[:, COLS[name]] = v
    consts = np.concatenate([np.ones((P, P)), np.eye(P), np.where(p[:, None] >= p[None, :], 0.0, MASKED)],
                            axis=1).astype(np.float32)
    lag = np.arange(T)[None, :] - p[:, None]
    decay = np.stack([np.where(lag >= 0, np.exp(np.maximum(lag, 0) * np.log(1 - 2.0 ** (-5.0 - h))), 0.0)
                      for h in range(RH)], axis=1) * RDK ** -0.5

    arrays = {
        "x_t": np.ascontiguousarray(w["x"][0].T.reshape(KD, P, T).transpose(1, 0, 2)),
        "pos_b": np.ascontiguousarray(np.broadcast_to(w["positions"][0][None, :], (P, T))),
        "w_ffn1": ffn_units(w["ffn1_w1"][0], w["ffn1_w2"][0]),
        "w_mix": np.stack([mix_unit(n) for n in MIX]),
        "w_ffn2": ffn_units(w["ffn2_w1"][0], w["ffn2_w2"][0]),
        "cols": cols, "consts": consts, "decay": decay.astype(np.float32),
    }
    nc = bacc.Bacc("TRN2", target_bir_lowering=False, num_devices=1)
    args = [nc.dram_tensor(n, a.shape, mybir.dt.from_np(a.dtype), kind="ExternalInput").ap()
            for n, a in arrays.items()]
    args.append(nc.dram_tensor("out_t", (P, KD, T), F32, kind="ExternalOutput").ap())
    build(nc, *args)
    r = run(nc, [arrays], core_ids=[0])
    got = r.results[0]["out_t"]
    return np.ascontiguousarray(got.transpose(2, 1, 0).reshape(1, T, D))
```

```python
import math

import concourse.bass as bass
from concourse import mybir

F32 = mybir.dt.float32
F32R = mybir.dt.float32r
BF16 = mybir.dt.bfloat16
I32 = mybir.dt.int32
ACT = mybir.ActivationFunctionType
ALU = mybir.AluOpType
AX = mybir.AxisListType

P = 128
D = 1024
KD = D // P
T = 512
TB = T // P
FF = 2816
NJ = FF // P
PART = [8, 7, 7]
PART0 = [0, 8, 15]
QR, KVR = 384, 256
NQ, NKV = QR // P, KVR // P
HEADS, NOPE, ROPE, DV = 8, 64, 32, 64
DQK = NOPE + ROPE
RH, RDK, RDV = 4, 64, 128
EPS = 1e-6
ROPE_BASE = 10000.0
MASKED = -1e30

UNIT = KD * P
HEAD_UNITS = ((NQ + NKV) * P, NQ * P)
W1_UNITS, W2_UNITS = 2 * NJ, len(PART) * KD
RING = 4
ROTATED = [0, 2, 1, 3]
HALVES = [slice(0, T // 2), slice(T // 2, T)]

MIX = (["cq0", "cq1", "cq2", "ckv0", "ckv1"] + [f"rv{i}" for i in range(4)] + ["kr", "rq0", "rk0", "rq1", "rk1"]
       + [f"rg{i}" for i in range(RH)] + ["head0", "v"])
CUT = 4
EARLY = [1, 0, 0, 0, 0, 0, 0, 2]
FILL = [["gr0", "gr1"], ["gr2"], ["gr3"], ["gr4"], ["gr5"], ["gr6"], ["gr7"], ["br0", "br1", "br2", "br3"]]
for _h in range(HEADS):
    if _h + 1 < HEADS:
        MIX.append(f"head{_h + 1}")
    MIX += FILL[_h]
for _i in range(4):
    MIX += [f"gm{2 * _i}", f"gm{2 * _i + 1}", f"bm{_i}"]
MIX += [f"wo{m}" for m in range(KD)]
UF1 = 0
UM = UF1 + W1_UNITS + W2_UNITS
UF2 = UM + len(MIX)
U_END = UF2 + W1_UNITS + W2_UNITS
UNIT_OF = {name: UM + i for i, name in enumerate(MIX)}

PRE1, POST1, PREM, CQ, CKV, GN, POSTM, PRE2, POST2 = 0, 1, 3, 5, 6, 7, 11, 13, 15
SPLIT = {POST1: 1, POSTM: 2, POST2: 1}
CHUNKS = [KD, KD, 1, KD, KD, NQ, NKV, 1, 1, 1, 1, KD, 2, KD, KD, KD, 1]
FIRST_HALF = (POST1, PREM, POSTM, PRE2, POST2)
SQ0 = [sum(CHUNKS[:n]) for n in range(len(CHUNKS) + 1)]
AS_IT_IS = (CQ, CKV, GN, GN + 1, GN + 2, GN + 3, POSTM, POST2 + 1)
AC0 = [sum(c - (m in AS_IT_IS) for m, c in enumerate(CHUNKS[:n])) for n in range(len(CHUNKS) + 1)]

COLS, _at = {}, 0
for _name, _n in (("pre1", KD), ("post1", KD), ("prem", KD), ("qn", NQ), ("kvn", NKV), ("gn", RH), ("postm", KD),
                  ("pre2", KD), ("post2", KD), ("eps", 1), ("eps4", 1), ("freq_m", 1), ("sign_m", 1),
                  ("freq_r", 1), ("sign_r", 1), ("half_pi", 1)):
    COLS[_name] = _at
    _at += _n
NCOLS = _at

ROW_AT = {512: 0, 384: 512, 128: 896, 256: 1024}
TRI = 1280
PARTS = [slice(0, T), slice(T, TRI)]



def pi_parts(n):
    rest, out = 2 * math.pi, []
    for i in range(n):
        step = 2.0 ** (-9 - 12 * i)
        part = math.floor(rest / step) * step if i < n - 1 else rest
        out.append(part)
        rest -= part
    return out


BANK = {"cq0": 0, "cq1": 1, "cq2": 2, "ckv0": 3, "ckv1": 0, "kr": 1, "rq0": 0, "rk0": 2, "rq1": 3, "rk1": 1,
        "rv0": 2, "rv1": 3, "rv2": 4, "rv3": 5, "rg0": 0, "rg1": 1, "rg2": 0, "rg3": 1,
        "v0": 7, "v1": 2, "v2": 3, "v3": 1, "q0": 1, "k0": 0}


def build(nc, x, pos, wf1, wmix, wf2, cols, consts, decay, out):
    h1_dram = nc.dram_tensor("h1_spill", (P, KD, T), F32, kind="Internal").ap()
    base = -(-nc.sbuf_base // 128) * 128
    top = [base]

    def at(name, shape, dt, offset):
        return nc.alloc_sbuf_tensor_at(name, shape, dt, offset=offset)

    def place(name, shape, dt):
        size = (math.prod(shape[1:]) * 4 + 31) // 32 * 32
        top[0] += size
        return at(name, shape, dt, top[0] - size)

    raw = [place(f"raw{s}", [P, UNIT], F32) for s in range(RING)]
    whi = [place(f"whi{s}", [P, UNIT], F32R) for s in range(RING)]
    wlo = [place(f"wlo{s}", [P, UNIT], F32R) for s in range(RING)]
    xh_at = top[0]
    xh = place("xh", [P, KD, T], F32R)
    xl = place("xl", [P, KD, T], F32R)
    fo = at("fo", [P, KD, T], F32, xh_at)
    sq = [place(f"sq{s}", [P, T], F32) for s in range(2)]
    av = [place(f"av{s}", [P, T], F32) for s in range(2)]
    acc = place("acc", [P, T], F32)
    rsb = place("rsb", [P, T], F32)
    dg = place("dg", [P, TB, P], F32)
    cst = place("cst", [P, 2 * P], F32)
    kf = acc
    ones, ident = cst[:, 0:P], cst[:, P:2 * P]
    gain = place("gain", [P, NCOLS], F32)
    rms = place("rms", [P, RH * TB], F32)
    rcol = place("rcol", [P, RH * TB], F32)
    vsum = place("vsum", [P, TB, RH], F32)
    rscol = place("rscol", [P, TB], F32)
    mx = place("mx", [P, TB], F32)
    unread = place("unread", [P, 1], F32)
    nmx = place("nmx", [P, TB], F32)
    lsum = place("lsum", [P, TB], F32)
    linv = place("linv", [P, TB], F32)
    u = -(-top[0] // 64) * 64

    ah = at("ah", [P, NJ, T], F32R, u)
    al = at("al", [P, NJ, T], F32R, u + 45056)
    hres = at("hres", [P, KD, T], F32, u + 90112)
    maskb = at("maskb", [P, P], BF16, u)
    identb = at("identb", [P, P], BF16, u + 256)
    rope_m = at("rope_m", [P, T], F32, u + 512)
    cnh = at("cnh", [P, NQ + NKV, T], F32R, u + 2560)
    cnl = at("cnl", [P, NQ + NKV, T], F32R, u + 12800)
    kr = at("kr", [P, T], F32, u + 23040)
    cos_r = at("cos_r", [P, T], F32, u + 25088)
    sin_r = at("sin_r", [P, T], F32, u + 27136)
    rh = at("rh", [P, 4, T], F32R, u + 29184)
    rl = at("rl", [P, 4, T], F32R, u + 37376)
    rvh = at("rvh", [P, TB, T], F32R, u + 45568)
    rvl = at("rvl", [P, TB, T], F32R, u + 53760)
    st = at("st", [P, TRI], F32, u + 61952)
    sth = at("sth", [P, TRI], F32R, u + 67072)
    stl = at("stl", [P, TRI], F32R, u + 72192)
    angle = at("angle", [P, 2, T], F32, u + 106496)
    turns = at("turns", [P, T], F32, u + 110592)
    turns_hi = at("turns_hi", [P, T], F32, u + 112640)
    posi = at("posi", [P, T], I32, u + 112640)
    angle_abs = at("angle_abs", [P, 2, T], F32, u + 61952)
    cf = at("cf", [P, NQ + NKV, T], F32, u + 77312)
    trif = at("trif", [P, P], F32, u + 87552)
    yr = at("yr", [P, RH, T], F32, u + 77312)
    dgb = at("dgb", [P, TB, P], F32, u + 85504)
    dec = at("dec", [P, RH, T], F32, u + 89600)
    yh = at("yh", [P, RH, T], F32R, u + 89600)
    yl = at("yl", [P, RH, T], F32R, u + 97792)
    rvc = at("rvc", [P, TB, T], F32, u + 106496)
    vh = at("vh", [P, TB, T], F32R, u + 25088)
    vl = at("vl", [P, TB, T], F32R, u + 33280)
    qh = at("qh", [P, T], F32R, u + 41472)
    ql = at("ql", [P, T], F32R, u + 43520)
    kh = at("kh", [P, T], F32R, u + 106496)
    kl = at("kl", [P, T], F32R, u + 108544)
    qf = at("qf", [P, T], F32, u + 110592)
    pr = at("pr", [P, TRI], F32, u + 51712)
    pth = at("pth", [P, TRI], F32R, u + 56832)
    ptl = at("ptl", [P, TRI], F32R, u + 61952)
    mret = at("mret", [P, KD, T], F32, u + 69120)
    oh = [at(f"oh{c}", [P, T], F32R, u + o) for c, o in enumerate((23040, 67072, 85504, 87552))]
    ol = [at(f"ol{c}", [P, T], F32R, u + o) for c, o in enumerate((45568, 47616, 49664, 112640))]
    mh = at("mh", [P, KD, T], F32R, u + 2560)
    ml = at("ml", [P, KD, T], F32R, u + 25088)
    assert u + 114688 <= nc.sbuf_usable_end, (u, nc.sbuf_usable_end)

    psum = nc.alloc_psum_tensor("psum", [P, 8, T], F32)
    tri = psum[:, 2:5, :].rearrange("p b t -> p (b t)")
    COL, BC, SECOND = 6, 7, 3

    def g(name, i=0, rows=slice(0, P)):
        return gain[rows, COLS[name] + i:COLS[name] + i + 1]

    sems = ("raw0 raw1 raw2 raw3 cols_landed cst_landed hi_ready lo_ready unit_used x0 x1 x2 x3 x4 x5 x6 "
            "x7 xh_ready xl_ready sq_ready acc_ready col_ready rms_ready rc_ready dg_ready bc_ready "
            "rsb_ready rscol_ready gs_ready silu_ready sgr_ready a_ready ah_ready al_ready f_copied "
            "fs_ready h_ready h_pool_ready spilled pos_landed tri_landed decay_landed mask_ready chain "
            "rope_args sin_ready cos_scaled evac_done cn_scaled cnh_ready cnl_ready rot_ready rh_ready "
            "rl_ready rvh_ready silu_rg sr_done st_ready sth_ready stl_ready y_done yg_ready yh_ready "
            "yl_ready vh_ready rvl_ready v_done yn_ready kf_ready kr_split qrot_ready qf_ready qh_ready "
            "kh_ready s_done nmx_ready exp_ready p_ready pt_done pth_ready ptl_ready pv_done oh_ready "
            "ol_ready tanh_ready merged_in mh_ready ml_ready h1_back preloaded half_done out_landed").split()
    S = {n: nc.alloc_semaphore(n) for n in sems}

    def s3(e, lhs_hi, lhs_lo, rhs_hi, rhs_lo, dst, start, stop):
        e.matmul(dst, lhs_hi, rhs_hi, start=start, stop=False, skip_group_check=True)
        e.matmul(dst, lhs_hi, rhs_lo, start=False, stop=False, skip_group_check=True)
        return e.matmul(dst, lhs_lo, rhs_hi, start=False, stop=stop, skip_group_check=True)

    EV = ["cq0", "cq1", "cq2", "ckv0", "ckv1", "rv0", "rv1", "rv2", "rv3", "kr", "rq0", "rk0", "rq1", "rk1",
          "rg0", "rg1", "rg2", "rg3", "k0", "q0", "v0", "v1", "v2", "v3"]
    MADE = list(EV)
    bank = dict(BANK)
    for h in range(HEADS):
        names = [p for f in FILL[h] for p in ((f + "a", f + "b") if f[:2] == "br" else (f,))]
        if h + 1 < HEADS:
            names = ([] if h % 2 == 0 else [f"k{h + 1}"]) + [f"q{h + 1}"] + names
            bank[f"q{h + 1}"], bank[f"k{h + 1}"] = 0, 1
        EV += names
        MADE += names
        for i, p in enumerate(names):
            if p[:2] == "br":
                bank[p] = (0, 1, COL, BC, 0, 1, COL, 0)[i]
            elif p[:2] == "gr":
                bank[p] = COL
    for i in range(4):
        names = [f"{kind}{m}" for kind in ("gm", "bm") for m in (2 * i, 2 * i + 1)]
        EV += names
        MADE += names
        bank.update(zip(names, range(4)))
    evac = {n: i + 1 for i, n in enumerate(EV)}

    def free(e, name):
        before = [n for n in MADE[:MADE.index(name)] if bank[n] == bank[name]]
        if name == FILL[0][0]:
            e.wait_ge(S["rms_ready"], POSTM)
        if name == FILL[-1][1] + "b":
            e.wait_ge(S["ol_ready"], HEADS - 2)
        if before:
            e.wait_ge(S["evac_done"], evac[before[-1]])

    def unit_size(n):
        name = MIX[n - UM] if UM <= n < UF2 else ""
        return HEAD_UNITS[int(name[4:]) % 2] if name.startswith("head") else UNIT


    def load(e, src, n0, adv=0):
        if n0 >= RING:
            e.wait_ge(S["lo_ready"], adv + n0 - RING + 1)
        e.dma_start(raw[n0 % RING][:, 0:src.shape[-1]], src).then_inc(S[f"raw{n0 % RING}"], 16)

    def split_hi(e, n0, adv=0, turns_of_ring=0):
        if isinstance(adv, int) and n0 >= U_END:
            return
        size = unit_size(n0) if isinstance(adv, int) else UNIT
        e.wait_ge(S[f"raw{n0 % RING}"], turns_of_ring * 16 + 16 * (n0 // RING + 1))
        if n0 >= RING:
            e.wait_ge(S["unit_used"], adv + n0 - RING + 1)
        e.activation(whi[n0 % RING][:, 0:size], raw[n0 % RING][:, 0:size], ACT.Copy).then_inc(S["hi_ready"], 1)

    def split_lo(e, n0, adv=0):
        if isinstance(adv, int) and n0 >= U_END:
            return
        size = unit_size(n0) if isinstance(adv, int) else UNIT
        e.wait_ge(S["hi_ready"], adv + n0 + 1)
        e.tensor_tensor(wlo[n0 % RING][:, 0:size], raw[n0 % RING][:, 0:size],
                        whi[n0 % RING][:, 0:size].bitcast(F32), ALU.subtract).then_inc(S["lo_ready"], 1)

    def tile(n0, k):
        return whi[n0 % RING][:, P * k:P * k + P], wlo[n0 % RING][:, P * k:P * k + P]

    def blocks_of(n):
        return (0, 1) if n in FIRST_HALF else (2, 3) if n - 1 in FIRST_HALF else range(TB)

    def tokens_of(n):
        return slice(P * blocks_of(n)[0], P * (blocks_of(n)[-1] + 1))

    BY_HALVES = (PREM, PREM + 1, PRE2, PRE2 + 1)

    def square_at(n, i):
        return (sq + av)[i % 4] if n in BY_HALVES else sq[(SQ0[n] + i) % 2]

    def square(e, n, i, src, cols=slice(0, T)):
        slots = 4 if n in BY_HALVES else 2
        if i >= slots:
            e.wait_ge(S["acc_ready"], AC0[n] + i - slots + 1)
        elif GN < n < GN + RH:
            e.wait_ge(S["col_ready"], n - 1)
        elif n:
            e.wait_ge(S["col_ready"], n - 1 if n in (PREM + 1, PRE2 + 1) else n)
        if i == 2 and n == PREM:
            e.wait_ge(S["al_ready"], NJ)
        if i == 2 and n == PRE2:
            e.wait_ge(S["merged_in"], KD)
        e.activation(square_at(n, i)[:, cols], src, ACT.Square).then_inc(S["sq_ready"], 1)

    def accumulate(e, n, i):
        if i == CHUNKS[n] - 1 and n in AS_IT_IS:
            return
        e.wait_ge(S["sq_ready"], SQ0[n] + i + 1)
        after_phase = n in (POST1, POSTM, POST2)
        t = slice(0, T) if after_phase and i < KD - SPLIT[n] else tokens_of(n)
        src = square_at(n, i)[:, t]
        if i == 0 and n - 1 not in (POST1, POSTM, POST2):
            if n:
                e.wait_ge(S["col_ready"], n - 1 if n in (PREM + 1, PRE2 + 1) else n)
            e.tensor_copy(acc[:, t], src).then_inc(S["acc_ready"], 1)
        else:
            e.wait_ge(S["acc_ready"], AC0[n] + i)
            e.tensor_tensor(acc[:, t], acc[:, t], src, ALU.add).then_inc(S["acc_ready"], 1)

    def sum_columns(e, n):
        if n:
            e.wait_ge(S["rms_ready"], GN if GN < n < GN + RH else n)
        if n == POSTM:
            e.wait_ge(S["evac_done"], len(EV))
        at_col = TB * (n - GN) if GN <= n < GN + RH else 0
        last_sq = square_at(n, CHUNKS[n] - 1)
        sources = [last_sq] if GN <= n < GN + RH else [acc, last_sq] if n in AS_IT_IS else [acc]
        if sources[0] is acc:
            e.wait_ge(S["acc_ready"], AC0[n + 1])
        for b in blocks_of(n):
            for i, src in enumerate(sources):
                if src is last_sq and b == blocks_of(n)[0]:
                    e.wait_ge(S["sq_ready"], SQ0[n + 1])
                mm = e.matmul(psum[:, COL, at_col + b:at_col + b + 1], src[:, P * b:P * b + P], ones[:, 0:1],
                              start=i == 0, stop=i == len(sources) - 1)
        mm.then_inc(S["col_ready"], 1)

    def root(e, n, width, halve=False, heads=1):
        e.wait_ge(S["col_ready"], n + heads)
        if n:
            e.wait_ge(S["rc_ready"], n)
        f = 4.0 if halve else 1.0
        c = slice(blocks_of(n)[0], blocks_of(n)[-1] + 1 + TB * (heads - 1))
        e.activation(rms[:, c], psum[:, COL, c], ACT.Sqrt, bias=g("eps4" if halve else "eps"),
                     scale=f / width).then_inc(S["rms_ready"], heads)

    def reciprocal(e, n, heads=1):
        e.wait_ge(S["rms_ready"], n + heads)
        if n:
            e.wait_ge(S["dg_ready"], n)
        c = slice(blocks_of(n)[0], blocks_of(n)[-1] + 1 + TB * (heads - 1))
        e.reciprocal(rcol[:, c], rms[:, c]).then_inc(S["rc_ready"], heads)
        e.wait_ge(S["rc_ready"], n + heads)

    def diagonal(e, n):
        h = n - GN if GN <= n < GN + RH else 0
        if h >= 2:
            e.wait_ge(S["bc_ready"], n - 1)
        elif h == 0 and n:
            e.wait_ge(S["bc_ready"], n)
        b = slice(blocks_of(n)[0], blocks_of(n)[-1] + 1)
        c = slice(TB * h + b.start, TB * h + b.stop)
        shape = [P, b.stop - b.start, P]
        e.tensor_tensor((dg, dgb)[h % 2][:, b, :], ident[:, None, :].broadcast_to(shape),
                        rcol[:, c, None].broadcast_to(shape), ALU.mult).then_inc(S["dg_ready"], 1)

    def invert(e, n):
        reciprocal(e, n)
        diagonal(e, n)

    def broadcast(e, n):
        h = n - GN if GN <= n < GN + RH else 0
        e.wait_ge(S["dg_ready"], n + 1)
        if n in (PREM, PRE2):
            e.wait_ge(S["fs_ready"], KD * (1 if n == PREM else 3))
        elif n in (POST1, PREM + 1, CQ, PRE2 + 1, POST2):
            e.wait_ge(S["rsb_ready"], {POST1: 1, PREM + 1: 2, CQ: 3, PRE2 + 1: 4, POST2: 5}[n])
        elif n == CKV:
            e.wait_ge(S["cn_scaled"], NQ)
        elif n == GN:
            e.wait_ge(S["evac_done"], evac["v0"])
        elif n == GN + 1:
            e.wait_ge(S["yg_ready"], RH)
        elif h:
            e.wait_ge(S["yn_ready"], h - 1)
        elif n == POSTM:
            e.wait_ge(S["ol_ready"], HEADS)
        b = SECOND if n in (POST1 + 1, POSTM + 1, POST2 + 1) else 5 if h % 2 else BC
        t = tokens_of(n)
        e.matmul(psum[:, b, t], ones, (dg, dgb)[h % 2][:].rearrange("p b t -> p (b t)")[:, t], start=True,
                 stop=True).then_inc(S["bc_ready"], 1)

    preloads = [0]

    def preload(e, func, turn=None):
        if preloads[0]:
            e.wait_ge(S["preloaded"], preloads[0] + (0 if turn is None else turn))
        e.activation(unread[:], g("eps"), func).then_inc(S["preloaded"], 1)
        preloads[0] += 1 if turn is None else NJ // 2

    def keep_rs(e, n):
        e.wait_ge(S["bc_ready"], n + 1)
        if n == PREM:
            e.wait_ge(S["al_ready"], NJ)
        if n == PRE2:
            e.wait_ge(S["evac_done"], len(EV))
        t = tokens_of(n)
        e.activation(rsb[:, t], psum[:, BC, t], ACT.Copy).then_inc(S["rsb_ready"], 1)

    PRE = ("pre1", "prem", "pre2")
    PRE_N = (PRE1, PREM, PRE2)
    POST_N = (POST1, POSTM, POST2)

    def entered(s, half, k):
        return k + 1 if s == 0 else KD + 2 * KD * (s - 1) + KD * half + k + 1

    def enter_act(e, s, k, half=0):
        t = HALVES[half] if s else slice(0, T)
        if s == 0:
            if k == 0:
                e.wait_ge(S["cols_landed"], 16)
            e.wait_ge(S[f"x{k}"], 16)
        else:
            e.wait_ge(S["h_ready"], 2 * KD * (s - 1) + KD * half + k + 1)
        e.activation(xh[:, k, t], hres[:, k, t], ACT.Copy, scale=g(PRE[s], k)).then_inc(S["xh_ready"], 1)
        if s and half:
            square(e, PRE_N[s] + 1, k, hres[:, k, t], t)

    def enter_dve(e, s, k, half=0):
        t = HALVES[half] if s else slice(0, T)
        e.wait_ge(S["xh_ready"], entered(s, half, k))
        e.scalar_tensor_tensor(out=xl[:, k, t], in0=hres[:, k, t], scalar=g(PRE[s], k),
                               in1=xh[:, k, t].bitcast(F32), op0=ALU.mult, op1=ALU.subtract).then_inc(S["xl_ready"], 1)

    def phase_out(e, n, m, post):
        src = psum[:, 4 + m % 2, :]
        e.activation(fo[:, m, :], src, ACT.Copy, scale=g(post, m)).then_inc(S["f_copied"], 1)
        square(e, n, m, src)

    def last_out(e, n, half, post, m=KD - 1):
        t = HALVES[half]
        src = psum[:, 5 - half if SPLIT[n] == 1 else 4 + m % 2, t]
        i = m if half == 0 else m - (KD - SPLIT[n])
        if m == KD - 1:
            square(e, n + half, i, src, t)
        e.activation(fo[:, m, t], src, ACT.Copy, scale=g(post, m)).then_inc(S["f_copied"], 1)
        if m < KD - 1:
            square(e, n + half, i, src, t)

    def last_root(e, n, half, post):
        root(e, n + half, D, halve=post != "postm")

    def exit_scaled(e, s, k, half):
        if k == 0 or s == 2:
            e.wait_ge(S["bc_ready"], POST_N[s] + half + 1)
        t = HALVES[half]
        e.tensor_tensor(fo[:, k, t], fo[:, k, t], psum[:, (BC, SECOND)[half], t], ALU.mult).then_inc(S["fs_ready"], 1)

    def exit_added(e, s, k, half, nth=None):
        if s == 1 and k == 0:
            e.wait_ge(S["h1_back"], 16)
        t = HALVES[half]
        e.wait_ge(S["fs_ready"], KD * (2 * s + half) + (k if nth is None else nth) + 1)
        e.tensor_tensor(hres[:, k, t], hres[:, k, t], fo[:, k, t], ALU.add).then_inc(S["h_ready"], 1)

    SUM_AT, CAST_AT = (1, 3), (5, 6)

    def cross(e, s, half, k):
        if k < KD:
            exit_scaled(e, s - 1, k, half)
        if k >= 2:
            enter_dve(e, s, k - 2, half)
        if k < KD:
            exit_added(e, s - 1, k, half)

    LAST_POOL = (1, 3, 5, 6)
    LAST_ORDER = (1, 0, 3, 2, 5, 4, 6, 7)
    LAST_DVE = [k for k in LAST_ORDER if k not in LAST_POOL]

    block = nc.Block()
    with block as block:
        @block.sync
        def _(sp):
            def ffn(w, n0, first=0):
                for c in range(first, 4):
                    load(sp, w[c], n0 + c)
                with sp.Fori(0, (W1_UNITS + W2_UNITS) // 4 - 1) as i:
                    for c in range(4):
                        load(sp, w[4 * i + (4 + c)], n0 + 4 + c, 4 * i)

            load(sp, wf1[0], 0)
            sp.dma_start(gain[:], cols).then_inc(S["cols_landed"], 16)
            sp.dma_start(hres[:, 0, :], x[:, 0, :]).then_inc(S["x0"], 16)
            load(sp, wf1[1], 1)
            for k in range(1, KD):
                sp.dma_start(hres[:, k, :], x[:, k, :]).then_inc(S[f"x{k}"], 16)
            sp.dma_start(cst[:], consts[:, 0:2 * P]).then_inc(S["cst_landed"], 16)
            sp.dma_start(posi[:], pos).then_inc(S["pos_landed"], 16)
            ffn(wf1, UF1, 2)
            for n in range(UM, UF2):
                load(sp, wmix[n - UM][:, 0:unit_size(n)], n)
                if n == UM + 7:
                    sp.wait_ge(S["unit_used"], UM)
                    sp.dma_start(trif[:], consts[:, 2 * P:3 * P]).then_inc(S["tri_landed"], 16)
                if n == UM + 8:
                    sp.wait_ge(S["h_ready"], 2 * KD)
                    sp.dma_start(h1_dram, hres[:]).then_inc(S["spilled"], 16)
                if n == UM + 13:
                    sp.wait_ge(S["spilled"], 16)
                    sp.wait_ge(S["xl_ready"], entered(1, 1, KD - 1))
                    sp.wait_ge(S["sq_ready"], SQ0[PREM] + 2 * KD)
                    sp.dma_start(dec[:], decay).then_inc(S["decay_landed"], 16)
                if n == UNIT_OF["bm3"] + 8:
                    sp.wait_ge(S["unit_used"], UNIT_OF["bm3"] + 1)
                    sp.dma_start(hres[:], h1_dram).then_inc(S["h1_back"], 16)
            ffn(wf2, UF2)
            for half in range(2):
                for k in LAST_ORDER:
                    if k in LAST_POOL:
                        sp.wait_ge(S["h_pool_ready"], len(LAST_POOL) * half + LAST_POOL.index(k) + 1)
                    else:
                        sp.wait_ge(S["h_ready"], 4 * KD + len(LAST_DVE) * half + LAST_DVE.index(k) + 1)
                    t = HALVES[half]
                    sp.dma_start(out[:, k, t], hres[:, k, t]).then_inc(S["out_landed"], 16)
            sp.wait_ge(S["out_landed"], 16 * 2 * KD)

        @block.tensor
        def _(pe):
            def first_units(s, n0, banks):
                for half in range(2 if s else 1):
                    t = HALVES[half] if s else slice(0, T)
                    for k in range(KD):
                        pe.wait_ge(S["xl_ready"], entered(s, half, k))
                        for c, dst in enumerate(banks):
                            if k == 0 and half == 0:
                                pe.wait_ge(S["lo_ready"], n0 + c + 1)
                            hi, lo = tile(n0 + c, k)
                            mm = s3(pe, hi, lo, xh[:, k, t], xl[:, k, t], psum[:, dst, t], k == 0, k == KD - 1)
                            if k == KD - 1 and (half or not s):
                                mm.then_inc(S["unit_used"], 1)
                        if s and k == SUM_AT[half]:
                            sum_columns(pe, (POST_N[s - 1] + 1, PRE_N[s])[half])
                        if s and k == CAST_AT[half]:
                            broadcast(pe, (POST_N[s - 1] + 1, PRE_N[s])[half])
                if s:
                    sum_columns(pe, PRE_N[s] + 1)

            def last_chunks(n, chunks, in_hi, in_lo, steps):
                for half in range(2):
                    t = HALVES[half]
                    tiles_done = 0
                    for c, units in enumerate(chunks):
                        if len(chunks) == 1:
                            bk = 5 - half
                            pe.wait_ge(S["sq_ready"], SQ0[n] + KD - 2 + half)
                        else:
                            bk = 4 + c
                            read = KD - 4 + c + 2 * half
                            pe.wait_ge(S["sq_ready"], SQ0[n] + read + 1)
                            pe.wait_ge(S["f_copied"], KD + SPLIT[POST1] + read + 1)
                        tiles_of = [(n0, k, k == tiles_in - 1) for n0, tiles_in in units for k in range(tiles_in)]
                        for j, (n0, k, last) in enumerate(tiles_of):
                            if k == 0:
                                pe.wait_ge(S["lo_ready"], n0 + 1)
                            hi, lo = tile(n0, k)
                            mm = s3(pe, hi, lo, in_hi[:, j, t], in_lo[:, j, t], psum[:, bk, t], j == 0,
                                    j == len(tiles_of) - 1)
                            if half and last:
                                mm.then_inc(S["unit_used"], 1)
                            if half and tiles_done == steps[0]:
                                sum_columns(pe, n)
                            if half and tiles_done == steps[1]:
                                broadcast(pe, n)
                            tiles_done += 1
                        if half == 0:
                            mm.then_inc(S["half_done"], 1)

            def unit8(n0, adv, dst, ks=range(KD)):
                if ks[0] == 0:
                    pe.wait_ge(S["lo_ready"], adv + n0 + 1)
                for k in ks:
                    hi, lo = tile(n0, k)
                    mm = s3(pe, hi, lo, xh[:, k, :], xl[:, k, :], dst, k == 0, k == KD - 1)
                if ks[-1] == KD - 1:
                    mm.then_inc(S["unit_used"], 1)

            def ffn(f, n0):
                s, j0 = (0, 2)[f], NJ * f
                if f:
                    pe.wait_ge(S["f_copied"], KD + SPLIT[POST1] + KD + SPLIT[POSTM])
                if f:
                    first_units(s, n0, (0, 2, 1))
                    pe.wait_ge(S["fs_ready"], 4 * KD)
                    unit8(n0 + 3, 0, psum[:, 3, :], range(3))
                    broadcast(pe, PRE2 + 1)
                    unit8(n0 + 3, 0, psum[:, 3, :], range(3, KD))
                else:
                    first_units(s, n0, (0, 2))
                    unit8(n0 + 2, 0, psum[:, 1, :], range(5))
                    pe.wait_ge(S["cst_landed"], 16)
                    sum_columns(pe, PRE1)
                    unit8(n0 + 2, 0, psum[:, 1, :], range(5, KD))
                    unit8(n0 + 3, 0, psum[:, 3, :], range(2))
                    broadcast(pe, PRE1)
                    unit8(n0 + 3, 0, psum[:, 3, :], range(2, KD))
                with pe.Fori(1, NJ // 2) as i:
                    for c in range(2):
                        for half, done in enumerate(("gs_ready", "a_ready")):
                            pe.wait_ge(S[done], 2 * i + (j0 + c - 1))
                            unit8(n0 + 2 * c + half, 4 * i, psum[:, c + 2 * half, :])
                nb = n0 + W1_UNITS
                sq0 = SQ0[POST_N[s]]

                def out_chunk(m, at_unit):
                    pe.wait_ge(S["sq_ready"], sq0 + m - 1)
                    for part, tiles_in in enumerate(PART):
                        pe.wait_ge(S["lo_ready"], at_unit + part + 1)
                        if m < 2:
                            pe.wait_ge(S["al_ready"], j0 + PART0[part] + tiles_in)
                        for k in range(tiles_in):
                            j = PART0[part] + k
                            hi, lo = tile(at_unit + part, k)
                            mm = s3(pe, hi, lo, ah[:, j, :], al[:, j, :], psum[:, 4 + m % 2, :], j == 0, j == NJ - 1)
                        mm.then_inc(S["unit_used"], 1)

                for m in range(KD - 1):
                    out_chunk(m, nb + 3 * m)
                last_chunks(POST_N[s], [[(nb + 3 * (KD - 1) + part, tiles_in) for part, tiles_in in enumerate(PART)]],
                            ah, al, (3, 6))

            def product(name, srcs, n0, tiles, done=True):
                free(pe, name)
                for i, (k, (hi_in, lo_in)) in enumerate(zip(tiles, srcs)):
                    hi, lo = tile(n0, k)
                    mm = s3(pe, hi, lo, hi_in, lo_in, psum[:, bank[name], :], i == 0, i == len(tiles) - 1)
                if done:
                    mm.then_inc(S["unit_used"], 1)

            def project(name, ks=range(KD)):
                n0 = UNIT_OF[name]
                if ks[0] == 0:
                    pe.wait_ge(S["lo_ready"], n0 + 1)
                    free(pe, name)
                for k in ks:
                    hi, lo = tile(n0, k)
                    mm = s3(pe, hi, lo, xh[:, k, :], xl[:, k, :], psum[:, bank[name], :], k == 0, k == KD - 1)
                if ks[-1] == KD - 1:
                    mm.then_inc(S["unit_used"], 1)

            def head_unit(h):
                n0 = UNIT_OF[f"head{h}"]
                pe.wait_ge(S["lo_ready"], n0 + 1)
                if h == 0:
                    pe.wait_ge(S["cnl_ready"], NQ + NKV)
                if h % 2 == 0:
                    product(f"k{h}", [(cnh[:, NQ + k, :], cnl[:, NQ + k, :]) for k in range(NKV)], n0,
                            range(NQ, NQ + NKV), done=False)
                product(f"q{h}", [(cnh[:, k, :], cnl[:, k, :]) for k in range(NQ)], n0, range(NQ))

            def ret_scores(h):
                c, r = h // 2, slice(64 * (h % 2), 64 * (h % 2) + 64)
                if h % 2 == 0:
                    pe.wait_ge(S["rl_ready"], 2 + h)
                if h == 0:
                    pe.wait_ge(S["evac_done"], evac["rq1"])
                else:
                    pe.wait_ge(S["st_ready"], h)
                for b in range(TB):
                    n = T - P * b
                    blk = slice(P * b, P * b + P)
                    mm = s3(pe, rh[r, 2 + c, blk], rl[r, 2 + c, blk], rh[r, c, P * b:], rl[r, c, P * b:],
                            tri[:, ROW_AT[n]:ROW_AT[n] + n], True, True)
                mm.then_inc(S["sr_done"], 1)

            def ret_out(h):
                pe.wait_ge(S["stl_ready"], h + 1)
                if h == 0:
                    pe.wait_ge(S["rvl_ready"], 1)
                else:
                    pe.wait_ge(S["yg_ready"], h)
                for b in range(TB):
                    n = T - P * b
                    row = slice(ROW_AT[n], ROW_AT[n] + n)
                    cols_h = slice(RDV * h, RDV * h + RDV)
                    mm = s3(pe, rvh[:, b, cols_h], rvl[:, b, cols_h], sth[:, row], stl[:, row],
                            psum[:, 5, P * b:], b == 0, b == TB - 1)
                mm.then_inc(S["y_done"], 1)

            def scores(h):
                pe.wait_ge(S["evac_done"], evac[f"q{h}"])
                if h == 0:
                    pe.wait_ge(S["kr_split"], 2)
                    pe.wait_ge(S["mask_ready"], 2)
                    pe.wait_ge(S["evac_done"], evac["v2"])
                    pe.wait_ge(S["st_ready"], RH)
                else:
                    pe.wait_ge(S["ptl_ready"], 2 * h)
                for i in range(TB):
                    n = P * (i + 1)
                    a = ROW_AT[n]
                    q = slice(P * i, P * i + P)
                    s3(pe, qh[0:DQK, q], ql[0:DQK, q], kh[0:DQK, 0:n], kl[0:DQK, 0:n], tri[:, a:a + n], True, False)
                    mm = pe.matmul(tri[:, a + n - P:a + n], identb[:], maskb[:], start=False, stop=True,
                                   skip_group_check=True)
                mm.then_inc(S["s_done"], 1)

            def turn_probs(h):
                pe.wait_ge(S["p_ready"], h + 1)
                for b in range(TB):
                    for i in range(b, TB):
                        src = ROW_AT[P * (i + 1)] + P * b
                        dst = ROW_AT[T - P * b] + P * (i - b)
                        mm = pe.transpose(tri[:, dst:dst + P], pr[:, src:src + P], ident)
                mm.then_inc(S["pt_done"], 1)

            def attend(h):
                if h < 2:
                    pe.wait_ge(S["yn_ready"], RH - h)
                else:
                    pe.wait_ge(S["ol_ready"], h - 1)
                if h == HEADS - 1:
                    pe.wait_ge(S["evac_done"], evac[FILL[-1][1] + "b"])
                for b in range(TB):
                    pe.wait_ge(S["ptl_ready"], 2 * h + 1 + (b > 0))
                    n = T - P * b
                    row = slice(ROW_AT[n], ROW_AT[n] + n)
                    pair = slice(P * (h // 2), P * (h // 2) + P)
                    mm = s3(pe, vh[:, b, pair], vl[:, b, pair], pth[:, row], ptl[:, row],
                            psum[:, 5 + 2 * (h % 2), P * b:], b == 0, b == TB - 1)
                mm.then_inc(S["pv_done"], 1)

            def fill(name):
                n0 = UNIT_OF[name]
                pe.wait_ge(S["lo_ready"], n0 + 1)
                pe.wait_ge(S["yl_ready"], RH)
                for half, part in enumerate("ab"):
                    product(name + part, [(yh[:, k, :], yl[:, k, :]) for k in range(4)], n0,
                            range(4 * half, 4 * half + 4), done=half == 1)

            ffn(0, UF1)

            first_units(1, UM, (0, 1, 2))
            pe.wait_ge(S["fs_ready"], 2 * KD)
            project("ckv0", range(3))
            broadcast(pe, PREM + 1)
            project("ckv0", range(3, KD))
            project("ckv1")
            for i in range(4):
                n0 = UNIT_OF[f"rv{i}"]
                pe.wait_ge(S["lo_ready"], n0 + 1)
                for b in range(TB):
                    if i == 0:
                        free(pe, f"rv{b}")
                        if b >= 2:
                            pe.wait_ge(S["f_copied"], KD + SPLIT[POST1])
                    for kk in range(2):
                        k = 2 * i + kk
                        blk = slice(P * b, P * b + P)
                        w = slice(T * kk, T * kk + T)
                        mm = s3(pe, xh[:, k, blk], xl[:, k, blk], whi[n0 % RING][:, w], wlo[n0 % RING][:, w],
                                psum[:, 2 + b, :], k == 0, k == KD - 1)
                mm.then_inc(S["unit_used"], 1)
                if i == 1:
                    sum_columns(pe, CQ)
            project("kr")
            broadcast(pe, CQ)
            project("rq0")
            project("rk0")
            project("rq1")
            sum_columns(pe, CKV)
            project("rk1")
            project("rg0")
            for h in range(RH):
                ret_scores(h)
                if h == 0:
                    broadcast(pe, CKV)
                if h + 1 < RH:
                    project(f"rg{h + 1}")
                else:
                    head_unit(0)
                if h:
                    sum_columns(pe, GN + h - 1)
                if h + 1 < RH:
                    ret_out(h)
            n0 = UNIT_OF["v"]
            pe.wait_ge(S["lo_ready"], n0 + 1)
            for b in range(TB):
                free(pe, f"v{b}")
                if b == 0:
                    pe.wait_ge(S["cn_scaled"], NQ + NKV)
                if b == 1:
                    pe.wait_ge(S["st_ready"], RH)
                for k in range(NKV):
                    blk = slice(P * b, P * b + P)
                    w = slice(T * k, T * k + T)
                    mm = s3(pe, cnh[:, NQ + k, blk], cnl[:, NQ + k, blk], whi[n0 % RING][:, w], wlo[n0 % RING][:, w],
                            psum[:, bank[f"v{b}"], :], k == 0, k == NKV - 1)
                mm.then_inc(S["unit_used" if b == TB - 1 else "v_done"], 1)
            ret_out(RH - 1)
            scores(0)
            sum_columns(pe, GN + RH - 1)
            for h in range(HEADS):
                if h:
                    attend(h - 1)
                if h + 1 < HEADS:
                    head_unit(h + 1)
                fills = FILL[h]
                if h == 0:
                    broadcast(pe, GN)
                    broadcast(pe, GN + 1)
                    project(fills[0])
                    broadcast(pe, GN + 2)
                    broadcast(pe, GN + 3)
                elif EARLY[h]:
                    fill(fills[0])
                    fill(fills[1])
                else:
                    project(fills[0], range(CUT))
                turn_probs(h)
                if h == 0:
                    project(fills[1])
                elif EARLY[h]:
                    fill(fills[2])
                    fill(fills[3])
                else:
                    project(fills[0], range(CUT, KD))
                if h + 1 < HEADS:
                    scores(h + 1)
            attend(HEADS - 1)
            for i in range(4):
                n0 = UNIT_OF[f"bm{i}"]
                project(f"gm{2 * i}")
                project(f"gm{2 * i + 1}")
                pe.wait_ge(S["lo_ready"], n0 + 1)
                if i == 0:
                    pe.wait_ge(S["ol_ready"], HEADS)
                for half in range(2):
                    product(f"bm{2 * i + half}", [(oh[k][:], ol[k][:]) for k in range(4)], n0,
                            range(4 * half, 4 * half + 4), done=half == 1)
            for m in range(KD - 2):
                n0 = UNIT_OF[f"wo{m}"]
                pe.wait_ge(S["lo_ready"], n0 + 1)
                if m >= 2:
                    pe.wait_ge(S["sq_ready"], SQ0[POSTM] + m - 1)
                for k in range(KD):
                    if m == 0:
                        pe.wait_ge(S["ml_ready"], k + 1)
                    hi, lo = tile(n0, k)
                    mm = s3(pe, hi, lo, mh[:, k, :], ml[:, k, :], psum[:, 4 + m % 2, :], k == 0, k == KD - 1)
                mm.then_inc(S["unit_used"], 1)
            last_chunks(POSTM, [[(UNIT_OF[f"wo{m}"], KD)] for m in (KD - 2, KD - 1)], mh, ml, (2, 5))

            ffn(1, UF2)
            sum_columns(pe, POST2 + 1)
            broadcast(pe, POST2 + 1)

        @block.scalar
        def _(act):
            def enter_halves(s):
                n0 = (UM, UF2)[s - 1]
                post = ("post1", "postm")[s - 1]
                if s == 2:
                    act.wait_ge(S["unit_used"], n0 - 1)
                    last_out(act, POSTM, 1, post, KD - 2)
                    split_hi(act, n0 + 2)
                for half in range(2):
                    for k in range(KD):
                        enter_act(act, s, k, half)
                        if half:
                            if k == SUM_AT[1] + 2:
                                root(act, PRE_N[s], D)
                            if k == KD - 1:
                                keep_rs(act, PRE_N[s])
                            continue
                        if s == 1 and k in (0, 1):
                            split_hi(act, n0 + 1 + k)
                        if k == (3, 0)[s - 1]:
                            act.wait_ge(S["unit_used"], n0)
                            last_out(act, POST_N[s - 1], 1, post)
                        if k == 7:
                            split_hi(act, n0 + 3)
                        if k == 4:
                            last_root(act, POST_N[s - 1], 1, post)
                        for i in {4: (0, 1), 5: (2, 3), 6: (4, 5), 7: (6, 7)}.get(k, ()):
                            square(act, PRE_N[s], i, hres[:, i, HALVES[0]], HALVES[0])

            def ffn(f, n0):
                s, j0 = (0, 2)[f], NJ * f
                if f == 0:
                    split_hi(act, n0)
                    for k in range(KD):
                        enter_act(act, 0, k)
                        if k == 0:
                            split_hi(act, n0 + 1)
                    for k in range(KD):
                        square(act, PRE1, k, hres[:, k, :])
                        if k == 3:
                            split_hi(act, n0 + 2)
                else:
                    enter_halves(2)
                if f == 0:
                    preload(act, ACT.Sqrt)
                    split_hi(act, n0 + 3)
                last = (PRE1, PRE2 + 1)[f]
                root(act, last, D)
                preload(act, ACT.Silu)
                keep_rs(act, last)

                with act.Fori(0, NJ // 2) as i:
                    preload(act, ACT.Silu, i)
                    for c in range(2):
                        j = 2 * i + c
                        split_hi(act, n0 + 4 + 2 * c, 4 * i, i)
                        act.wait_ge(S["gs_ready"], j + (j0 + 1))
                        act.activation(sq[c][:], sq[c][:], ACT.Silu).then_inc(S["silu_ready"], 1)
                        split_hi(act, n0 + 5 + 2 * c, 4 * i, i)
                        act.wait_ge(S["a_ready"], j + (j0 + 1))
                        act.activation(ah[:, j, :], av[c][:], ACT.Copy).then_inc(S["ah_ready"], 1)

                nb, n, post = n0 + W1_UNITS, POST_N[s], ("post1", "postm", "post2")[s]
                for m in range(KD - 1):
                    u0 = nb + 3 * m
                    split_hi(act, u0 + 4)
                    split_hi(act, u0 + 5)
                    act.wait_ge(S["unit_used"], u0 + 3)
                    phase_out(act, n, m, post)
                    split_hi(act, u0 + 6)
                preload(act, ACT.Sqrt)
                act.wait_ge(S["half_done"], (1, 4)[f])
                last_out(act, n, 0, post)
                last_root(act, n, 0, post)
                if f:
                    act.wait_ge(S["unit_used"], U_END)
                    last_out(act, n, 1, post)
                    last_root(act, n, 1, post)

            ffn(0, UF1)

            def nxt(name, ahead=4):
                split_hi(act, UNIT_OF[name] + ahead)

            enter_halves(1)
            nxt("cq0")
            root(act, PREM + 1, D)
            keep_rs(act, PREM + 1)
            for c in range(NQ):
                act.wait_ge(S["evac_done"], evac[f"cq{c}"])
                square(act, CQ, c, cf[:, c, :])
                if c < 2:
                    nxt(("cq1", "cq2")[c])
            nxt("ckv0")
            nxt("ckv1")
            act.wait_ge(S["rope_args"], 1)
            act.activation(cos_r[:], angle_abs[:, 1, :], ACT.Sin, bias=g("half_pi"),
                           scale=-1.0).then_inc(S["sin_ready"], 1)
            act.activation(sin_r[:], angle[:, 1, :], ACT.Sin, scale=g("sign_r")).then_inc(S["sin_ready"], 1)
            act.activation(rope_m[64:96, :], angle_abs[64:96, 0, :], ACT.Sin, bias=g("half_pi", rows=slice(64, 96)),
                           scale=-1.0).then_inc(S["sin_ready"], 1)
            act.activation(rope_m[96:P, :], angle[96:P, 0, :], ACT.Sin,
                           scale=g("sign_m", rows=slice(96, P))).then_inc(S["sin_ready"], 1)
            nxt("rv0")
            nxt("rv1")
            root(act, CQ, QR)
            nxt("rv2")
            for c in range(NKV):
                act.wait_ge(S["evac_done"], evac[f"ckv{c}"])
                square(act, CKV, c, cf[:, NQ + c, :])
            nxt("rv3")
            for b in range(TB):
                act.wait_ge(S["evac_done"], evac[f"rv{b}"])
                act.activation(rvh[:, b, :], rvc[:, b, :], ACT.Copy, scale=rscol[:, b:b + 1]).then_inc(S["rvh_ready"], 1)

            def latent_hi(c):
                act.wait_ge(S["cn_scaled"], c + 1)
                act.activation(cnh[:, c, :], cf[:, c, :], ACT.Copy,
                               scale=g("qn", c) if c < NQ else g("kvn", c - NQ)).then_inc(S["cnh_ready"], 1)

            def rotated_hi(nth):
                act.wait_ge(S["rot_ready"], nth + 1)
                act.activation(rh[:, ROTATED[nth], :], av[1][:], ACT.Copy).then_inc(S["rh_ready"], 1)

            nxt("kr")
            for c in range(NQ):
                latent_hi(c)
            nxt("rq0")
            rotated_hi(0)
            nxt("rk0")
            rotated_hi(1)
            nxt("rq1")
            rotated_hi(2)
            root(act, CKV, KVR)
            nxt("rk1")
            rotated_hi(3)

            def gate_silu(h):
                nxt(f"rg{h}")
                act.wait_ge(S["evac_done"], evac[f"rg{h}"])
                act.activation(yr[:, h, :], av[h % 2][:], ACT.Silu).then_inc(S["silu_rg"], 1)

            def ret_square(h):
                act.wait_ge(S["y_done"], h + 1)
                square(act, GN + h, 0, psum[:, 5, :])

            def ret_high(h):
                act.wait_ge(S["yn_ready"], h + 1)
                act.activation(yh[:, h, :], yr[:, h, :], ACT.Copy, scale=g("gn", h)).then_inc(S["yh_ready"], 1)

            for h in range(RH):
                act.wait_ge(S["st_ready"], h + 1)
                if h:
                    act.wait_ge(S["y_done"], h)
                act.activation(sth[:], st[:], ACT.Copy).then_inc(S["sth_ready"], 1)
                if h == 0:
                    gate_silu(0)
                if h + 1 < RH:
                    gate_silu(h + 1)
                    if h == 0:
                        for c in range(NQ, NQ + NKV):
                            latent_hi(c)
                    ret_square(h)

            def head_split(h):
                act.wait_ge(S["unit_used"], UNIT_OF[f"head{h}"] + 1)
                if h % 2 == 0:
                    act.activation(kf[0:NOPE, :], psum[NOPE:P, bank[f"k{h}"], :], ACT.Copy).then_inc(S["kf_ready"], 1)
                    act.activation(kh[0:NOPE, :], psum[0:NOPE, bank[f"k{h}"], :], ACT.Copy).then_inc(S["kh_ready"], 1)
                else:
                    act.wait_ge(S["kf_ready"], h // 2 + 1)
                    act.activation(kh[0:NOPE, :], kf[0:NOPE, :], ACT.Copy).then_inc(S["kh_ready"], 1)
                act.activation(qf[0:NOPE, :], psum[0:NOPE, bank[f"q{h}"], :], ACT.Copy).then_inc(S["qf_ready"], 1)

            def query_split(h):
                act.wait_ge(S["qrot_ready"], h + 1)
                act.wait_ge(S["qf_ready"], h + 1)
                act.activation(qh[0:DQK, :], qf[0:DQK, :], ACT.Copy).then_inc(S["qh_ready"], 1)

            def fill_act(name):
                nxt(name)
                if name[:2] == "gr":
                    m = int(name[2])
                    act.wait_ge(S["evac_done"], evac[name])
                    act.activation(mret[:, m, :], av[m % 2][:], ACT.Tanh, scale=0.5).then_inc(S["tanh_ready"], 1)

            act.activation(kh[64:96, :], kr[64:96, :], ACT.Copy).then_inc(S["kr_split"], 1)
            head_split(0)
            query_split(0)
            for b in range(TB):
                if b < TB - 1:
                    act.wait_ge(S["v_done"], b + 1)
                else:
                    act.wait_ge(S["unit_used"], UNIT_OF["v"] + 1)
                act.activation(vh[:, b, :], psum[:, bank[f"v{b}"], :], ACT.Copy).then_inc(S["vh_ready"], 1)
            nxt("head0")
            nxt("v")
            preload(act, ACT.Sqrt)
            ret_square(RH - 1)
            root(act, GN, RDV, heads=RH)
            scale = 1.0 / math.sqrt(DQK)

            def out_hi(h):
                act.wait_ge(S["pv_done"], h + 1)
                r = slice(64 * (h % 2), 64 * (h % 2) + 64)
                act.activation(oh[h // 2][r, :], psum[r, 5 + 2 * (h % 2), :], ACT.Copy).then_inc(S["oh_ready"], 1)

            for h in range(HEADS):
                if h:
                    out_hi(h - 1)
                act.wait_ge(S["nmx_ready"], h + 1)
                for i in range(TB):
                    n = P * (i + 1)
                    row = slice(ROW_AT[n], ROW_AT[n] + n)
                    act.activation(pr[:, row], tri[:, row], ACT.Exp, bias=nmx[:, i:i + 1], scale=scale,
                                   accum_out=lsum[:, i:i + 1]).then_inc(S["exp_ready"], 1)
                if h + 1 < HEADS:
                    head_split(h + 1)
                    nxt(f"head{h + 1}")
                if h + 1 < HEADS:
                    query_split(h + 1)
                if h == 0:
                    ret_high(0)
                    ret_high(1)
                for f in FILL[h][:EARLY[h]]:
                    fill_act(f)
                if h == 0:
                    ret_high(2)
                    ret_high(3)
                act.wait_ge(S["pt_done"], h + 1)
                for part in PARTS:
                    act.activation(pth[:, part], tri[:, part], ACT.Copy).then_inc(S["pth_ready"], 1)
                for f in FILL[h][EARLY[h]:]:
                    fill_act(f)
            out_hi(HEADS - 1)
            for i in range(4):
                for m in (2 * i, 2 * i + 1):
                    nxt(f"gm{m}")
                    act.wait_ge(S["evac_done"], evac[f"gm{m}"])
                    act.activation(av[m % 2][:], av[m % 2][:], ACT.Tanh, scale=0.5).then_inc(S["tanh_ready"], 1)
                nxt(f"bm{i}")
                for m in (2 * i, 2 * i + 1):
                    act.wait_ge(S["merged_in"], m + 1)
                    act.activation(mh[:, m, :], mret[:, m, :], ACT.Copy, scale=0.5).then_inc(S["mh_ready"], 1)
            for m in range(KD - 2):
                act.wait_ge(S["unit_used"], UNIT_OF[f"wo{m}"] + 1)
                phase_out(act, POSTM, m, "postm")
                nxt(f"wo{m}")
            preload(act, ACT.Sqrt)
            for m in (KD - 2, KD - 1):
                act.wait_ge(S["half_done"], m - (KD - 4))
                last_out(act, POSTM, 0, "postm", m)
            last_root(act, POSTM, 0, "postm")

            ffn(1, UF2)

        @block.vector
        def _(dve):
            chain = [0]

            def link(ins):
                chain[0] += 1
                ins.then_inc(S["chain"], 1)
                dve.wait_ge(S["chain"], chain[0])

            def rotation_angle(t):
                if t == 0:
                    dve.wait_ge(S["pos_landed"], 16)
                    for i, name in enumerate(("freq_m", "freq_r")):
                        link(dve.tensor_scalar(angle[:, i, :], posi[:], g(name), None, ALU.mult))
                a = angle[:, t, :]
                magic = 1.5 * 2.0 ** 23
                link(dve.tensor_scalar(turns[:], a, 1 / (2 * math.pi), magic, ALU.mult, ALU.add))
                link(dve.tensor_scalar(turns[:], turns[:], magic, None, ALU.subtract))
                link(dve.tensor_scalar(turns_hi[:], turns[:], 1 / 4096.0, magic, ALU.mult, ALU.add))
                link(dve.tensor_scalar(turns_hi[:], turns_hi[:], magic, None, ALU.subtract))
                link(dve.scalar_tensor_tensor(out=turns[:], in0=turns_hi[:], scalar=-4096.0, in1=turns[:],
                                              op0=ALU.mult, op1=ALU.add))
                for part in pi_parts(4):
                    for src, f in ((turns_hi, 4096.0), (turns, 1.0)):
                        link(dve.scalar_tensor_tensor(out=a, in0=src[:], scalar=-part * f, in1=a,
                                                      op0=ALU.mult, op1=ALU.add))
                link(dve.tensor_scalar(a, a, 3.1415925, -3.1415925, ALU.min, ALU.max))

            def cross_halves(s):
                for half in range(2):
                    for k in range(KD + 2):
                        cross(dve, s, half, k)
                        if half == 0 and k in (1, 2) and s == 1:
                            split_lo(dve, UM + k)
                        if half == 0 and k == 0 and s == 2:
                            accumulate(dve, POSTM + 1, 0)
                        if half == 0 and k == (4, 1)[s - 1]:
                            accumulate(dve, POST_N[s - 1] + 1, s - 1)
                        if half and k == CAST_AT[1] + 1:
                            invert(dve, PRE_N[s])
                        if half == 0 and k == 5:
                            invert(dve, POST_N[s - 1] + 1)

            def ffn(f, n0):
                s, j0 = (0, 2)[f], NJ * f
                if f == 0:
                    split_lo(dve, n0)
                if f == 1:
                    cross_halves(2)
                for k in range(KD if f == 0 else 0):
                    enter_dve(dve, s, k)
                    if k == 0:
                        split_lo(dve, n0 + 1)
                if f == 0:
                    for k in range(KD):
                        accumulate(dve, PRE1, k)
                        if k == 3:
                            split_lo(dve, n0 + 2)
                invert(dve, (PRE1, PRE2 + 1)[f])
                if f == 0:
                    split_lo(dve, n0 + 3)
                else:
                    dve.wait_ge(S["lo_ready"], n0 + 4)
                dve.wait_ge(S["rsb_ready"], (1, 5)[f])

                def gates(i, first=False):
                    for c in range(2):
                        j = 2 * i + c
                        dve.wait_ge(S["unit_used"], 4 * i + (n0 + 2 * c + 1))
                        if not first:
                            dve.wait_ge(S["a_ready"], j + (j0 - 1))
                        dve.tensor_tensor(sq[c][:], psum[:, c, :], rsb[:], ALU.mult).then_inc(S["gs_ready"], 1)
                        split_lo(dve, n0 + 4 + 2 * c, 4 * i)
                        dve.wait_ge(S["sgr_ready"], j + (j0 + 1))
                        dve.wait_ge(S["unit_used"], 4 * i + (n0 + 2 * c + 2))
                        dve.tensor_tensor(av[c][:], psum[:, 2 + c, :], av[c][:], ALU.mult).then_inc(S["a_ready"], 1)
                        split_lo(dve, n0 + 5 + 2 * c, 4 * i)
                        dve.wait_ge(S["ah_ready"], j + (j0 + 1))
                        dve.tensor_tensor(al[:, j, :], av[c][:], ah[:, j, :].bitcast(F32),
                                          ALU.subtract).then_inc(S["al_ready"], 1)

                gates(0, first=True)
                with dve.Fori(1, NJ // 2) as i:
                    gates(i)
                nb, n = n0 + W1_UNITS, POST_N[s]
                for m in range(KD - 1):
                    for part in range(2):
                        split_lo(dve, nb + 3 * m + 4 + part)
                    accumulate(dve, n, m)
                    split_lo(dve, nb + 3 * m + 6)
                    if f == 0 and m in (1, 3):
                        rotation_angle(m // 2)
                accumulate(dve, n, KD - 1)
                invert(dve, n)

            ffn(0, UF1)

            cross_halves(1)
            invert(dve, PREM + 1)
            dve.scalar_tensor_tensor(out=angle_abs[:], in0=angle[:], scalar=-1.0, in1=angle[:], op0=ALU.mult,
                                     op1=ALU.max).then_inc(S["rope_args"], 1)
            dve.tensor_copy(rscol[:], rcol[:, 0:TB]).then_inc(S["rscol_ready"], 1)

            given = [0]

            def gives(ins, name):
                assert EV[given[0]] == name, (EV[given[0]], name)
                given[0] += 1
                ins.then_inc(S["evac_done"], 1)

            def used(name):
                dve.wait_ge(S["unit_used"], UNIT_OF[name] + 1)

            def latent(name, c):
                used(name)
                gives(dve.tensor_tensor(cf[:, c, :], psum[:, bank[name], :], rsb[:], ALU.mult), name)

            def latent_low(c):
                dve.wait_ge(S["cnh_ready"], c + 1)
                dve.scalar_tensor_tensor(out=cnl[:, c, :], in0=cf[:, c, :],
                                         scalar=g("qn", c) if c < NQ else g("kvn", c - NQ),
                                         in1=cnh[:, c, :].bitcast(F32), op0=ALU.mult,
                                         op1=ALU.subtract).then_inc(S["cnl_ready"], 1)

            def latent_scale(c):
                dve.wait_ge(S["bc_ready"], (CQ if c < NQ else CKV) + 1)
                dve.tensor_tensor(cf[:, c, :], cf[:, c, :], psum[:, BC, :], ALU.mult).then_inc(S["cn_scaled"], 1)

            dve.wait_ge(S["rsb_ready"], 3)
            for c in range(NQ):
                latent(f"cq{c}", c)
                accumulate(dve, CQ, c)
            latent("ckv0", NQ)
            latent("ckv1", NQ + 1)
            dve.wait_ge(S["sin_ready"], 2)
            dve.tensor_tensor(cos_r[:], cos_r[:], rsb[:], ALU.mult).then_inc(S["cos_scaled"], 1)
            dve.tensor_tensor(sin_r[:], sin_r[:], rsb[:], ALU.mult).then_inc(S["cos_scaled"], 1)
            invert(dve, CQ)
            accumulate(dve, CKV, 0)
            accumulate(dve, CKV, 1)
            dve.wait_ge(S["sin_ready"], 4)
            for b in range(TB):
                used("rv3")
                heads_of = psum[:, 2 + b, :].rearrange("p (h d) -> p h d", h=RH)
                link(dve.tensor_reduce(vsum[:, b, :], heads_of, AX.X, ALU.add))
                gives(dve.scalar_tensor_tensor(out=rvc[:, b, :].rearrange("p (h d) -> p h d", h=RH),
                                               in0=vsum[:, b, :, None].broadcast_to([P, RH, RDV]), scalar=-1.0 / RDV,
                                               in1=heads_of, op0=ALU.mult, op1=ALU.add), f"rv{b}")
            for b in range(TB):
                dve.wait_ge(S["rvh_ready"], b + 1)
                ins = dve.scalar_tensor_tensor(out=rvl[:, b, :], in0=rvc[:, b, :], scalar=rscol[:, b:b + 1],
                                               in1=rvh[:, b, :].bitcast(F32), op0=ALU.mult, op1=ALU.subtract)
            ins.then_inc(S["rvl_ready"], 1)
            used("kr")
            dve.wait_ge(S["sin_ready"], 4)
            b = bank["kr"]
            dve.tensor_tensor(av[0][64:96, :], psum[96:P, b, :], rope_m[96:P, :], ALU.mult).then_inc(S["chain"], 1)
            chain[0] += 1
            gives(dve.tensor_tensor(av[1][64:96, :], psum[64:96, b, :], rope_m[64:96, :], ALU.mult), "kr")
            dve.wait_ge(S["chain"], chain[0])
            dve.wait_ge(S["evac_done"], evac["kr"])
            link(dve.tensor_tensor(av[0][64:96, :], av[0][64:96, :], av[1][64:96, :], ALU.add))
            link(dve.tensor_tensor(kr[64:96, :], av[0][64:96, :], rsb[64:96, :], ALU.mult))
            for c in range(NQ):
                latent_scale(c)
            for c in range(NQ):
                latent_low(c)

            def rotate(name, nth):
                used(name)
                c4 = ROTATED[nth]
                if nth:
                    dve.wait_ge(S["rl_ready"], nth)
                dve.wait_ge(S["cos_scaled"], 2)
                bk = bank[name]
                for q in range(4):
                    src, dst = 32 * (q ^ 1), 32 * q
                    ins = dve.tensor_tensor(av[0][dst:dst + 32, :], psum[src:src + 32, bk, :],
                                            sin_r[src:src + 32, :], ALU.mult)
                ins.then_inc(S["chain"], 1)
                chain[0] += 1
                gives(dve.tensor_tensor(av[1][:], psum[:, bk, :], cos_r[:], ALU.mult), name)
                dve.wait_ge(S["chain"], chain[0])
                dve.wait_ge(S["evac_done"], evac[name])
                dve.tensor_tensor(av[1][:], av[1][:], av[0][:], ALU.add).then_inc(S["rot_ready"], 1)
                dve.wait_ge(S["rh_ready"], nth + 1)
                dve.tensor_tensor(rl[:, c4, :], av[1][:], rh[:, c4, :].bitcast(F32),
                                  ALU.subtract).then_inc(S["rl_ready"], 1)

            rotate("rq0", 0)
            rotate("rk0", 1)
            rotate("rq1", 2)
            invert(dve, CKV)
            rotate("rk1", 3)

            def gate_scaled(h):
                used(f"rg{h}")
                if h >= 2:
                    dve.wait_ge(S["silu_rg"], h - 1)
                ins = dve.tensor_tensor(av[h % 2][:], psum[:, bank[f"rg{h}"], :], rsb[:], ALU.mult)
                gives(ins, f"rg{h}")

            def ret_gated(h):
                dve.wait_ge(S["sq_ready"], SQ0[GN + h + 1])
                dve.wait_ge(S["silu_rg"], h + 1)
                dve.tensor_tensor(yr[:, h, :], psum[:, 5, :], yr[:, h, :], ALU.mult).then_inc(S["yg_ready"], 1)

            def ret_normed(h):
                dve.wait_ge(S["bc_ready"], GN + h + 1)
                dve.wait_ge(S["yg_ready"], h + 1)
                dve.tensor_tensor(yr[:, h, :], yr[:, h, :], psum[:, 5 if h % 2 else BC, :],
                                  ALU.mult).then_inc(S["yn_ready"], 1)

            def ret_low(h):
                dve.wait_ge(S["yh_ready"], h + 1)
                dve.scalar_tensor_tensor(out=yl[:, h, :], in0=yr[:, h, :], scalar=g("gn", h),
                                         in1=yh[:, h, :].bitcast(F32), op0=ALU.mult,
                                         op1=ALU.subtract).then_inc(S["yl_ready"], 1)

            dve.wait_ge(S["decay_landed"], 16)
            for h in range(RH):
                dve.wait_ge(S["sr_done"], h + 1)
                for b in range(TB):
                    n = T - P * b
                    row = slice(ROW_AT[n], ROW_AT[n] + n)
                    if h:
                        dve.wait_ge(S["stl_ready"], h)
                    ins = dve.tensor_tensor(st[:, row], tri[:, row], dec[:, h, 0:n], ALU.mult)
                ins.then_inc(S["st_ready"], 1)
                if h == 0:
                    gate_scaled(0)
                dve.wait_ge(S["sth_ready"], h + 1)
                dve.tensor_tensor(stl[:], st[:], sth[:].bitcast(F32), ALU.subtract).then_inc(S["stl_ready"], 1)
                if h + 1 < RH:
                    gate_scaled(h + 1)
                    if h == 0:
                        for c in range(NQ, NQ + NKV):
                            latent_scale(c)
                        for c in range(NQ, NQ + NKV):
                            latent_low(c)
                    ret_gated(h)
            dve.wait_ge(S["kr_split"], 1)
            dve.tensor_tensor(kl[64:96, :], kr[64:96, :], kh[64:96, :].bitcast(F32),
                              ALU.subtract).then_inc(S["kr_split"], 1)

            def head_split(h):
                used(f"head{h}")
                gates_before = sum(f[:2] == "gr" for fills in FILL[:h - 1] for f in fills) if h else 0
                if gates_before:
                    dve.wait_ge(S["tanh_ready"], gates_before)
                bq = bank[f"q{h}"]
                link(dve.tensor_tensor(av[0][64:96, :], psum[96:P, bq, :], rope_m[96:P, :], ALU.mult))
                link(dve.tensor_tensor(av[1][64:96, :], psum[64:96, bq, :], rope_m[64:96, :], ALU.mult))
                dve.tensor_tensor(qf[64:96, :], av[0][64:96, :], av[1][64:96, :], ALU.add).then_inc(S["qrot_ready"], 1)
                dve.wait_ge(S["kh_ready"], h + 1)
                if h % 2 == 0:
                    gives(dve.tensor_tensor(kl[0:NOPE, :], psum[0:NOPE, bank[f"k{h}"], :], kh[0:NOPE, :].bitcast(F32),
                                            ALU.subtract), f"k{h}")
                else:
                    dve.tensor_tensor(kl[0:NOPE, :], kf[0:NOPE, :], kh[0:NOPE, :].bitcast(F32), ALU.subtract)

            def query_split(h):
                dve.wait_ge(S["qh_ready"], h + 1)
                ins = dve.tensor_tensor(ql[0:DQK, :], qf[0:DQK, :], qh[0:DQK, :].bitcast(F32), ALU.subtract)
                gives(ins, f"q{h}")

            def fill_dve(name):
                n0 = UNIT_OF[name]
                used(name)
                if name[:2] == "gr":
                    m = int(name[2])
                    if m >= 2:
                        dve.wait_ge(S["tanh_ready"], m - 1)
                    gives(dve.tensor_tensor(av[m % 2][:], psum[:, bank[name], :], rsb[:], ALU.mult), name)
                    return
                for half, part in enumerate("ab"):
                    m = 2 * int(name[2]) + half
                    dve.wait_ge(S["tanh_ready"], m + 1)
                    gives(dve.scalar_tensor_tensor(out=mret[:, m, :], in0=mret[:, m, :], scalar=1.0,
                                                   in1=psum[:, bank[name + part], :], op0=ALU.add,
                                                   op1=ALU.mult), name + part)

            head_split(0)
            query_split(0)
            for b in range(TB):
                dve.wait_ge(S["vh_ready"], b + 1)
                gives(dve.tensor_tensor(vl[:, b, :], psum[:, bank[f"v{b}"], :], vh[:, b, :].bitcast(F32),
                                        ALU.subtract), f"v{b}")
            ret_gated(RH - 1)
            scale = 1.0 / math.sqrt(DQK)

            def out_low(h):
                dve.wait_ge(S["oh_ready"], h + 1)
                r = slice(64 * (h % 2), 64 * (h % 2) + 64)
                dve.tensor_tensor(ol[h // 2][r, :], psum[r, 5 + 2 * (h % 2), :], oh[h // 2][r, :].bitcast(F32),
                                  ALU.subtract).then_inc(S["ol_ready"], 1)

            for h in range(HEADS):
                dve.wait_ge(S["s_done"], h + 1)
                for i in range(TB):
                    n = P * (i + 1)
                    row = slice(ROW_AT[n], ROW_AT[n] + n)
                    ins = dve.tensor_reduce(mx[:, i:i + 1], tri[:, row], AX.X, ALU.max)
                link(ins)
                dve.tensor_scalar(nmx[:], mx[:], -scale, None, ALU.mult).then_inc(S["nmx_ready"], 1)
                if h == 0:
                    reciprocal(dve, GN, heads=RH)
                    diagonal(dve, GN)
                    diagonal(dve, GN + 1)
                else:
                    out_low(h - 1)
                dve.wait_ge(S["exp_ready"], 4 * h + 4)
                link(dve.reciprocal(linv[:], lsum[:]))
                for i in range(TB):
                    n = P * (i + 1)
                    row = slice(ROW_AT[n], ROW_AT[n] + n)
                    ins = dve.tensor_scalar(pr[:, row], pr[:, row], linv[:, i:i + 1], None, ALU.mult)
                ins.then_inc(S["p_ready"], 1)
                if h + 1 < HEADS:
                    head_split(h + 1)
                if h + 1 < HEADS:
                    query_split(h + 1)
                if h == 0:
                    ret_normed(0)
                    diagonal(dve, GN + 2)
                    ret_normed(1)
                    diagonal(dve, GN + 3)
                    ret_low(0)
                    ret_low(1)
                for f in FILL[h][:EARLY[h]]:
                    fill_dve(f)
                if h == 0:
                    for r in (2, 3):
                        ret_normed(r)
                        ret_low(r)
                for i, part in enumerate(PARTS):
                    dve.wait_ge(S["pth_ready"], 2 * h + i + 1)
                    dve.tensor_tensor(ptl[:, part], tri[:, part], pth[:, part].bitcast(F32),
                                      ALU.subtract).then_inc(S["ptl_ready"], 1)
                for f in FILL[h][EARLY[h]:]:
                    fill_dve(f)
            out_low(HEADS - 1)
            for i in range(4):
                for m in (2 * i, 2 * i + 1):
                    used(f"gm{m}")
                    if i:
                        dve.wait_ge(S["merged_in"], m - 1)
                    gives(dve.tensor_tensor(av[m % 2][:], psum[:, bank[f"gm{m}"], :], rsb[:], ALU.mult), f"gm{m}")
                for m in (2 * i, 2 * i + 1):
                    used(f"bm{i}")
                    dve.wait_ge(S["tanh_ready"], KD + m + 1)
                    gives(dve.scalar_tensor_tensor(out=av[m % 2][:], in0=av[m % 2][:], scalar=1.0,
                                                   in1=psum[:, bank[f"bm{m}"], :], op0=ALU.add,
                                                   op1=ALU.mult), f"bm{m}")
                    dve.wait_ge(S["evac_done"], evac[f"bm{m}"])
                    dve.tensor_tensor(mret[:, m, :], mret[:, m, :], av[m % 2][:], ALU.add).then_inc(S["merged_in"], 1)
                for m in (2 * i, 2 * i + 1):
                    dve.wait_ge(S["mh_ready"], m + 1)
                    dve.scalar_tensor_tensor(out=ml[:, m, :], in0=mret[:, m, :], scalar=0.5,
                                             in1=mh[:, m, :].bitcast(F32), op0=ALU.mult,
                                             op1=ALU.subtract).then_inc(S["ml_ready"], 1)
            for m in range(KD):
                accumulate(dve, POSTM, m)
            invert(dve, POSTM)

            ffn(1, UF2)
            for half in range(2):
                if half:
                    accumulate(dve, POST2 + 1, 0)
                    invert(dve, POST2 + 1)
                for nth, k in enumerate(LAST_ORDER):
                    exit_scaled(dve, 2, k, half)
                    if k in LAST_DVE:
                        exit_added(dve, 2, k, half, nth)

        @block.gpsimd
        def _(pool):
            def ffn(f):
                s, j0 = (0, 2)[f], NJ * f
                if f:
                    for k in range(2 * KD):
                        accumulate(pool, PRE2 + k // KD, k % KD)
                        if k == KD - 1:
                            split_lo(pool, UF2 + 3)
                pool.wait_ge(S["rsb_ready"], (1, 5)[f])

                def gates(i, first=False):
                    for c in range(2):
                        j = 2 * i + c
                        pool.wait_ge(S["silu_ready"], j + (j0 + 1))
                        if not first:
                            pool.wait_ge(S["al_ready"], j + (j0 - 1))
                        pool.tensor_tensor(av[c][:], sq[c][:], rsb[:], ALU.mult).then_inc(S["sgr_ready"], 1)

                gates(0, first=True)
                with pool.Fori(1, NJ // 2) as i:
                    gates(i)

            ffn(0)
            for k in range(2 * KD):
                accumulate(pool, PREM + k // KD, k % KD)
                if k == KD - 1:
                    pool.wait_ge(S["lo_ready"], UM + 3)
                    split_lo(pool, UM + 3)
            for n in range(UM + 4, UF2 + 3):
                split_lo(pool, n)
                if n == UM + 8:
                    pool.wait_ge(S["tri_landed"], 16)
                    pool.tensor_copy(maskb[:], trif[:]).then_inc(S["mask_ready"], 1)
                    pool.tensor_copy(identb[:], ident).then_inc(S["mask_ready"], 1)
            ffn(1)
            for half in range(2):
                t = HALVES[half]
                for k in LAST_POOL:
                    pool.wait_ge(S["fs_ready"], KD * (4 + half) + LAST_ORDER.index(k) + 1)
                    pool.tensor_tensor(hres[:, k, t], hres[:, k, t], fo[:, k, t], ALU.add).then_inc(S["h_pool_ready"], 1)


def kernel(**inputs):
    import numpy as np
    import concourse.bacc as bacc
    from concourse.bass_utils import run_bass_kernel_spmd as run

    w = {k: np.asarray(v) for k, v in inputs.items()}

    def tiles(m, col_lists):
        t = m.reshape(-1, P, m.shape[1])
        return [np.ascontiguousarray(t[:, :, c].transpose(1, 0, 2).reshape(P, -1)) for c in col_lists]

    def ffn_units(w1, w2):
        order = []
        for j in range(NJ):
            order += [np.arange(P * j, P * j + P), FF + np.arange(P * j, P * j + P)]
        units = np.zeros((W1_UNITS + W2_UNITS, P, UNIT), w1.dtype)
        units[:W1_UNITS] = tiles(w1, order)
        for part, (k0, n) in enumerate(zip(PART0, PART)):
            units[W1_UNITS + part::len(PART), :, :n * P] = tiles(
                w2[P * k0:P * (k0 + n)], [np.arange(P * m, P * m + P) for m in range(KD)])
        return units

    w_in, uq, ukv = w["w_in"][0], w["mla_w_uq"][0], w["mla_w_ukv"][0]
    at = np.cumsum([0, QR, KVR, ROPE, RH * RDK, RH * RDK, RH * RDV, RH * RDV, D, D])
    half = ROPE // 2

    def mix_unit(name):
        kind, i = name.rstrip("0123456789"), int(name[len(name.rstrip("0123456789")):] or 0)
        run_of = {"cq": at[0], "ckv": at[1], "rq": at[3], "rk": at[4], "rg": at[6], "gm": at[7], "gr": at[8]}
        if kind in run_of:
            return tiles(w_in, [run_of[kind] + P * i + np.arange(P)])[0]
        if kind == "kr":
            r = at[2] + np.arange(ROPE)
            return tiles(w_in, [np.concatenate([at[2] - 64 + np.arange(64), r, r[half:], r[:half]])])[0]
        if kind == "rv":
            return tiles(w_in[2 * P * i:2 * P * (i + 1)], [at[5] + np.arange(T)])[0]
        if kind == "v":
            c = np.concatenate([(NOPE + DV) * h + NOPE + np.arange(DV) for h in range(HEADS)])
            return tiles(ukv, [c])[0]
        if kind == "head":
            c = DQK * i + np.arange(DQK)
            q = tiles(uq, [np.concatenate([c, c[NOPE + half:], c[NOPE:NOPE + half]])])[0]
            k = tiles(ukv, [np.concatenate([(NOPE + DV) * j + np.arange(NOPE) for j in (i - i % 2, i - i % 2 + 1)])])[0]
            return np.concatenate([q, k, np.zeros((P, UNIT - HEAD_UNITS[0]), q.dtype)], axis=1)
        if kind in ("br", "bm"):
            m = w["w_branch_ret" if kind == "br" else "w_branch_mla"][0]
            return np.concatenate(tiles(m, [P * c + np.arange(P) for c in (2 * i, 2 * i + 1)]), axis=1)
        return tiles(w["w_out"][0], [P * i + np.arange(P)])[0]

    cols = np.zeros((P, NCOLS), np.float32)
    for name, key in (("pre1", "ffn1_pre_w"), ("post1", "ffn1_post_w"), ("prem", "mix_pre_w"),
                      ("qn", "mla_q_norm_w"), ("kvn", "mla_kv_norm_w"), ("gn", "ret_gn_w"),
                      ("postm", "mix_post_w"), ("pre2", "ffn2_pre_w"), ("post2", "ffn2_post_w")):
        v = w[key][0].reshape(-1, P).T
        cols[:, COLS[name]:COLS[name] + v.shape[1]] = v
    p = np.arange(P)
    for name, v in (("eps", EPS), ("eps4", 4 * EPS), ("half_pi", math.pi / 2),
                    ("freq_m", ROPE_BASE ** (-(p % half) / half)),
                    ("sign_m", np.where(p % ROPE < half, -1.0, 1.0)),
                    ("freq_r", ROPE_BASE ** (-(p % 32) / 32.0)),
                    ("sign_r", np.where(p % 64 < 32, 1.0, -1.0))):
        cols[:, COLS[name]] = v
    consts = np.concatenate([np.ones((P, P)), np.eye(P), np.where(p[:, None] >= p[None, :], 0.0, MASKED)],
                            axis=1).astype(np.float32)
    lag = np.arange(T)[None, :] - p[:, None]
    decay = np.stack([np.where(lag >= 0, np.exp(np.maximum(lag, 0) * np.log(1 - 2.0 ** (-5.0 - h))), 0.0)
                      for h in range(RH)], axis=1) * RDK ** -0.5

    arrays = {
        "x_t": np.ascontiguousarray(w["x"][0].T.reshape(KD, P, T).transpose(1, 0, 2)),
        "pos_b": np.ascontiguousarray(np.broadcast_to(w["positions"][0][None, :], (P, T))),
        "w_ffn1": ffn_units(w["ffn1_w1"][0], w["ffn1_w2"][0]),
        "w_mix": np.stack([mix_unit(n) for n in MIX]),
        "w_ffn2": ffn_units(w["ffn2_w1"][0], w["ffn2_w2"][0]),
        "cols": cols, "consts": consts, "decay": decay.astype(np.float32),
    }
    nc = bacc.Bacc("TRN2", target_bir_lowering=False, num_devices=1)
    args = [nc.dram_tensor(n, a.shape, mybir.dt.from_np(a.dtype), kind="ExternalInput").ap()
            for n, a in arrays.items()]
    args.append(nc.dram_tensor("out_t", (P, KD, T), F32, kind="ExternalOutput").ap())
    build(nc, *args)
    r = run(nc, [arrays], core_ids=[0])
    got = r.results[0]["out_t"]
    return np.ascontiguousarray(got.transpose(2, 1, 0).reshape(1, T, D))
```
